# Optimizing a Trainium2 kernel written in Bass

```python
import jax, jax.numpy as jnp
from jax import lax
import numpy as np

D_MODEL = 1024
BATCH = 1
SEQ = 512
DEPTH = 1
DEC_BATCH = 8
DEC_SEQ = 8
PAST_LEN = 4096
PAGE_SIZE = 128

D_CONV = D_MODEL // 2
CONV_W = 31
N_HEADS = 4
HEAD_DIM = D_MODEL // N_HEADS
D_MLSTM = N_HEADS * HEAD_DIM
D_FF = -(-8 * D_MODEL // (3 * 256)) * 256
CHUNK = 64
EPS = 1e-6
D_IN = 2 * D_CONV + 4 * D_MLSTM + 2 * N_HEADS + 2 * D_MODEL

kernel_name = "hybrid_conformer_mlstm_decode_step"

def _split_points():
    sizes = [D_CONV, D_CONV, D_MLSTM, D_MLSTM, D_MLSTM, D_MLSTM, N_HEADS, N_HEADS, D_MODEL, D_MODEL]
    pts, acc = [], 0
    for s in sizes[:-1]:
        acc += s
        pts.append(acc)
    return pts

def _rmsnorm(x, g):
    xf = x.astype(jnp.float32)
    y = xf * lax.rsqrt(jnp.mean(xf * xf, axis=-1, keepdims=True) + EPS)
    return (y * g.astype(jnp.float32)).astype(x.dtype)

def _layernorm(x, g, b):
    xf = x.astype(jnp.float32)
    mu = jnp.mean(xf, axis=-1, keepdims=True)
    var = jnp.mean(jnp.square(xf - mu), axis=-1, keepdims=True)
    y = (xf - mu) * lax.rsqrt(var + EPS)
    return (y * g.astype(jnp.float32) + b.astype(jnp.float32)).astype(x.dtype)

def _causal_depthwise(buf, a, w, b):
    full = jnp.concatenate([buf.astype(a.dtype), a], axis=1)
    y = lax.conv_general_dilated(full, w[:, None, :].astype(a.dtype), window_strides=(1,),
                                 padding='VALID', dimension_numbers=('NWC', 'WIO', 'NWC'),
                                 feature_group_count=a.shape[-1])
    return y + b.astype(a.dtype), full[:, -(CONV_W - 1):]

def _mlstm_chunkwise(q, k, v, log_i, log_f, C0, n0, m0):
    B, H, T, Dh = q.shape
    L = CHUNK if T >= CHUNK else T
    nc = -(-T // L)
    pad = nc * L - T
    q = jnp.pad(q, ((0, 0), (0, 0), (0, pad), (0, 0)))
    k = jnp.pad(k, ((0, 0), (0, 0), (0, pad), (0, 0)))
    v = jnp.pad(v, ((0, 0), (0, 0), (0, pad), (0, 0)))
    log_i = jnp.pad(log_i, ((0, 0), (0, 0), (0, pad)), constant_values=-jnp.inf)
    log_f = jnp.pad(log_f, ((0, 0), (0, 0), (0, pad)))

    def to_chunks(t):
        t = t.reshape((B, H, nc, L) + t.shape[3:])
        return jnp.moveaxis(t, 2, 0)

    xs = (to_chunks(q), to_chunks(k), to_chunks(v), to_chunks(log_i), to_chunks(log_f))
    causal = jnp.tril(jnp.ones((L, L), dtype=bool))

    def step(carry, inp):
        C, n, m = carry
        qc, kc, vc, li, lf = inp
        bcum = jnp.cumsum(lf, axis=-1)
        D = bcum[..., :, None] - bcum[..., None, :] + li[..., None, :]
        D = jnp.where(causal, D, -jnp.inf)
        inter = bcum + m[..., None]
        m_t = jnp.maximum(inter, jnp.max(D, axis=-1))
        w_intra = jnp.exp(D - m_t[..., None])
        w_inter = jnp.exp(inter - m_t)
        s = jnp.einsum('bhjd,bhsd->bhjs', qc, kc) * w_intra
        num = (jnp.einsum('bhjs,bhsd->bhjd', s, vc)
               + w_inter[..., None] * jnp.einsum('bhvk,bhjk->bhjv', C, qc))
        nq = jnp.sum(s, axis=-1) + w_inter * jnp.einsum('bhk,bhjk->bhj', n, qc)
        h = num / jnp.maximum(jnp.abs(nq), jnp.exp(-m_t))[..., None]
        m_new = m_t[..., -1]
        w_s = jnp.exp(bcum[..., -1:] - bcum + li - m_new[..., None])
        decay = jnp.exp(bcum[..., -1] + m - m_new)
        C_new = decay[..., None, None] * C + jnp.einsum('bhs,bhsv,bhsk->bhvk', w_s, vc, kc)
        n_new = decay[..., None] * n + jnp.einsum('bhs,bhsk->bhk', w_s, kc)
        return (C_new, n_new, m_new), h

    init = (C0.astype(jnp.float32), n0.astype(jnp.float32), m0.astype(jnp.float32))
    (C1, n1, m1), hs = lax.scan(step, init, xs)
    hs = jnp.moveaxis(hs, 0, 2).reshape(B, H, nc * L, Dh)[:, :, :T]
    return hs, C1, n1, m1

def _layer(x, conv_buf, C0, n0, m0, g_mix, w_in, b_in, w_dw, b_dw, g_cn, b_cn, w_co,
           g_mn, w_o, g_fn, w_fi, w_fo):
    B, T, _ = x.shape
    h = _rmsnorm(x, g_mix)
    proj = h @ w_in + b_in
    cv, cg, q, k, v, og, ig, fg, ga, gb = jnp.split(proj, _split_points(), axis=-1)

    a = cv * jax.nn.sigmoid(cg)
    c, new_buf = _causal_depthwise(conv_buf, a, w_dw, b_dw)
    c = jax.nn.silu(_layernorm(c, g_cn, b_cn))
    conv_out = c @ w_co

    def heads(t):
        return t.reshape(B, T, N_HEADS, HEAD_DIM).transpose(0, 2, 1, 3).astype(jnp.float32)
    qh = heads(q)
    kh = heads(k) * (HEAD_DIM ** -0.5)
    vh = heads(v)
    log_i = ig.astype(jnp.float32).transpose(0, 2, 1)
    log_f = jax.nn.log_sigmoid(fg.astype(jnp.float32)).transpose(0, 2, 1)
    hm, C1, n1, m1 = _mlstm_chunkwise(qh, kh, vh, log_i, log_f, C0, n0, m0)
    mu = jnp.mean(hm, axis=-1, keepdims=True)
    var = jnp.mean(jnp.square(hm - mu), axis=-1, keepdims=True)
    hm = (hm - mu) * lax.rsqrt(var + EPS)
    hm = hm.transpose(0, 2, 1, 3).reshape(B, T, D_MLSTM) * g_mn.astype(jnp.float32)
    mlstm_out = (jax.nn.sigmoid(og.astype(jnp.float32)) * hm).astype(x.dtype)

    merged = jax.nn.sigmoid(ga) * conv_out + jax.nn.sigmoid(gb) * mlstm_out
    x = x + merged @ w_o

    h2 = _rmsnorm(x, g_fn)
    gt, up = jnp.split(h2 @ w_fi, 2, axis=-1)
    x = x + (jax.nn.silu(gt) * up) @ w_fo
    return (x, new_buf, C1.astype(C0.dtype), n1.astype(n0.dtype), m1.astype(m0.dtype))

def _trunk(x, conv_bufs, Cs, ns, ms, g_mix_norm, w_in, b_in, w_dwconv, b_dwconv, g_conv_norm,
           b_conv_norm, w_conv_out, g_mlstm_norm, w_out, g_ffn_norm, w_ffn_in, w_ffn_out, g_final):
    bufs, C_list, n_list, m_list = [], [], [], []
    for l in range(DEPTH):
        x, nb, C1, n1, m1 = _layer(x, conv_bufs[l], Cs[l], ns[l], ms[l], g_mix_norm[l], w_in[l], b_in[l],
                                   w_dwconv[l], b_dwconv[l], g_conv_norm[l], b_conv_norm[l],
                                   w_conv_out[l], g_mlstm_norm[l], w_out[l], g_ffn_norm[l],
                                   w_ffn_in[l], w_ffn_out[l])
        bufs.append(nb)
        C_list.append(C1)
        n_list.append(n1)
        m_list.append(m1)
    y = _rmsnorm(x, g_final)
    return y, jnp.stack(bufs), jnp.stack(C_list), jnp.stack(n_list), jnp.stack(m_list)

def setup_inputs(seed: int = 0) -> dict:
    key = jax.random.key(seed)
    ks = jax.random.split(key, 24)
    f32 = jnp.float32
    nrm = lambda k, shape, s: jax.random.normal(k, shape, f32) * s
    f_off = 2 * D_CONV + 4 * D_MLSTM + N_HEADS
    b_in = nrm(ks[5], (DEPTH, D_IN), 0.02)
    b_in = b_in.at[:, f_off:f_off + N_HEADS].add(3.0)
    return {
        "x_prompt": nrm(ks[0], (BATCH, SEQ, D_MODEL), 1.0),
        "x_sample": nrm(ks[1], (DEC_BATCH, DEC_SEQ, D_MODEL), 1.0),
        "cache_conv": nrm(ks[2], (DEPTH, DEC_BATCH, CONV_W - 1, D_CONV), 0.5),
        "state_mlstm_C": nrm(ks[3], (DEPTH, DEC_BATCH, N_HEADS, HEAD_DIM, HEAD_DIM), 0.05),
        "state_mlstm_n": nrm(ks[4], (DEPTH, DEC_BATCH, N_HEADS, HEAD_DIM), 0.1),
        "state_mlstm_m": nrm(ks[6], (DEPTH, DEC_BATCH, N_HEADS), 0.5),
        "g_mix_norm": 1.0 + nrm(ks[7], (DEPTH, D_MODEL), 0.02),
        "w_in": nrm(ks[8], (DEPTH, D_MODEL, D_IN), D_MODEL ** -0.5),
        "b_in": b_in,
        "w_dwconv": nrm(ks[9], (DEPTH, CONV_W, D_CONV), CONV_W ** -0.5),
        "b_dwconv": nrm(ks[10], (DEPTH, D_CONV), 0.02),
        "g_conv_norm": 1.0 + nrm(ks[11], (DEPTH, D_CONV), 0.02),
        "b_conv_norm": nrm(ks[12], (DEPTH, D_CONV), 0.02),
        "w_conv_out": nrm(ks[13], (DEPTH, D_CONV, D_MODEL), D_CONV ** -0.5),
        "g_mlstm_norm": 1.0 + nrm(ks[14], (DEPTH, D_MLSTM), 0.02),
        "w_out": nrm(ks[15], (DEPTH, D_MODEL, D_MODEL), D_MODEL ** -0.5),
        "g_ffn_norm": 1.0 + nrm(ks[16], (DEPTH, D_MODEL), 0.02),
        "w_ffn_in": nrm(ks[17], (DEPTH, D_MODEL, 2 * D_FF), D_MODEL ** -0.5),
        "w_ffn_out": nrm(ks[18], (DEPTH, D_FF, D_MODEL), D_FF ** -0.5),
        "g_final": 1.0 + nrm(ks[19], (D_MODEL,), 0.02),
    }

def reference(x_prompt, x_sample, cache_conv, state_mlstm_C, state_mlstm_n, state_mlstm_m,
              g_mix_norm, w_in, b_in, w_dwconv, b_dwconv, g_conv_norm, b_conv_norm, w_conv_out,
              g_mlstm_norm, w_out, g_ffn_norm, w_ffn_in, w_ffn_out, g_final):
    Bp = x_prompt.shape[0]
    conv0 = jnp.zeros((DEPTH, Bp, CONV_W - 1, D_CONV), x_prompt.dtype)
    C0 = jnp.zeros((DEPTH, Bp, N_HEADS, HEAD_DIM, HEAD_DIM), state_mlstm_C.dtype)
    n0 = jnp.zeros((DEPTH, Bp, N_HEADS, HEAD_DIM), state_mlstm_n.dtype)
    m0 = jnp.zeros((DEPTH, Bp, N_HEADS), state_mlstm_m.dtype)
    y_prompt, conv_p, C_p, n_p, m_p = _trunk(
        x_prompt, conv0, C0, n0, m0, g_mix_norm, w_in, b_in, w_dwconv, b_dwconv, g_conv_norm,
        b_conv_norm, w_conv_out, g_mlstm_norm, w_out, g_ffn_norm, w_ffn_in, w_ffn_out, g_final)
    y_sample, conv_s, C_s, n_s, m_s = _trunk(
        x_sample, cache_conv, state_mlstm_C, state_mlstm_n, state_mlstm_m, g_mix_norm, w_in, b_in,
        w_dwconv, b_dwconv, g_conv_norm, b_conv_norm, w_conv_out, g_mlstm_norm, w_out, g_ffn_norm,
        w_ffn_in, w_ffn_out, g_final)
    return (y_prompt, y_sample, conv_p, C_p, n_p, m_p, conv_s, C_s, n_s, m_s)


_drawn_inputs = setup_inputs


def setup_inputs(seed=0):
    import zlib

    import numpy as np

    out = dict(_drawn_inputs(seed))
    spreads = {}
    factors = {'b_dwconv': 4.055,
     'g_conv_norm': 6.853,
     'b_conv_norm': 8.0,
     'g_mlstm_norm': 8.0,
     'g_ffn_norm': 4.145,
     'g_final': 2.835}
    for name, (base, spread) in spreads.items():
        noise = np.random.default_rng([zlib.crc32(name.encode()), seed]).standard_normal(out[name].shape)
        drawn = base * np.exp(spread * noise) if base else spread * noise
        out[name] = __import__('jax').numpy.asarray(drawn.astype(out[name].dtype))
    for name, factor in factors.items():
        out[name] = (out[name] * factor).astype(out[name].dtype)
    return out
```

```python
from contextlib import ExitStack

import numpy as np

import concourse.bass as bass
from concourse import mybir

F32 = mybir.dt.float32
F32R = mybir.dt.float32r
ALU = mybir.AluOpType
ACT = mybir.ActivationFunctionType

P = 128
D = 1024
KT = D // P
TP, TS = 512, 64
T = TP + TS
HALF = T // 2
SB, SL = 8, 8
NH, HD = 4, 256
VE = HD + 1
NB = TP // P
DC = 512
CT = DC // P
CW = 31
PAST = CW - 1
FF = 2816
FT = FF // P
GROUPS = (8, 8, 6)
EPS = 1e-6
BIG = 1e30

U_A = 0
N_A = 2 * CT
U_B = U_A + N_A
PER_HEAD = 10
U_GA = U_B + NH * PER_HEAD
U_CO = U_GA + KT
U_O = U_CO + KT
U_FF = U_O + KT
U_E, U_F, Q_E = [], [], []
_u, _q = U_FF, 0
for _g in GROUPS:
    U_E.append(_u)
    U_F.append(_u + 2 * _g)
    Q_E.append(_q)
    _u += 2 * _g + KT
    _q += _g
NU = _u

V_BIAS = 0
V_GMIX = U_CO
V_GFFN = V_GMIX + KT
V_GFIN = V_GFFN + KT
V_GMN = V_GFIN + KT
V_GCN = V_GMN + KT
V_BCN = V_GCN + CT
V_BDW = V_BCN + CT
V_WDW = V_BDW + CT
NV = V_WDW + CT * CW

I_G = 0
I_EM = 5
I_WS = 10
I_OFF = 15
I_WI = 21
NI = 22
OFF = {}
for _s in range(NB):
    for _t in range(_s + 1, NB):
        OFF[_s, _t] = I_OFF + len(OFF)

S_USE, T_USE, I_USE, PV_USE, CP_USE, CS_USE, N_USE, HT_USE = 0, 5, 10, 11, 16, 18, 26, 27
USES = 30
READER = ["dve"] * 5 + ["act"] * 5 + ["act"] + ["act"] * 5 + ["act"] * 2 + ["dve"] * 8 + ["dve"] + ["dve"] * 3
ACT_USES, DVE_USES = READER.count("act"), READER.count("dve")
W_OFF = [0, 512, 896, 1152, 1280]
W_COLS = 1280 + TS

C_B = 1 + 2
C_GA = C_B + NH * PER_HEAD // 2
C_CO = C_GA + 4
C_O = C_CO + 4
C_E, C_F = [], []
_c, _c2, _c3 = C_O + 4, 8, 6
for _g in GROUPS:
    C_E.append((_c, _c, _c2, _c3))
    C_F.append(_c + _g // 2)
    _c, _c2, _c3 = _c + _g // 2 + 4, _c2 + _g // 2, _c3 + _g // 2
C2_END = _c2

START = 1
POOL_SET = 16
DVE_HEAD_STEPS = 84
CONV_TAPS = (3, 4, 3, 2, 4, 4, 4, 4, 2, 1)


class Tally:

    def __init__(self, eng, sem):
        self.eng, self.sem, self.n, self.turn = eng, sem, 0, 0

    def on(self, ins):
        ins.then_inc(self.sem, 1)
        self.n += 1

    def settle(self, back=0):
        self.eng.wait_ge(self.sem, self.turn + (self.n - back))

    def loop(self, i, per):
        self.start, self.per, self.turn = self.n, per, i * per

    def end(self, iters):
        assert self.n - self.start == self.per, f"per iteration: {self.n - self.start}, not {self.per}"
        self.n, self.turn = self.start + iters * self.per, 0


def build(nc, xT, vecs, gate_w, gate_b, cache, w_cvcg, w_head, w_ga, w_co, w_o, w_fi, w_fo0, w_fo1, w_fo2,
          st_c, st_n, st_m, y, conv_p, conv_s, cn_p, m_p, c_s, n_s, m_s):
    with ExitStack() as ctx:
        place = [-(-nc.sbuf_base // 32) * 32]

        def sb(name, cols, dt=F32, parts=P):
            shape = [parts] + (list(cols) if isinstance(cols, (list, tuple)) else [cols])
            t = nc.alloc_sbuf_tensor_at(name, shape, dt, offset=place[0])
            place[0] += -(-4 * int(np.prod(shape[1:])) // 32) * 32
            return t

        def sem(name):
            return ctx.enter_context(nc.semaphore(name))

        x = sb("x", [KT, T])
        h_hi = sb("h_hi", [KT, T], F32R)
        h_lo = sb("h_lo", [KT, T], F32R)
        raw = sb("raw", [2, KT * P])
        w_hi = sb("w_hi", [2, KT * P], F32R)
        w_lo = sb("w_lo", [2, KT * P], F32R)
        vec = sb("vec", NV)
        mean_d = sb("mean_d", P)
        mean_c = sb("mean_c", P)
        eps = sb("eps", 1)
        tmp = sb("tmp", [2, T])
        hf = sb("hf", [2, T])
        acc = sb("acc", T)
        rs = sb("rs", T)
        merged = sb("merged", [KT, T])
        conv = sb("conv", [CT, T])
        pool_base = place[0]
        ident = sb("ident", P)
        a_p = sb("a_p", [CT, PAST + TP])
        a_s = sb("a_s", [CT, SB, PAST + SL])
        negm = sb("negm", [NH, T])
        cols = sb("cols", [NI, NH])
        dec = sb("dec", [NH, SB])
        onehot = sb("onehot", SB)
        wb = sb("wb", [NH, SB])
        nst = sb("nst", [NH, 2, SB])
        nnew = sb("nnew", [NH, 2, SB])
        cmask = sb("cmask", P)
        smask = sb("smask", TS)
        head_base = place[0]
        gw = sb("gw", [KT, 2 * NH])
        gstat = sb("gstat", [KT, P], F32R)
        gt = sb("gt", [2, T], parts=NH)
        gb = sb("gb", 2, parts=NH)
        m0 = sb("m0", SB, parts=NH)
        li = sb("li", T, parts=NH)
        fz = sb("fz", T, parts=NH)
        lf = sb("lf", T, parts=NH)
        ft = sb("ft", T, parts=NH)
        seg = sb("seg", T, parts=NH)
        lfm = sb("lfm", T, parts=NH)
        lim = sb("lim", T, parts=NH)
        mrow = sb("mrow", T, parts=NH)
        nrow = sb("nrow", T, parts=NH)
        rows = sb("rows", NI * P, parts=NH)
        t8 = sb("t8", SB, parts=NH)
        mend = sb("mend", SB, parts=NH)
        drow = sb("drow", SB, parts=NH)
        sel = sb("sel", [NH, P], parts=NH)
        assert place[0] <= nc.sbuf_usable_end
        place[0] = head_base
        qkv = sb("qkv", [3, 2, T])
        qk_flat = qkv[:, :, :, :].rearrange("p a b n -> p (a b n)")
        wvn = qk_flat[:, 0:NB * VE].rearrange("p (s v) -> p s v", s=NB)
        wvs = qk_flat[:, 2 * T:2 * T + SB * HD].rearrange("p (b v) -> p b v", b=SB)
        kvn = sb("kvn", [5, 2 * HD + 1])
        num = sb("num", [5, VE])
        wts = sb("wts", W_COLS)
        mdiag = sb("mdiag", [NB, P])
        msamp = sb("msamp", TS)
        qm = sb("qm", [2, SB * (TS + SL)])
        cs = sb("cs", [SB, 2, HD])
        cp = sb("cp", [2, VE])
        inter = sb("inter", HD + SB)
        stats = sb("stats", [5, 6])
        mv = sb("mv", [5, 2])
        small = sb("small", [4, 5])
        nq8 = sb("nq8", SB)
        nq1 = sb("nq1", 1)
        assert place[0] <= nc.sbuf_usable_end, place[0]
        place[0] = pool_base
        ga = sb("ga", [KT, T])
        c_hi = sb("c_hi", [CT, T], F32R)
        c_lo = sb("c_lo", [CT, T], F32R)
        csq = sb("csq", [CT, T])
        chalf = sb("chalf", [2, T])
        cmean = sb("cmean", T)
        assert place[0] <= nc.sbuf_usable_end, place[0]
        place[0] = pool_base
        hid_hi = sb("hid_hi", [8, T], F32R)
        hid_lo = sb("hid_lo", [8, T], F32R)

        ps = ctx.enter_context(nc.psum_tensor("ps", [P, 8, 512], F32))

        def slot(s):
            return ps[:, 2 * s:2 * s + 2, 0:HALF]

        def bank(k):
            return ps[:, 4 + k % 4, :]

        def halves(t, j):
            if isinstance(j, int):
                return t[:, j, :].rearrange("p (b n) -> p b n", b=2)
            return t[:, bass.ds(j, 1), :].rearrange("p o (b n) -> p (o b) n", b=2)

        def flat(t):
            return t[:, :].rearrange("p (b n) -> p b n", b=2)

        def row(t, j):
            if isinstance(j, int):
                return t[:, j, :]
            return t[:, bass.ds(j, 1), :].rearrange("p o n -> p (o n)")

        def vcol(c, parts=P):
            return vec[0:parts, c:c + 1] if isinstance(c, int) else vec[0:parts, bass.ds(c, 1)]

        x_loaded = [sem(f"x_loaded{k}") for k in range(KT)]
        vec_loaded = sem("vec_loaded")
        gw_loaded = sem("gw_loaded")
        gb_loaded = sem("gb_loaded")
        m0_loaded = sem("m0_loaded")
        cache_loaded = sem("cache_loaded")
        n_loaded = sem("n_loaded")
        cs_loaded = sem("cs_loaded")
        raw_loaded = [sem(f"raw_loaded{s}") for s in range(2)]
        consts_ready = sem("consts_ready")
        masks_ready = sem("masks_ready")
        head_bufs_set = sem("head_bufs_set")
        hi_ready = sem("hi_ready")
        lo_ready = sem("lo_ready")
        unit_done = sem("unit_done")
        slot_read = [sem(f"slot_read{s}") for s in range(4)]
        sq_ready = sem("sq_ready")
        sq_added = sem("sq_added")
        sum_done = sem("sum_done")
        hf_ready = sem("hf_ready")
        hhi_ready = sem("hhi_ready")
        hlo_even = sem("hlo_even_ready")
        hlo_odd = sem("hlo_odd_ready")
        gstat_hi = sem("gstat_hi_ready")
        gstat_lo = sem("gstat_lo_ready")
        gates_done = sem("gates_done")
        gt_ready = sem("gt_ready")
        fabs_ready = sem("fabs_ready")
        ln_ready = sem("ln_ready")
        mrow_ready = sem("mrow_ready")
        exps_in = sem("exp_rows_ready")
        exps_out = sem("exps_done")
        turned = sem("cols_turned")
        negm_spread = sem("negm_spread")
        mdiag_ready = sem("mdiag_ready")
        w_ready = sem("w_ready")
        qm_ready = sem("qm_ready")
        gb_used = sem("gb_used")
        attn_ready = sem("attn_ready")
        act_read = sem("bank_read_by_act")
        dve_read = sem("bank_read_by_dve")
        wv_ready = sem("wv_ready")
        hm_ready = sem("hm_ready")
        rs_ready = sem("rs_ready")
        hvar_ready = sem("hvar_ready")
        hdev_ready = sem("hdev_ready")
        cp_stored = sem("cp_stored")
        cp_free = sem("cp_free")
        cs_stored = sem("cs_stored")
        out_stored = sem("out_stored")
        csum_ready = sem("csum_ready")
        cstat_done = sem("cstat_done")
        cnorm_ready = sem("cnorm_ready")
        csilu_ready = sem("csilu_ready")
        chi_ready = sem("chi_ready")
        clo_ready = sem("clo_ready")
        m_ready = sem("merged_ready")
        mhi_ready = sem("merged_hi_ready")
        mlo_ready = sem("merged_lo_ready")
        hidhi_ready = sem("hid_hi_ready")
        hidlo_ready = sem("hid_lo_ready")
        y_ready = sem("y_ready")
        y_stored = sem("y_stored")
        acc_zero = sem("acc_zero")
        dve_step = sem("dve_step")
        act_step = sem("act_step")
        pool_step = sem("pool_step")

        block = ctx.enter_context(nc.Block())

        @block.sync
        def _(sp):
            for s in (slot_read[0], slot_read[1], act_read, dve_read, gb_used, hidlo_ready, cp_free):
                sp.sem_inc(s, START)
            for k in range(KT):
                sp.dma_start(x[:, k, :], xT[:, k, :]).then_inc(x_loaded[k], 16)
                if k < 2:
                    sp.dma_start(raw[:, k, :], w_cvcg[k]).then_inc(raw_loaded[k], 16)

            def loads(base, w, count, cols=KT * P, first=0):
                with sp.Fori(first, count // 2) as i:
                    for s in range(2):
                        sp.wait_ge(lo_ready, i * 2 + (base + s - 1))
                        sp.dma_start(raw[:, s, 0:cols], w[bass.ds(i * 2 + s, 1)].rearrange("o p n -> (o p) n"))\
                          .then_inc(raw_loaded[s], 16)

            loads(U_A, w_cvcg, N_A, first=1)
            loads(U_B, w_head, NH * PER_HEAD)
            loads(U_GA, w_ga, KT)
            loads(U_CO, w_co, KT, CT * P)
            loads(U_O, w_o, KT)
            for g, w in enumerate((w_fo0, w_fo1, w_fo2)):
                loads(U_E[g], w_fi[2 * Q_E[g]:2 * (Q_E[g] + GROUPS[g])], 2 * GROUPS[g])
                loads(U_F[g], w, KT, GROUPS[g] * P)
            for k in range(KT):
                sp.wait_ge(y_ready, k + 1)
                sp.dma_start(y[:, k, :], x[:, k, :]).then_inc(y_stored, 16)
            sp.wait_ge(y_stored, 16 * KT)

        @block.gpsimd
        def _(pool):
            steps = Tally(pool, pool_step)
            pool.dma_start(vec[:, :], vecs).then_inc(vec_loaded, 16)
            pool.dma_start(gw[:, :, :], gate_w).then_inc(gw_loaded, 16)
            pool.dma_start(gb[:, :], gate_b).then_inc(gb_loaded, 16)
            pool.dma_start(m0[:, :], st_m).then_inc(m0_loaded, 16)
            pool.dma_start(a_s[:, :, :, 0:PAST], cache).then_inc(cache_loaded, 16)
            pool.dma_start(nst[:, :, :, :], st_n).then_inc(n_loaded, 16)
            pool.memset(mean_d[:, :], 1.0 / D).then_inc(consts_ready, 1)
            pool.memset(mean_c[:, :], 1.0 / DC).then_inc(consts_ready, 1)
            pool.memset(eps[:, :], EPS).then_inc(consts_ready, 1)

            def norm_lo(done):
                for k in range(0, KT, 2):
                    pool.wait_ge(hhi_ready, done + k + 1)
                    pool.tensor_tensor(h_lo[:, k, :], hf[:, k % 2, :], h_hi[:, k, :].bitcast(F32), ALU.subtract)\
                        .then_inc(hlo_even, 1)

            steps.on(pool.memset(gstat[:, :, :].rearrange("p k c -> p (k c)").bitcast(F32), 0.0))
            norm_lo(0)
            steps.on(pool.memset(seg[:, :], 1.0))
            steps.on(pool.memset(rows[:, :], 1.0))
            steps.on(pool.memset(a_p[:, :, 0:PAST], 0.0))
            steps.on(pool.memset(ident[:, :], 0.0))
            steps.on(pool.memset(cmask[:, :], 0.0))
            steps.on(pool.memset(smask[:, :], 0.0))
            steps.on(pool.memset(onehot[:, :], 1.0))
            steps.on(pool.memset(sel[:, :, :], 1.0))
            steps.settle()
            steps.on(pool.memset(seg[:, 0:TP:P], 0.0))
            steps.on(pool.memset(seg[:, TP:T:SL], 0.0))
            steps.on(pool.affine_select(out=ident[:, :], in_=ident[:, :], compare_op=ALU.not_equal, fill=1.0,
                                        base=0, pattern=[[-1, P]], channel_multiplier=1))
            steps.on(pool.affine_select(out=cmask[:, :], in_=cmask[:, :], compare_op=ALU.is_ge, fill=-BIG,
                                        base=0, pattern=[[1, P]], channel_multiplier=-1))
            steps.on(pool.affine_select(out=smask[:, :], in_=smask[:, :], compare_op=ALU.is_ge, fill=-BIG,
                                        base=0, pattern=[[1, TS]], channel_multiplier=-1))
            steps.on(pool.affine_select(out=onehot[:, :], in_=onehot[:, :], compare_op=ALU.is_ge, fill=0.0,
                                        base=0, pattern=[[-SL, SB]], channel_multiplier=1))
            steps.on(pool.affine_select(out=sel[:, :, :], in_=sel[:, :, :], compare_op=ALU.is_equal, fill=0.0,
                                        base=0, pattern=[[-1, NH], [0, P]], channel_multiplier=1))
            steps.settle()
            sm = smask[:, :].rearrange("p (b j) -> p b j", b=SB)
            pool.affine_select(out=sm, in_=sm, compare_op=ALU.is_ge, fill=-BIG,
                               base=0, pattern=[[-SL, SB], [0, SL]], channel_multiplier=1).then_inc(masks_ready, 1)
            pool.affine_select(out=onehot[:, :], in_=onehot[:, :], compare_op=ALU.is_ge, fill=0.0,
                               base=SL - 1, pattern=[[SL, SB]], channel_multiplier=-1).then_inc(masks_ready, 1)
            pool.wait_ge(mrow_ready, 1)
            pool.dma_start(m_p, mrow[:, TP - 1:TP]).then_inc(out_stored, 16)
            pool.wait_ge(exps_in, 1)
            pool.dma_start(m_s, mend[:, :]).then_inc(out_stored, 16)
            pool.wait_ge(out_stored, 32)
            pool.wait_ge(slot_read[2], 6)
            pool.wait_ge(slot_read[3], 5)
            pool.memset(qm[:, :, :], 0.0).then_inc(head_bufs_set, 1)
            pool.memset(num[:, 4, :], 0.0).then_inc(head_bufs_set, 1)
            pool.memset(kvn[:, :, 2 * HD:2 * HD + 1], 1.0).then_inc(head_bufs_set, 1)
            pool.dma_start(cs[:, :, :, :], st_c[0]).then_inc(cs_loaded, 16)

            pool.wait_ge(slot_read[0], C_B)
            pool.wait_ge(slot_read[2], 3)
            pool.dma_start(conv_p, a_p[:, :, TP:TP + PAST]).then_inc(out_stored, 16)
            pool.wait_ge(cache_loaded, 16)
            pool.dma_start(conv_s, a_s[:, :, :, SL:SL + PAST]).then_inc(out_stored, 16)

            def states(h, last=False):
                pool.wait_ge(act_read, h * ACT_USES + (START + ACT_USES))
                pool.dma_start(cn_p[bass.ds(h, 1)].rearrange("o p k v -> (o p) k v"), cp[:, :, :])\
                    .then_inc(cp_stored, 16)
                pool.wait_ge(dve_read, h * DVE_USES + (START + 13))
                pool.dma_start(c_s[bass.ds(h, 1)].rearrange("o p b k v -> (o p) b k v"), cs[:, :, :, :])\
                    .then_inc(cs_stored, 16)
                pool.wait_ge(cs_stored, h * 16 + 16)
                pool.wait_ge(cp_stored, h * 16 + 16)
                pool.sem_inc(cp_free, 1)
                if not last:
                    pool.dma_start(cs[:, :, :, :], st_c[bass.ds(h + 1, 1)].rearrange("o p b k v -> (o p) b k v"))\
                        .then_inc(cs_loaded, 16)

            with pool.Fori(0, NH - 1) as h:
                states(h)
            states(NH - 1, last=True)
            pool.wait_ge(dve_read, START + NH * DVE_USES)
            pool.dma_start(n_s, nnew[:, :, :, :]).then_inc(out_stored, 16)
            pool.wait_ge(cp_stored, 16 * NH)
            pool.wait_ge(out_stored, 16 * 5)


            def sum4(src, sig):
                steps.on(pool.tensor_tensor(chalf[:, 0, :], src(0), src(1), ALU.add))
                steps.on(pool.tensor_tensor(chalf[:, 1, :], src(2), src(3), ALU.add))
                steps.settle()
                pool.tensor_tensor(acc[:, :], chalf[:, 0, :], chalf[:, 1, :], ALU.add).then_inc(sig, 1)

            sum4(lambda j: conv[:, j, :], csum_ready)
            pool.wait_ge(slot_read[2], 7)
            for j in range(CT):
                steps.on(pool.tensor_tensor(conv[:, j, :], conv[:, j, :], cmean[:, :], ALU.subtract))
            steps.settle()
            for j in range(CT):
                steps.on(pool.tensor_tensor(csq[:, j, :], conv[:, j, :], conv[:, j, :], ALU.mult))
            steps.settle()
            sum4(lambda j: csq[:, j, :], csum_ready)
            pool.wait_ge(rs_ready, 2)
            for j in range(CT):
                pool.tensor_tensor(conv[:, j, :], conv[:, j, :], rs[:, :], ALU.mult).then_inc(cnorm_ready, 1)
            for j in range(CT):
                pool.wait_ge(chi_ready, j + 1)
                pool.tensor_tensor(c_lo[:, j, :], conv[:, j, :], c_hi[:, j, :].bitcast(F32), ALU.subtract)\
                    .then_inc(clo_ready, 1)
            with pool.Fori(0, KT) as j:
                pool.wait_ge(mhi_ready, j + 1)
                pool.tensor_tensor(row(h_lo, j), row(merged, j), row(h_hi, j).bitcast(F32), ALU.subtract)\
                    .then_inc(mlo_ready, 1)
            norm_lo(KT)
            for g, n in enumerate(GROUPS):
                with pool.Fori(0, n // 2) as i:
                    for s in range(2):
                        pool.wait_ge(hidhi_ready, i * 2 + (Q_E[g] + s + 1))
                        pool.tensor_tensor(row(hid_lo, i * 2 + s), hf[:, s, :], row(hid_hi, i * 2 + s).bitcast(F32),
                                           ALU.subtract).then_inc(hidlo_ready, 1)

        @block.scalar
        def _(act):
            steps = Tally(act, act_step)

            def split_hi(pair, s, first=False):
                act.wait_ge(raw_loaded[s], pair * 16 + 16)
                if not first:
                    act.wait_ge(unit_done, pair * 2 + (s - 1))
                act.activation(w_hi[:, s, :], raw[:, s, :], ACT.Copy).then_inc(hi_ready, 1)

            for k in range(KT):
                act.wait_ge(x_loaded[k], 16)
                if k >= 2:
                    act.wait_ge(sq_added, k - 1)
                act.activation(tmp[:, k % 2, :], x[:, k, :], ACT.Square).then_inc(sq_ready, 1)
            split_hi(0, 0, True)
            split_hi(0, 1, True)
            act.wait_ge(gw_loaded, 16)
            act.wait_ge(pool_step, 1)
            for g in range(2):
                act.activation(gstat[:, :, 64 * g:64 * g + NH], gw[:, :, NH * g:NH * g + NH], ACT.Copy)\
                    .then_inc(gstat_hi, 1)

            def deviation(s, done_sem, n):
                act.wait_ge(done_sem, n)
                act.activation(flat(rs), slot(s), ACT.Sqrt, bias=eps[:, :]).then_inc(slot_read[s], 1)

            def norm_hi(done):
                for k in range(KT):
                    act.wait_ge(hf_ready, done + k + 1)
                    act.activation(h_hi[:, k, :], hf[:, k % 2, :], ACT.Copy).then_inc(hhi_ready, 1)

            act.wait_ge(consts_ready, 3)
            deviation(3, sum_done, 1)
            norm_hi(0)
            act.wait_ge(gates_done, 1)
            for g in range(2):
                act.activation(gt[:, g, :].rearrange("p (b n) -> p b n", b=2),
                               ps[64 * g + 32:64 * g + 32 + NH, 4:6, 0:HALF], ACT.Copy).then_inc(gt_ready, 1)
            act.wait_ge(fabs_ready, 1)
            steps.on(act.activation(ft[:, :], ft[:, :], ACT.Exp, scale=-1.0))
            steps.settle()
            act.activation(ft[:, :], ft[:, :], ACT.Ln, bias=1.0).then_inc(ln_ready, 1)

            act.wait_ge(vec_loaded, 16)
            with act.Fori(0, N_A // 4) as i:
                for j in range(4):
                    act_pair = i * 2 + (j // 2 + 1)
                    split_hi(act_pair, j % 2)
                    if j % 2:
                        act.wait_ge(slot_read[j - 1], i + 1)
                        act.wait_ge(unit_done, i * 4 + (j + 1))
                        act.activation(halves(tmp, j // 2), slot(j), ACT.Sigmoid, bias=vcol(i * 4 + j))\
                            .then_inc(slot_read[j], 1)

            act.wait_ge(mrow_ready, 1)
            act.activation(rows[:, I_EM * P:I_EM * P + T], mrow[:, :], ACT.Exp, scale=-1.0).then_inc(exps_out, 1)
            act.wait_ge(exps_in, 1)
            act.activation(rows[:, I_WS * P:I_WS * P + T], rows[:, I_WS * P:I_WS * P + T], ACT.Exp)\
                .then_inc(exps_out, 1)
            act.activation(rows[:, I_WI * P:I_WI * P + TS], rows[:, I_WI * P:I_WI * P + TS], ACT.Exp)\
                .then_inc(exps_out, 1)
            act.activation(drow[:, :], t8[:, :], ACT.Exp).then_inc(exps_out, 1)
            for h in range(NH):
                act.wait_ge(negm_spread, h + 1)
                act.activation(halves(negm, h), slot(3 - h % 2), ACT.Copy).then_inc(slot_read[3 - h % 2], 1)

            def evac_bias(h, j, dst):
                act.wait_ge(unit_done, h * PER_HEAD + (U_B + j + 1))
                act.activation(dst, slot(j % 2), ACT.Identity, bias=vcol(h * PER_HEAD + (U_B + j)))\
                    .then_inc(slot_read[j % 2], 1)

            act.wait_ge(head_bufs_set, 3)
            act.wait_ge(slot_read[2], 4)
            with act.Fori(0, NH) as h:
                def hi_of(j):
                    split_hi(h * (PER_HEAD // 2) + (U_B + j + 2) // 2, j % 2)

                def use(k):
                    act.wait_ge(attn_ready, h * USES + (k + 1))

                for j in range(2):
                    hi_of(j)
                    evac_bias(h, j, halves(qkv[:, 0, :, :], j))
                hi_of(2)
                act.wait_ge(mdiag_ready, h + 1)

                def gcol(item, parts=P):
                    return cols[0:parts, item, bass.ds(h, 1)]

                for s in range(NB):
                    act.activation(wts[:, W_OFF[s]:W_OFF[s] + P], mdiag[:, s, :], ACT.Exp, bias=gcol(I_G + s))\
                        .then_inc(w_ready, 1)
                    for t in range(s + 1, NB):
                        o = W_OFF[s] + (t - s) * P
                        act.activation(wts[:, o:o + P], negm[:, bass.ds(h, 1), t * P:t * P + P]
                                       .rearrange("p o n -> p (o n)"), ACT.Exp,
                                       bias=gcol(OFF[s, t])).then_inc(w_ready, 1)
                act.activation(wts[0:TS, W_OFF[NB]:W_COLS], msamp[0:TS, :], ACT.Exp, bias=gcol(I_G + NB, TS))\
                    .then_inc(w_ready, 1)
                hi_of(3)
                for j in range(4, 6):
                    hi_of(j)
                    evac_bias(h, j, halves(qkv[:, 2, :, :], j - 4))
                for i in range(5):
                    use(T_USE + i)
                    n = P if i < NB else TS
                    act.activation(kvn[0:n, i, 0:2 * HD], bank(T_USE + i)[0:n, :], ACT.Copy).then_inc(act_read, 1)
                use(I_USE)
                act.activation(inter[0:TS, :], bank(I_USE)[0:TS, 0:HD + SB], ACT.Copy).then_inc(act_read, 1)
                for j in range(6, 8):
                    hi_of(j)
                    act.wait_ge(unit_done, h * PER_HEAD + (U_B + j + 1))
                    act.activation(halves(merged, h * 2 + (j - 6)), slot(j % 2), ACT.Sigmoid,
                                   bias=vcol(h * PER_HEAD + (U_B + j))).then_inc(slot_read[j % 2], 1)
                for i in range(5):
                    use(PV_USE + i)
                    n = P if i < NB else TS
                    act.activation(num[0:n, i, :], bank(PV_USE + i)[0:n, 0:VE], ACT.Copy).then_inc(act_read, 1)
                act.wait_ge(cp_free, h + START)
                for k in range(2):
                    use(CP_USE + k)
                    act.activation(cp[:, k, :], bank(CP_USE + k)[:, 0:VE], ACT.Copy).then_inc(act_read, 1)
                act.wait_ge(hvar_ready, h + 1)
                act.activation(small[:, 2, :], small[:, 1, :], ACT.Sqrt, bias=eps[:, :]).then_inc(hdev_ready, 1)
                for j in range(8, 10):
                    hi_of(j)
                    act.wait_ge(unit_done, h * PER_HEAD + (U_B + j + 1))
                    act.wait_ge(gb_used, h * 2 + START)
                    act.activation(halves(tmp, j % 2), slot(j % 2), ACT.Sigmoid,
                                   bias=vcol(h * PER_HEAD + (U_B + j))).then_inc(slot_read[j % 2], 1)

            def ga_pair(i):
                for s in range(2):
                    split_hi(i + (U_GA + 2) // 2, s)
                    act.wait_ge(unit_done, i * 2 + (U_GA + s + 1))
                    act.activation(halves(ga, i * 2 + s), slot(s), ACT.Sigmoid, bias=vcol(i * 2 + (U_GA + s)))\
                        .then_inc(slot_read[s], 1)

            act.wait_ge(dve_read, START + NH * DVE_USES)
            act.wait_ge(out_stored, 16 * 5)
            act.wait_ge(cp_stored, 16 * NH)
            act.wait_ge(cs_stored, 16 * NH)
            with act.Fori(0, 2) as i:
                ga_pair(i)
            act.wait_ge(cstat_done, 1)
            act.activation(flat(cmean), slot(2), ACT.Copy).then_inc(slot_read[2], 1)
            ga_pair(2)
            deviation(3, cstat_done, 2)
            ga_pair(3)
            for j in range(CT):
                act.wait_ge(cnorm_ready, j + 1)
                act.activation(conv[:, j, :], conv[:, j, :], ACT.Silu, bias=vcol(V_BCN + j), scale=vcol(V_GCN + j))\
                    .then_inc(csilu_ready, 1)
                act.wait_ge(csilu_ready, j + 1)
                act.activation(c_hi[:, j, :], conv[:, j, :], ACT.Copy).then_inc(chi_ready, 1)

            with act.Fori(0, KT // 2) as i:
                for s in range(2):
                    split_hi(i + (U_CO + 2) // 2, s)
                    act.wait_ge(m_ready, i * 2 + (s + 1))
                    act.activation(row(h_hi, i * 2 + s), row(merged, i * 2 + s), ACT.Copy).then_inc(mhi_ready, 1)

            def squares(i, base, contents, sq_base, last=False):
                for s in range(2):
                    if not last:
                        split_hi(i + (base + 2) // 2, s)
                    act.wait_ge(slot_read[s], i + (contents + 1))
                    act.wait_ge(sq_added, i * 2 + (sq_base + s - 1))
                    act.activation(tmp[:, s, :], row(x, i * 2 + s), ACT.Square).then_inc(sq_ready, 1)

            with act.Fori(0, KT // 2) as i:
                squares(i, U_O, C_O, KT)
            deviation(2, sum_done, 2)
            norm_hi(KT)
            for g, n in enumerate(GROUPS):
                with act.Fori(0, n // 2) as i:
                    for p in range(2):
                        split_hi(i * 2 + (U_E[g] // 2 + p + 1), 0)
                        act.wait_ge(unit_done, i * 4 + (U_E[g] + 2 * p + 1))
                        act.wait_ge(slot_read[2 * p + 1], i + C_E[g][2 * p + 1])
                        act.activation(halves(tmp, p), slot(2 * p), ACT.Silu).then_inc(slot_read[2 * p], 1)
                        split_hi(i * 2 + (U_E[g] // 2 + p + 1), 1)
                        act.wait_ge(slot_read[2 * p + 1], i + (C_E[g][2 * p + 1] + 1))
                        act.activation(row(hid_hi, i * 2 + p), hf[:, p, :], ACT.Copy).then_inc(hidhi_ready, 1)
                if g < len(GROUPS) - 1:
                    with act.Fori(0, KT // 2) as i:
                        for s in range(2):
                            split_hi(i + (U_F[g] + 2) // 2, s)
            with act.Fori(0, KT // 2 - 1) as i:
                squares(i, U_F[-1], C_F[-1], 2 * KT)
            squares(KT // 2 - 1, U_F[-1], C_F[-1], 2 * KT, last=True)
            deviation(2, sum_done, 3)

        @block.tensor
        def _(pe):
            def unit(u, s, w, occupied, hi, lo, nkt, done=None, ready=None):
                pe.wait_ge(lo_ready, u + 1)
                pe.wait_ge(slot_read[s], occupied)
                for k in range(nkt):
                    if ready is not None:
                        ready(k)
                    for wt, parts in ((w_hi, (hi, lo)), (w_lo, (hi,))):
                        for src in parts:
                            for b in range(2):
                                last = pe.matmul(ps[:, 2 * s + b, 0:HALF], wt[:, w, k * P:k * P + P],
                                                 src[:, k, b * HALF:b * HALF + HALF],
                                                 start=(k == 0 and wt is w_hi and src is hi),
                                                 stop=(k == nkt - 1 and wt is w_lo))
                last.then_inc(unit_done, 1)

            def mean(s, weights, src, done):
                for b in range(2):
                    last = pe.matmul(ps[:, 2 * s + b, 0:HALF], weights[:, :], src[:, b * HALF:b * HALF + HALF],
                                     start=True, stop=True)
                last.then_inc(done, 1)

            def hlo_waits(base):
                def ready(k):
                    pe.wait_ge(hlo_odd if k % 2 else hlo_even, base + k // 2 + 1)
                return ready

            pe.wait_ge(consts_ready, 2)
            pe.wait_ge(sq_added, KT)
            mean(3, mean_d, acc, sum_done)
            pe.wait_ge(gstat_hi, 2)
            pe.wait_ge(gstat_lo, 2)
            for k in range(KT):
                hlo_waits(0)(k)
                for src in (h_hi, h_lo):
                    for b in range(2):
                        last = pe.matmul(ps[:, 4 + b, 0:HALF], gstat[:, k, :], src[:, k, b * HALF:b * HALF + HALF],
                                         start=(k == 0 and src is h_hi), stop=(k == KT - 1 and src is h_lo))
            last.then_inc(gates_done, 1)
            with pe.Fori(0, N_A // 4) as i:
                for j in range(4):
                    unit(i * 4 + j, j, j % 2, i + 1, h_hi, h_lo, KT)
            pe.wait_ge(slot_read[2], 3)
            pe.wait_ge(exps_out, 4)
            pe.wait_ge(masks_ready, 2)
            for n in range(NI):
                pe.transpose(ps[:, 4, n * NH:n * NH + NH], rows[:, n * P:n * P + P], ident[0:NH, 0:NH])
            for h in range(NH):
                last = pe.matmul(ps[:, 5, h * SB:h * SB + SB], sel[:, h, :], drow[:, :], start=True, stop=True)
            last.then_inc(turned, 1)
            for h in range(NH):
                s = 3 - h % 2
                pe.wait_ge(slot_read[s], (3 if s == 3 else 4) + h // 2)
                for b in range(2):
                    last = pe.matmul(ps[:, 2 * s + b, 0:HALF], sel[:, h, :], nrow[:, b * HALF:b * HALF + HALF],
                                     start=True, stop=True)
                last.then_inc(negm_spread, 1)
            pe.wait_ge(slot_read[3], 5)
            pe.wait_ge(slot_read[2], 6)

            with pe.Fori(0, NH) as h:
                def head_unit(j):
                    unit(h * PER_HEAD + (U_B + j), j % 2, j % 2, h * (PER_HEAD // 2) + (C_B + j // 2), h_hi, h_lo, KT)

                def use(k):
                    samples = (S_USE + 4, T_USE + 4, PV_USE + 4, HT_USE + 2)
                    if k + 1 in samples and k >= 3:
                        read(k - 3)
                    if k in samples:
                        return
                    if k == 0:
                        pe.wait_ge(act_read, h * ACT_USES + START)
                        pe.wait_ge(dve_read, h * DVE_USES + START)
                    elif k >= 4:
                        read(k - 4)

                def read(k):
                    if READER[k] == "act":
                        pe.wait_ge(act_read, h * ACT_USES + (READER[:k].count("act") + START + 1))
                    else:
                        pe.wait_ge(dve_read, h * DVE_USES + (READER[:k].count("dve") + START + 1))

                for j in range(6):
                    head_unit(j)
                for s in range(2):
                    pe.wait_ge(slot_read[s], h * (PER_HEAD // 2) + (C_B + 2))
                for s in range(5):
                    use(S_USE + s)
                    t0, n, rows_ = (s * P, TP - s * P, P) if s < NB else (TP, TS, TS)
                    for k in range(2):
                        last = pe.matmul(bank(S_USE + s)[0:rows_, 0:n], qkv[:, 1, k, t0:t0 + rows_],
                                         qkv[:, 0, k, t0:t0 + n], start=(k == 0), stop=(k == 1))
                    last.then_inc(attn_ready, 1)
                for s in range(2):
                    pe.wait_ge(slot_read[s], h * (PER_HEAD // 2) + (C_B + 3))
                for s in range(5):
                    use(T_USE + s)
                    n = P if s < NB else TS
                    for c in range(4):
                        last = pe.transpose(bank(T_USE + s)[0:n, c * P:c * P + P],
                                            qkv[:, 1 + c // 2, c % 2, s * P:s * P + n], ident[:, :])
                    last.then_inc(attn_ready, 1)
                use(I_USE)
                pe.wait_ge(qm_ready, h * 2 + 2)
                pe.wait_ge(cs_loaded, h * 16 + 16)
                for b in range(SB):
                    for k in range(2):
                        pe.matmul(bank(I_USE)[0:TS, 0:HD], qm[:, k, b * TS:b * TS + TS], cs[:, b, k, :],
                                  start=(b == 0 and k == 0), stop=(b == SB - 1 and k == 1))
                pe.wait_ge(n_loaded, 16)
                for k in range(2):
                    last = pe.matmul(bank(I_USE)[0:TS, HD:HD + SB], qkv[:, 0, k, TP:T],
                                     nst[:, bass.ds(h, 1), k, :].rearrange("p o b -> p (o b)"),
                                     start=(k == 0), stop=(k == 1))
                last.then_inc(attn_ready, 1)
                head_unit(6)
                head_unit(7)
                for t in range(5):
                    use(PV_USE + t)
                    if t == 0:
                        read(T_USE + 4)
                    if t < NB:
                        for s in range(t + 1):
                            o = W_OFF[s] + (t - s) * P
                            last = pe.matmul(bank(PV_USE + t)[:, 0:VE], wts[:, o:o + P], kvn[:, s, HD:2 * HD + 1],
                                             start=(s == 0), stop=(s == t))
                    else:
                        last = pe.matmul(bank(PV_USE + t)[0:TS, 0:VE], wts[0:TS, W_OFF[NB]:W_COLS],
                                         kvn[0:TS, NB, HD:2 * HD + 1], start=True, stop=True)
                    last.then_inc(attn_ready, 1)
                pe.wait_ge(wv_ready, h * (NB + SB) + (NB + SB))
                for k in range(2):
                    use(CP_USE + k)
                    for s in range(NB):
                        last = pe.matmul(bank(CP_USE + k)[:, 0:VE], kvn[:, s, k * P:k * P + P], wvn[:, s, :],
                                         start=(s == 0), stop=(s == NB - 1))
                    last.then_inc(attn_ready, 1)
                for b in range(SB):
                    use(CS_USE + b)
                    for k in range(2):
                        last = pe.matmul(bank(CS_USE + b)[:, k * HD:k * HD + HD], kvn[0:TS, NB, k * P:k * P + P],
                                         wvs[0:TS, b, :], start=True, stop=True)
                    last.then_inc(attn_ready, 1)
                use(N_USE)
                for k in range(2):
                    last = pe.matmul(bank(N_USE)[:, k * SB:k * SB + SB], kvn[0:TS, NB, k * P:k * P + P],
                                     wb[0:TS, bass.ds(h, 1), :].rearrange("p o b -> p (o b)"), start=True, stop=True)
                last.then_inc(attn_ready, 1)
                head_unit(8)
                head_unit(9)
                pe.wait_ge(hm_ready, h * 5 + 5)
                for v in range(2):
                    use(HT_USE + v)
                    for s in range(NB):
                        last = pe.transpose(bank(HT_USE + v)[:, s * P:s * P + P], num[:, s, v * P:v * P + P],
                                            ident[:, :])
                    last.then_inc(attn_ready, 1)
                use(HT_USE + 2)
                for v in range(2):
                    last = pe.transpose(bank(HT_USE + 2)[:, v * TS:v * TS + TS], num[0:TS, NB, v * P:v * P + P],
                                        ident[0:TS, 0:TS])
                last.then_inc(attn_ready, 1)

            def ga_pair(i):
                for s in range(2):
                    unit(i * 2 + (U_GA + s), s, s, i + C_GA, h_hi, h_lo, KT)

            with pe.Fori(0, 2) as i:
                ga_pair(i)
            pe.wait_ge(act_read, START + NH * ACT_USES)
            pe.wait_ge(dve_read, START + NH * DVE_USES)
            pe.wait_ge(csum_ready, 1)
            mean(2, mean_c, acc, cstat_done)
            ga_pair(2)
            pe.wait_ge(csum_ready, 2)
            mean(3, mean_c, acc, cstat_done)
            ga_pair(3)

            def two_units(base, count_before, hi, lo, nkt, ready_sem, ready_base):
                with pe.Fori(0, KT // 2) as i:
                    for s in range(2):
                        unit(i * 2 + (base + s), s, s, i + count_before, hi, lo, nkt,
                             ready=(lambda k: pe.wait_ge(ready_sem, ready_base + k + 1)) if s == 0 else None)

            two_units(U_CO, C_CO, c_hi, c_lo, CT, clo_ready, 0)
            two_units(U_O, C_O, h_hi, h_lo, KT, mlo_ready, 0)
            pe.wait_ge(sq_added, 2 * KT)
            pe.wait_ge(slot_read[2], 7)
            mean(2, mean_d, acc, sum_done)
            for g, n in enumerate(GROUPS):
                with pe.Fori(0, n // 2) as i:
                    for j in range(4):
                        unit(i * 4 + (U_E[g] + j), j, j % 2, i + C_E[g][j], h_hi, h_lo, KT,
                             ready=hlo_waits(KT // 2) if j == 0 else None)
                two_units(U_F[g], C_F[g], hid_hi, hid_lo, n, hidlo_ready, START + Q_E[g])
            pe.wait_ge(sq_added, 3 * KT)
            pe.wait_ge(slot_read[2], C2_END)
            mean(2, mean_d, acc, sum_done)

        @block.vector
        def _(dve):
            steps = Tally(dve, dve_step)

            def split_lo(u, s):
                dve.wait_ge(hi_ready, u + 1)
                dve.tensor_tensor(w_lo[:, s, :], raw[:, s, :], w_hi[:, s, :].bitcast(F32), ALU.subtract)\
                    .then_inc(lo_ready, 1)

            def add_square(k, n):
                dve.wait_ge(sq_ready, n)
                if k == 0:
                    dve.tensor_copy(acc[:, :], tmp[:, 0, :]).then_inc(sq_added, 1)
                else:
                    dve.wait_ge(sq_added, n - 1)
                    dve.tensor_tensor(acc[:, :], acc[:, :], tmp[:, k % 2, :], ALU.add).then_inc(sq_added, 1)

            def rstd(s, contents, n):
                dve.wait_ge(slot_read[s], contents)
                dve.reciprocal(rs[:, :], rs[:, :]).then_inc(rs_ready, 1)

            def normalise(done, gain, n, s, contents):
                rstd(s, contents, n)
                dve.wait_ge(rs_ready, n)
                for k in range(KT):
                    if k >= 2:
                        if k % 2:
                            dve.wait_ge(hlo_odd, done // 2 + (k - 1) // 2)
                        else:
                            dve.wait_ge(hlo_even, done // 2 + k // 2)
                    dve.scalar_tensor_tensor(hf[:, k % 2, :], x[:, k, :], vcol(gain + k), rs[:, :], ALU.mult, ALU.mult)\
                        .then_inc(hf_ready, 1)
                    if k % 2 == 0 and k:
                        lo_odd(done, k - 1)
                lo_odd(done, KT - 1)

            def lo_odd(done, k):
                dve.wait_ge(hhi_ready, done + k + 1)
                dve.tensor_tensor(h_lo[:, k, :], hf[:, 1, :], h_hi[:, k, :].bitcast(F32), ALU.subtract)\
                    .then_inc(hlo_odd, 1)


            for k in range(KT):
                add_square(k, k + 1)
            split_lo(0, 0)
            split_lo(1, 1)
            for g in range(2):
                dve.wait_ge(gstat_hi, g + 1)
                dve.tensor_tensor(gstat[:, :, 64 * g + 32:64 * g + 32 + NH], gw[:, :, NH * g:NH * g + NH],
                                  gstat[:, :, 64 * g:64 * g + NH].bitcast(F32), ALU.subtract).then_inc(gstat_lo, 1)
            dve.wait_ge(vec_loaded, 16)
            normalise(0, V_GMIX, 1, 3, 1)
            dve.wait_ge(gates_done, 1)
            dve.wait_ge(gb_loaded, 16)
            for g, dst in enumerate((li, fz)):
                dve.wait_ge(gt_ready, g + 1)
                ins = dve.scalar_tensor_tensor(flat(dst), ps[64 * g:64 * g + NH, 4:6, 0:HALF], gb[:, g:g + 1],
                                               gt[:, g, :].rearrange("p (b n) -> p b n", b=2), ALU.add, ALU.add)
                if g:
                    ins.then_inc(slot_read[2], 1)
                else:
                    steps.on(ins)
            dve.wait_ge(slot_read[2], 1)
            dve.scalar_tensor_tensor(ft[:, :], fz[:, :], -1.0, fz[:, :], ALU.mult, ALU.max).then_inc(fabs_ready, 1)

            dve.wait_ge(pool_step, POOL_SET)
            with dve.Fori(0, N_A // 4) as i:
                steps.loop(i, 4)
                for j in range(4):
                    split_lo(i * 4 + (U_A + j + 2), j % 2)
                    if j % 2 == 0:
                        continue
                    pair = i * 2 + j // 2
                    dve.wait_ge(slot_read[j], i + 2)
                    bias, sg, v = vcol(i * 4 + (j - 1)), tmp[:, j // 2, :], ps[:, 2 * (j - 1):2 * (j - 1) + 2, :]
                    ap = row(a_p, pair)[:, PAST:PAST + TP]
                    as_ = a_s[:, bass.ds(pair, 1), :, PAST:PAST + SL].rearrange("p o b n -> p (o b) n")
                    steps.on(dve.scalar_tensor_tensor(ap[:, 0:HALF], v[:, 0, 0:HALF], bias, sg[:, 0:HALF],
                                                      ALU.add, ALU.mult))
                    steps.on(dve.scalar_tensor_tensor(ap[:, HALF:TP], v[:, 1, 0:TP - HALF], bias, sg[:, HALF:TP],
                                                      ALU.add, ALU.mult))
                    dve.scalar_tensor_tensor(as_, v[:, 1, TP - HALF:HALF].rearrange("p (b n) -> p b n", b=SB), bias,
                                             sg[:, TP:T].rearrange("p (b n) -> p b n", b=SB), ALU.add, ALU.mult)\
                        .then_inc(slot_read[j - 1], 1)
                steps.end(2)

            dve.wait_ge(ln_ready, 1)
            steps.on(dve.scalar_tensor_tensor(lf[:, :], fz[:, :], 0.0, ft[:, :], ALU.min, ALU.subtract))
            steps.on(dve.tensor_copy(lim[:, :], li[:, :]))
            steps.settle()
            dve.wait_ge(m0_loaded, 16)
            first = slice(TP, T, SL)
            steps.on(dve.tensor_tensor(t8[:, :], lf[:, first], m0[:, :], ALU.add))
            steps.on(dve.tensor_copy(lfm[:, :], lf[:, :]))
            steps.on(dve.tensor_tensor_scan(ft[:, :], seg[:, :], lf[:, :], 0.0, ALU.mult, ALU.add))
            steps.settle()
            steps.on(dve.tensor_tensor(lim[:, first], t8[:, :], li[:, first], ALU.max))
            steps.on(dve.memset(lfm[:, first], -BIG))
            steps.settle()
            steps.on(dve.tensor_tensor(rows[:, 0:T], li[:, :], ft[:, :], ALU.subtract))
            dve.tensor_tensor_scan(mrow[:, :], lfm[:, :], lim[:, :], 0.0, ALU.add, ALU.max).then_inc(mrow_ready, 1)
            dve.wait_ge(mrow_ready, 1)
            end = slice(TP + SL - 1, T, SL)
            steps.on(dve.tensor_tensor(nrow[:, :], ft[:, :], mrow[:, :], ALU.subtract))
            steps.on(dve.tensor_tensor(t8[:, :], ft[:, end], mrow[:, end], ALU.subtract))
            steps.on(dve.tensor_copy(mend[:, :], mrow[:, end]))

            def total(t):
                return ft[:, t * P + P - 1:t * P + P]

            def item(n):
                return rows[:, n * P:n * P + P]

            for t in range(NB):
                steps.settle()
                for s in range(t + 1):
                    src = item(I_G + s) if s == t else item(OFF[s, t])
                    if t < NB - 1:
                        steps.on(dve.tensor_scalar(item(OFF[s, t + 1]), src, total(t), None, ALU.add))
                    else:
                        steps.on(dve.tensor_scalar(item(I_WS + s), src, total(t), mrow[:, TP - 1:TP],
                                                   ALU.add, ALU.subtract))

            def per_sample(t):
                return t.rearrange("p (b j) -> p b j", b=SB)

            def spread(t):
                return t.unsqueeze(2).broadcast_to([NH, SB, SL])

            steps.on(dve.tensor_tensor(per_sample(rows[:, I_WS * P + TP:I_WS * P + T]), per_sample(rows[:, TP:T]),
                                       spread(t8[:, :]), ALU.add))
            steps.on(dve.tensor_tensor(per_sample(rows[:, I_WI * P:I_WI * P + TS]), per_sample(nrow[:, TP:T]),
                                       spread(m0[:, :]), ALU.add))
            steps.settle()
            dve.tensor_tensor(t8[:, :], t8[:, :], m0[:, :], ALU.add).then_inc(exps_in, 1)
            dve.wait_ge(turned, 1)
            steps.on(dve.tensor_copy(dec[:, :, :].rearrange("p h b -> p (h b)"), ps[:, 5, 0:NH * SB]))
            dve.tensor_copy(cols[:, :, :].rearrange("p i h -> p (i h)"), ps[:, 4, 0:NI * NH]).then_inc(slot_read[2], 1)
            dve.wait_ge(slot_read[2], 4)
            dve.wait_ge(masks_ready, 2)
            dve.wait_ge(n_loaded, 16)
            steps.on(dve.tensor_tensor(wb[0:TS, :, :], cols[0:TS, I_WS + NB, :].unsqueeze(2).broadcast_to([TS, NH, SB]),
                                       onehot[0:TS, :].unsqueeze(1).broadcast_to([TS, NH, SB]), ALU.mult))
            for k in range(2):
                steps.on(dve.tensor_tensor(nnew[:, :, k, :], nst[:, :, k, :], dec[:, :, :], ALU.mult))
            steps.settle()
            dve.wait_ge(slot_read[2], 6)
            dve.wait_ge(slot_read[3], 5)
            dve.wait_ge(head_bufs_set, 3)
            dve.wait_ge(cache_loaded, 16)
            dve.wait_ge(slot_read[0], C_B)
            dve.wait_ge(slot_read[2], 3)

            with dve.Fori(0, NH) as h:
                steps.loop(h, DVE_HEAD_STEPS)
                tap = [0]

                def lo_of(j):
                    split_lo(h * PER_HEAD + (U_B + j + 2), j % 2)
                    for _ in range(CONV_TAPS[j]):
                        conv_tap(tap[0])
                        tap[0] += 1

                def conv_tap(w):
                    out = row(conv, h)
                    wcol = vcol(h * CW + (V_WDW + w))
                    outs = (out[:, 0:TP], out[:, TP:T].rearrange("p (b j) -> p b j", b=SB))
                    ins = (row(a_p, h)[:, w:w + TP],
                           a_s[:, bass.ds(h, 1), :, w:w + SL].rearrange("p o b n -> p (o b) n"))
                    for o, a in zip(outs, ins):
                        if w == 0:
                            steps.on(dve.tensor_scalar(o, a, wcol, vcol(h + V_BDW), ALU.mult, ALU.add))
                        else:
                            steps.settle(back=1)
                            steps.on(dve.scalar_tensor_tensor(o, a, wcol, o, ALU.mult, ALU.add))

                def use(k):
                    dve.wait_ge(attn_ready, h * USES + (k + 1))

                def evacuated(s, n):
                    dve.wait_ge(slot_read[s], h * (PER_HEAD // 2) + (C_B + n))

                def hcol(item, parts=P):
                    return cols[0:parts, item, bass.ds(h, 1)]

                nh = row(negm, h)
                steps.on(dve.tensor_tensor(mdiag[:, :, :], nh[:, 0:TP].rearrange("p (s t) -> p s t", s=NB),
                                           cmask[:, :].unsqueeze(1).broadcast_to([P, NB, P]), ALU.add))
                dve.tensor_tensor(msamp[0:TS, :], nh[0:TS, TP:T], smask[0:TS, :], ALU.add).then_inc(mdiag_ready, 1)
                lo_of(0)
                lo_of(1)
                for j in (2, 3):
                    lo_of(j)
                    dve.wait_ge(unit_done, h * PER_HEAD + (U_B + j + 1))
                    dve.tensor_scalar(halves(qkv[:, 1, :, :], j - 2), slot(j % 2), vcol(h * PER_HEAD + (U_B + j)),
                                      HD ** -0.5, ALU.add, ALU.mult).then_inc(slot_read[j % 2], 1)
                for k in range(2):
                    evacuated(k, 1)
                    dve.tensor_copy(qm[:, k, :].rearrange("p (b t) -> p b t", b=SB)[:, :, 0:SL],
                                    qkv[:, 0, k, TP:T].rearrange("p (b j) -> p b j", b=SB)).then_inc(qm_ready, 1)
                lo_of(4)
                lo_of(5)
                for s in range(5):
                    use(S_USE + s)
                    dve.wait_ge(w_ready, h * 11 + (4, 7, 9, 10, 11)[s])
                    parts, o, n = (P, W_OFF[s], TP - s * P) if s < NB else (TS, W_OFF[s], TS)
                    dve.tensor_tensor(wts[0:parts, o:o + n], bank(S_USE + s)[0:parts, 0:n], wts[0:parts, o:o + n],
                                      ALU.mult).then_inc(dve_read, 1)
                use(I_USE)
                for s in range(NB):
                    dve.wait_ge(act_read, h * ACT_USES + (START + s + 1))
                    dve.tensor_scalar(wvn[:, s, :], kvn[:, s, HD:2 * HD + 1], hcol(I_WS + s), None, ALU.mult)\
                        .then_inc(wv_ready, 1)
                dve.wait_ge(act_read, h * ACT_USES + (START + 5))
                for b in range(SB):
                    dve.tensor_scalar(wvs[0:TS, b, :], kvn[0:TS, NB, HD:2 * HD],
                                      wb[0:TS, bass.ds(h, 1), b:b + 1].rearrange("p o b -> p (o b)"), None, ALU.mult)\
                        .then_inc(wv_ready, 1)
                lo_of(6)
                lo_of(7)
                for b in range(SB):
                    use(CS_USE + b)
                    c = cs[:, b, :, :].rearrange("p k v -> p (k v)")
                    dve.scalar_tensor_tensor(c, c, dec[:, bass.ds(h, 1), b:b + 1].rearrange("p o b -> p (o b)"),
                                             bank(CS_USE + b), ALU.mult, ALU.add).then_inc(dve_read, 1)
                use(N_USE)
                nn = nnew[:, bass.ds(h, 1), :, :].rearrange("p o k b -> p (o k b)")
                dve.tensor_tensor(nn, nn, bank(N_USE)[:, 0:2 * SB], ALU.add).then_inc(dve_read, 1)
                dve.wait_ge(act_read, h * ACT_USES + (START + 11))
                wi = hcol(I_WI, TS)
                steps.on(dve.tensor_tensor(nq8[0:TS, :], inter[0:TS, HD:HD + SB], onehot[0:TS, :], ALU.mult))
                steps.on(dve.scalar_tensor_tensor(num[0:TS, NB, 0:HD], inter[0:TS, 0:HD], wi, num[0:TS, NB, 0:HD],
                                                  ALU.mult, ALU.add))
                steps.settle(back=1)
                steps.on(dve.reduce_sum(nq1[0:TS, :], nq8[0:TS, :], axis=mybir.AxisListType.X))
                steps.settle()
                steps.on(dve.scalar_tensor_tensor(num[0:TS, NB, HD:VE], nq1[0:TS, :], wi, num[0:TS, NB, HD:VE],
                                                  ALU.mult, ALU.add))
                for i in range(5):
                    steps.on(dve.bn_stats(stats[:, i, :], num[:, i, 0:HD]))
                em = cols[:, I_EM:I_EM + 5, bass.ds(h, 1)].rearrange("p i o -> p (i o)")
                steps.settle()
                steps.on(dve.scalar_tensor_tensor(small[:, 0, :], num[:, :, HD], -1.0, num[:, :, HD],
                                                  ALU.mult, ALU.max))
                for i in range(5):
                    steps.on(dve.bn_aggr(mv[:, i, :], stats[:, i, :]))
                steps.settle()
                steps.on(dve.tensor_tensor(small[:, 0, :], small[:, 0, :], em, ALU.max))
                steps.settle()
                steps.on(dve.reciprocal(small[:, 0, :], small[:, 0, :]))
                steps.settle()
                steps.on(dve.tensor_tensor(small[:, 1, :], mv[:, :, 1], small[:, 0, :], ALU.mult))
                steps.settle()
                dve.tensor_tensor(small[:, 1, :], small[:, 1, :], small[:, 0, :], ALU.mult).then_inc(hvar_ready, 1)
                dve.wait_ge(hdev_ready, h + 1)
                steps.on(dve.reciprocal(small[:, 2, :], small[:, 2, :]))
                steps.settle()
                steps.on(dve.tensor_tensor(small[:, 3, :], small[:, 2, :], small[:, 0, :], ALU.mult))
                steps.settle()
                for i in range(5):
                    dve.tensor_scalar(num[:, i, 0:HD], num[:, i, 0:HD], mv[:, i, 0:1], small[:, 3, i:i + 1],
                                      ALU.subtract, ALU.mult).then_inc(hm_ready, 1)
                for j in (8, 9):
                    lo_of(j)
                    evacuated(j % 2, 5)
                    m = row(merged, h * 2 + (j - 8))
                    dve.tensor_tensor(m, m, tmp[:, j % 2, :], ALU.mult).then_inc(gb_used, 1)
                assert tap[0] == CW
                dve.wait_ge(gb_used, h * 2 + (START + 2))
                for v in range(2):
                    use(HT_USE + v)
                    m = row(merged, h * 2 + v)[:, 0:TP]
                    dve.scalar_tensor_tensor(m, bank(HT_USE + v), vcol(h * 2 + (V_GMN + v)), m, ALU.mult, ALU.mult)\
                        .then_inc(dve_read, 1)
                use(HT_USE + 2)
                for v in range(2):
                    m = row(merged, h * 2 + v)[:, TP:T]
                    ins = dve.scalar_tensor_tensor(m, bank(HT_USE + 2)[:, v * TS:v * TS + TS],
                                                   vcol(h * 2 + (V_GMN + v)), m, ALU.mult, ALU.mult)
                    if v:
                        ins.then_inc(dve_read, 1)
                    else:
                        steps.on(ins)
                steps.end(NH)

            with dve.Fori(0, 3) as i:
                for s in range(2):
                    split_lo(i * 2 + (U_GA + s + 2), s)
            rstd(3, 6, 2)
            for s in range(2):
                split_lo(3 * 2 + (U_GA + s + 2), s)
            dve.wait_ge(dve_read, START + NH * DVE_USES)
            with dve.Fori(0, KT // 2) as i:
                for s in range(2):
                    split_lo(i * 2 + (U_CO + s + 2), s)
                    dve.wait_ge(slot_read[s], i + (C_GA + 1))
                    dve.wait_ge(unit_done, i * 2 + (U_CO + s + 1))
                    g = halves(ga, i * 2 + s)
                    dve.tensor_tensor(g, slot(s), g, ALU.mult).then_inc(slot_read[s], 1)
                    dve.wait_ge(slot_read[s], i + (C_CO + 1))
                    m = row(merged, i * 2 + s)
                    dve.tensor_tensor(m, m, row(ga, i * 2 + s), ALU.add).then_inc(m_ready, 1)

            def add_units(i, base, contents, sq_base=None, last=False):
                for s in range(2):
                    if not last:
                        split_lo(i * 2 + (base + s + 2), s)
                    dve.wait_ge(unit_done, i * 2 + (base + s + 1))
                    xs = halves(x, i * 2 + s)
                    dve.tensor_tensor(xs, slot(s), xs, ALU.add).then_inc(slot_read[s], 1)
                    if sq_base is not None:
                        dve.wait_ge(sq_ready, i * 2 + (sq_base + s + 1))
                        dve.wait_ge(sq_added, i * 2 + (sq_base + s))
                        dve.tensor_tensor(acc[:, :], acc[:, :], tmp[:, s, :], ALU.add).then_inc(sq_added, 1)

            dve.wait_ge(slot_read[3], 6)
            dve.wait_ge(cstat_done, 2)
            dve.memset(acc[:, :], 0.0).then_inc(acc_zero, 1)
            dve.wait_ge(acc_zero, 1)
            with dve.Fori(0, KT // 2) as i:
                add_units(i, U_O, C_O, KT)
            normalise(KT, V_GFFN, 3, 2, 8)
            dve.memset(acc[:, :], 0.0).then_inc(acc_zero, 1)
            dve.wait_ge(acc_zero, 2)
            dve.wait_ge(hlo_even, KT)
            for g, n in enumerate(GROUPS):
                with dve.Fori(0, n // 2) as i:
                    for p in range(2):
                        split_lo(i * 4 + (U_E[g] + 2 * p + 2), 0)
                        split_lo(i * 4 + (U_E[g] + 2 * p + 3), 1)
                        dve.wait_ge(slot_read[2 * p], i + (C_E[g][2 * p] + 1))
                        dve.wait_ge(hidlo_ready, i * 2 + (START + Q_E[g]))
                        dve.wait_ge(unit_done, i * 4 + (U_E[g] + 2 * p + 2))
                        dve.tensor_tensor(halves(hf, p), slot(2 * p + 1), halves(tmp, p), ALU.mult)\
                            .then_inc(slot_read[2 * p + 1], 1)
                if g < len(GROUPS) - 1:
                    with dve.Fori(0, KT // 2) as i:
                        add_units(i, U_F[g], C_F[g])
            with dve.Fori(0, KT // 2 - 1) as i:
                add_units(i, U_F[-1], C_F[-1], 2 * KT)
            add_units(KT // 2 - 1, U_F[-1], C_F[-1], 2 * KT, last=True)
            rstd(2, C2_END + 1, 4)
            dve.wait_ge(rs_ready, 4)
            for k in range(KT):
                dve.scalar_tensor_tensor(x[:, k, :], x[:, k, :], vcol(V_GFIN + k), rs[:, :], ALU.mult, ALU.mult)\
                    .then_inc(y_ready, 1)


def kernel(**inputs):
    import concourse.bacc as bacc
    from concourse.bass_utils import run_bass_kernel_spmd

    a = {k: np.asarray(v) for k, v in inputs.items()}

    def blocks(w):
        k, n = w.shape[0] // P, w.shape[1] // P
        return w.reshape(k, P, n, P).transpose(2, 1, 0, 3).reshape(n, P, k * P)

    def per_tile(v):
        return v.reshape(-1, P).T

    w_in, b_in = a["w_in"][0], a["b_in"][0]
    sizes = [DC, DC] + [NH * HD] * 4 + [NH, NH, D, D]
    at = np.cumsum([0] + sizes)
    cut = [slice(int(at[i]), int(at[i + 1])) for i in range(len(sizes))]
    wb = {n: blocks(w_in[:, cut[i]]) for n, i in zip("cv cg q k v og ga gb".split(), (0, 1, 2, 3, 4, 5, 8, 9))}
    bb = {n: b_in[cut[i]].reshape(-1, P) for n, i in zip("cv cg q k v og ga gb".split(), (0, 1, 2, 3, 4, 5, 8, 9))}

    def heads(d):
        return np.concatenate([d[n][2 * h:2 * h + 2] for h in range(NH) for n in ("q", "k", "v", "og", "gb")])

    def pairs(p, q):
        return np.stack([p, q], 1).reshape((-1,) + p.shape[1:])

    vecs = np.concatenate(
        [pairs(bb["cv"], bb["cg"]).T, heads(bb).T, bb["ga"].T]
        + [per_tile(a[n].reshape(-1)) for n in ("g_mix_norm", "g_ffn_norm", "g_final", "g_mlstm_norm",
                                                "g_conv_norm", "b_conv_norm", "b_dwconv")]
        + [a["w_dwconv"][0].reshape(CW, CT, P).transpose(2, 1, 0).reshape(P, CT * CW)], axis=1)
    wfi = blocks(a["w_ffn_in"][0])
    wfo = a["w_ffn_out"][0]
    rows_of = np.cumsum([0] + [P * g for g in GROUPS])
    x_all = np.concatenate([a["x_prompt"].reshape(TP, D), a["x_sample"].reshape(TS, D)])
    ins = {
        "xT": x_all.reshape(T, KT, P).transpose(2, 1, 0),
        "vecs": vecs,
        "gate_w": w_in[:, cut[6].start:cut[7].stop].reshape(KT, P, 2 * NH).transpose(1, 0, 2),
        "gate_b": np.stack([b_in[cut[6]], b_in[cut[7]]], 1),
        "cache": a["cache_conv"][0].reshape(SB, PAST, CT, P).transpose(3, 2, 0, 1),
        "w_cvcg": pairs(wb["cv"], wb["cg"]),
        "w_head": heads(wb),
        "w_ga": wb["ga"],
        "w_co": blocks(a["w_conv_out"][0]),
        "w_o": blocks(a["w_out"][0]),
        "w_fi": pairs(wfi[:FT], wfi[FT:]),
        "w_fo0": blocks(wfo[rows_of[0]:rows_of[1]]),
        "w_fo1": blocks(wfo[rows_of[1]:rows_of[2]]),
        "w_fo2": blocks(wfo[rows_of[2]:rows_of[3]]),
        "st_c": a["state_mlstm_C"][0].reshape(SB, NH, HD, 2, P).transpose(1, 4, 0, 3, 2),
        "st_n": a["state_mlstm_n"][0].reshape(SB, NH, 2, P).transpose(3, 1, 2, 0),
        "st_m": a["state_mlstm_m"][0].T,
    }
    outs = {
        "y": (P, KT, T), "conv_p": (P, CT, PAST), "conv_s": (P, CT, SB, PAST), "cn_p": (NH, P, 2, VE),
        "m_p": (NH, 1), "c_s": (NH, P, SB, 2, HD), "n_s": (P, NH, 2, SB), "m_s": (NH, SB),
    }
    nc = bacc.Bacc("TRN2", target_bir_lowering=False, num_devices=1)
    ins = {f"{k}_in": np.ascontiguousarray(v) for k, v in ins.items()}
    args = [nc.dram_tensor(k, v.shape, F32, kind="ExternalInput").ap() for k, v in ins.items()]
    args += [nc.dram_tensor(f"{k}_out", v, F32, kind="ExternalOutput").ap() for k, v in outs.items()]
    build(nc, *args)
    res = run_bass_kernel_spmd(nc, [ins], core_ids=[0]).results[0]
    r = {k: res[f"{k}_out"] for k in outs}

    yt = r["y"].transpose(2, 1, 0).reshape(T, D)
    cn = r["cn_p"].transpose(0, 3, 2, 1).reshape(NH, VE, HD)
    c = np.ascontiguousarray
    return (c(yt[:TP]).reshape(1, TP, D), c(yt[TP:]).reshape(SB, SL, D),
            c(r["conv_p"].transpose(2, 1, 0)).reshape(1, 1, PAST, DC),
            c(cn[:, :HD]).reshape(1, 1, NH, HD, HD), c(cn[:, HD]).reshape(1, 1, NH, HD),
            c(r["m_p"]).reshape(1, 1, NH),
            c(r["conv_s"].transpose(2, 3, 1, 0)).reshape(1, SB, PAST, DC),
            c(r["c_s"].transpose(2, 0, 4, 3, 1)).reshape(1, SB, NH, HD, HD),
            c(r["n_s"].transpose(3, 1, 2, 0)).reshape(1, SB, NH, HD),
            c(r["m_s"].T).reshape(1, SB, NH))
```

```python
from contextlib import ExitStack

import numpy as np

import concourse.bass as bass
from concourse import mybir

F32 = mybir.dt.float32
F32R = mybir.dt.float32r
ALU = mybir.AluOpType
ACT = mybir.ActivationFunctionType

P = 128
D = 1024
KT = D // P
TP, TS = 512, 64
T = TP + TS
HALF = T // 2
SB, SL = 8, 8
NH, HD = 4, 256
VE = HD + 1
NB = TP // P
DC = 512
CT = DC // P
CW = 31
PAST = CW - 1
FF = 2816
FT = FF // P
GROUPS = (8, 8, 6)
EPS = 1e-6
BIG = 1e30

U_A = 0
N_A = 2 * CT
U_B = U_A + N_A
PER_HEAD = 10
U_GA = U_B + NH * PER_HEAD
U_CO = U_GA + KT
N_CO = KT // 2
U_O = U_CO + N_CO
U_FF = U_O + KT
U_E, U_F, Q_E = [], [], []
_u, _q = U_FF, 0
for _g in GROUPS:
    U_E.append(_u)
    U_F.append(_u + 2 * _g)
    Q_E.append(_q)
    _u += 2 * _g + KT
    _q += _g
NU = _u

V_BIAS = 0
V_GMIX = U_CO
V_GFFN = V_GMIX + KT
V_GFIN = V_GFFN + KT
V_GMN = V_GFIN + KT
V_GCN = V_GMN + KT
V_BCN = V_GCN + CT
V_BDW = V_BCN + CT
V_WDW = V_BDW + CT
NV = V_WDW + CT * CW

I_G = 0
I_EM = 5
I_WS = 10
I_OFF = 15
I_WI = 21
NI = 22
OFF = {}
for _s in range(NB):
    for _t in range(_s + 1, NB):
        OFF[_s, _t] = I_OFF + len(OFF)

S_USE, T_USE, I_USE, PV_USE, CP_USE, CS_USE, N_USE, HT_USE = 0, 5, 10, 11, 16, 18, 26, 27
USES = 30
READER = ["dve"] * 5 + ["act"] * 5 + ["act"] + ["act"] * 5 + ["act"] * 2 + ["dve"] * 8 + ["dve"] + ["dve"] * 3
ACT_USES, DVE_USES = READER.count("act"), READER.count("dve")
W_OFF = [0, 512, 896, 1152, 1280]
W_COLS = 1280 + TS

START = 1
C_B = START + N_A // 2
C_GA = C_B + NH * PER_HEAD // 2
C_CO = C_GA + KT // 2
C_O = C_CO + N_CO // 2
C2_HEADS, C3_HEADS = 4, 3
C2_CO, C3_CO = C2_HEADS + 1, C3_HEADS + 1
C2_NORM = C2_CO + N_CO // 2
C_E, C_F = [], []
_c, _c2, _c3 = C_O + 4, C2_NORM + 1, C3_CO + N_CO // 2
for _g in GROUPS:
    C_E.append((_c, _c, _c2, _c3))
    C_F.append(_c + _g // 2)
    _c, _c2, _c3 = _c + _g // 2 + 4, _c2 + _g // 2, _c3 + _g // 2
C2_END = _c2

POOL_SET = 16
DVE_HEAD_STEPS = 84
CONV_TAPS = (3, 4, 3, 2, 4, 4, 4, 4, 2, 1)


class Tally:

    def __init__(self, eng, sem):
        self.eng, self.sem, self.n, self.turn = eng, sem, 0, 0

    def on(self, ins):
        ins.then_inc(self.sem, 1)
        self.n += 1

    def settle(self, back=0):
        self.eng.wait_ge(self.sem, self.turn + (self.n - back))

    def loop(self, i, per):
        self.start, self.per, self.turn = self.n, per, i * per

    def end(self, iters):
        assert self.n - self.start == self.per, f"per iteration: {self.n - self.start}, not {self.per}"
        self.n, self.turn = self.start + iters * self.per, 0


def build(nc, xT, vecs, gate_w, gate_b, cache, w_cgcv, w_head, w_ga, w_co, w_o, w_fi, w_fo0, w_fo1, w_fo2,
          st_c, st_n, st_m, y, conv_p, conv_s, cn_p, m_p, c_s, n_s, m_s):
    with ExitStack() as ctx:
        place = [-(-nc.sbuf_base // 32) * 32]

        def sb(name, cols, dt=F32, parts=P):
            shape = [parts] + (list(cols) if isinstance(cols, (list, tuple)) else [cols])
            t = nc.alloc_sbuf_tensor_at(name, shape, dt, offset=place[0])
            place[0] += -(-4 * int(np.prod(shape[1:])) // 32) * 32
            return t

        def sem(name):
            return ctx.enter_context(nc.semaphore(name))

        x = sb("x", [KT, T])
        h_hi = sb("h_hi", [KT, T], F32R)
        h_lo = sb("h_lo", [KT, T], F32R)
        raw = sb("raw", [2, KT * P])
        w_hi = sb("w_hi", [2, KT * P], F32R)
        w_lo = sb("w_lo", [2, KT * P], F32R)
        vec = sb("vec", NV)
        mean_d = sb("mean_d", P)
        mean_c = sb("mean_c", P)
        eps = sb("eps", 1)
        tmp = sb("tmp", [2, T])
        hf = sb("hf", [2, T])
        acc = sb("acc", T)
        rs = sb("rs", T)
        merged_base = place[0]
        merged = sb("merged", [KT, T])
        conv = sb("conv", [CT, T])
        ident = sb("ident", P)
        xg_hi = nc.alloc_sbuf_tensor_at("xg_hi", [P, KT, T], F32R, offset=merged_base)
        pool_base = place[0]
        a_p = sb("a_p", [CT, PAST + TP])
        a_s = sb("a_s", [CT, SB, PAST + SL])
        negm = sb("negm", [NH, T])
        cols = sb("cols", [NI, NH])
        dec = sb("dec", [NH, SB])
        onehot = sb("onehot", SB)
        wb = sb("wb", [NH, SB])
        nst = sb("nst", [NH, 2, SB])
        nnew = sb("nnew", [NH, 2, SB])
        cmask = sb("cmask", P)
        smask = sb("smask", TS)
        head_base = place[0]
        gw = sb("gw", [KT, 2 * NH])
        gstat = sb("gstat", [KT, P], F32R)
        gt = sb("gt", [2, T], parts=NH)
        gb = sb("gb", 2, parts=NH)
        m0 = sb("m0", SB, parts=NH)
        li = sb("li", T, parts=NH)
        fz = sb("fz", T, parts=NH)
        lf = sb("lf", T, parts=NH)
        ft = sb("ft", T, parts=NH)
        seg = sb("seg", T, parts=NH)
        lfm = sb("lfm", T, parts=NH)
        lim = sb("lim", T, parts=NH)
        mrow = sb("mrow", T, parts=NH)
        nrow = sb("nrow", T, parts=NH)
        rows = sb("rows", NI * P, parts=NH)
        t8 = sb("t8", SB, parts=NH)
        mend = sb("mend", SB, parts=NH)
        drow = sb("drow", SB, parts=NH)
        sel = sb("sel", [NH, P], parts=NH)
        xg_lo = sb("xg_lo", [KT, T], F32R)
        assert place[0] <= nc.sbuf_usable_end
        place[0] = head_base
        qkv = sb("qkv", [3, 2, T])
        qk_flat = qkv[:, :, :, :].rearrange("p a b n -> p (a b n)")
        wvn = qk_flat[:, 0:NB * VE].rearrange("p (s v) -> p s v", s=NB)
        wvs = qk_flat[:, 2 * T:2 * T + SB * HD].rearrange("p (b v) -> p b v", b=SB)
        kvn = sb("kvn", [5, 2 * HD + 1])
        num = sb("num", [5, VE])
        wts = sb("wts", W_COLS)
        mdiag = sb("mdiag", [NB, P])
        msamp = sb("msamp", TS)
        qm = sb("qm", [2, SB * (TS + SL)])
        cs = sb("cs", [SB, 2, HD])
        cp = sb("cp", [2, VE])
        inter = sb("inter", HD + SB)
        stats = sb("stats", [5, 6])
        mv = sb("mv", [5, 2])
        small = sb("small", [4, 5])
        nq8 = sb("nq8", SB)
        nq1 = sb("nq1", 1)
        assert place[0] <= nc.sbuf_usable_end, place[0]
        place[0] = pool_base
        ga = sb("ga", [KT, T])
        place[0] = head_base
        c_hi = sb("c_hi", [CT, T], F32R)
        c_lo = sb("c_lo", [CT, T], F32R)
        m_hi = sb("m_hi", [KT, T], F32R)
        m_lo = sb("m_lo", [KT, T], F32R)
        assert place[0] <= nc.sbuf_usable_end, place[0]
        place[0] = pool_base
        hid_hi = sb("hid_hi", [8, T], F32R)
        hid_lo = sb("hid_lo", [8, T], F32R)
        assert place[0] <= head_base + 2 * CT * T * 4

        ps = ctx.enter_context(nc.psum_tensor("ps", [P, 8, 512], F32))

        def slot(s):
            return ps[:, 2 * s:2 * s + 2, 0:HALF]

        def bank(k):
            return ps[:, 4 + k % 4, :]

        def halves(t, j):
            if isinstance(j, int):
                return t[:, j, :].rearrange("p (b n) -> p b n", b=2)
            return t[:, bass.ds(j, 1), :].rearrange("p o (b n) -> p (o b) n", b=2)

        def flat(t):
            return t[:, :].rearrange("p (b n) -> p b n", b=2)

        def row(t, j):
            if isinstance(j, int):
                return t[:, j, :]
            return t[:, bass.ds(j, 1), :].rearrange("p o n -> p (o n)")

        def vcol(c, parts=P):
            return vec[0:parts, c:c + 1] if isinstance(c, int) else vec[0:parts, bass.ds(c, 1)]

        x_loaded = [sem(f"x_loaded{k}") for k in range(KT)]
        vec_loaded = sem("vec_loaded")
        gw_loaded = sem("gw_loaded")
        gb_loaded = sem("gb_loaded")
        m0_loaded = sem("m0_loaded")
        cache_loaded = sem("cache_loaded")
        n_loaded = sem("n_loaded")
        cs_loaded = sem("cs_loaded")
        raw_loaded = [sem(f"raw_loaded{s}") for s in range(2)]
        consts_ready = sem("consts_ready")
        masks_ready = sem("masks_ready")
        head_bufs_set = sem("head_bufs_set")
        hi_ready = sem("hi_ready")
        lo_ready = sem("lo_ready")
        unit_done = sem("unit_done")
        slot_read = [sem(f"slot_read{s}") for s in range(4)]
        sq_ready = sem("sq_ready")
        sq_added = sem("sq_added")
        sum_done = sem("sum_done")
        xg_ready = sem("xg_ready")
        xghi_ready = sem("xg_hi_ready")
        xglo_even = sem("xg_lo_even_ready")
        xglo_odd = sem("xg_lo_odd_ready")
        hf_ready = sem("hf_ready")
        hhi_ready = sem("h_hi_ready")
        hlo_ready = sem("h_lo_ready")
        sig_ready = sem("sigmoid_ready")
        a_ready = sem("a_ready")
        gstat_hi = sem("gstat_hi_ready")
        gstat_lo = sem("gstat_lo_ready")
        gates_done = sem("gates_done")
        gt_ready = sem("gt_ready")
        fabs_ready = sem("fabs_ready")
        ln_ready = sem("ln_ready")
        mrow_ready = sem("mrow_ready")
        exps_in = sem("exp_rows_ready")
        exps_out = sem("exps_done")
        turned = sem("cols_turned")
        negm_spread = sem("negm_spread")
        mdiag_ready = sem("mdiag_ready")
        w_ready = sem("w_ready")
        qm_ready = sem("qm_ready")
        gb_used = sem("gb_used")
        attn_ready = sem("attn_ready")
        act_read = sem("bank_read_by_act")
        dve_read = sem("bank_read_by_dve")
        wv_ready = sem("wv_ready")
        hm_ready = sem("hm_ready")
        rs_ready = sem("rs_ready")
        hvar_ready = sem("hvar_ready")
        hdev_ready = sem("hdev_ready")
        cp_stored = sem("cp_stored")
        cp_free = sem("cp_free")
        cs_stored = sem("cs_stored")
        out_stored = sem("out_stored")
        csum_ready = sem("csum_ready")
        cstat_done = sem("cstat_done")
        cdev_ready = sem("cdev_ready")
        csq_ready = sem("csq_ready")
        csq_added = sem("csq_added")
        cnorm_ready = sem("cnorm_ready")
        csilu_ready = sem("csilu_ready")
        chi_ready = sem("chi_ready")
        clo_ready = sem("clo_ready")
        co_first = sem("co_first_done")
        m_ready = sem("merged_ready")
        mhi_ready = sem("merged_hi_ready")
        mlo_ready = sem("merged_lo_ready")
        silu_ready = sem("silu_ready")
        hid_ready = sem("hid_ready")
        hidhi_ready = sem("hid_hi_ready")
        hidlo_ready = sem("hid_lo_ready")
        y_ready = sem("y_ready")
        y_stored = sem("y_stored")
        acc_zero = sem("acc_zero")
        dve_step = sem("dve_step")
        act_step = sem("act_step")
        pool_step = sem("pool_step")

        block = ctx.enter_context(nc.Block())

        @block.sync
        def _(sp):
            for s in (slot_read[0], slot_read[1], act_read, dve_read, gb_used, hidlo_ready, cp_free):
                sp.sem_inc(s, START)
            sp.dma_start(vec[:, :], vecs).then_inc(vec_loaded, 16)
            for k in range(KT):
                sp.dma_start(x[:, k, :], xT[:, k, :]).then_inc(x_loaded[k], 16)
                if k == 0:
                    sp.dma_start(raw[:, 0, :], w_cgcv[0]).then_inc(raw_loaded[0], 16)
            sp.dma_start(raw[:, 1, :], w_cgcv[1]).then_inc(raw_loaded[1], 16)

            def loads(base, w, count, cols=KT * P, first=0):
                with sp.Fori(first, count // 2) as i:
                    for s in range(2):
                        sp.wait_ge(lo_ready, i * 2 + (base + s - 1))
                        sp.dma_start(raw[:, s, 0:cols], w[bass.ds(i * 2 + s, 1)].rearrange("o p n -> (o p) n"))\
                          .then_inc(raw_loaded[s], 16)

            loads(U_A, w_cgcv, N_A, first=1)
            loads(U_B, w_head, NH * PER_HEAD)
            loads(U_GA, w_ga, KT)
            loads(U_CO, w_co, N_CO)
            loads(U_O, w_o, KT)
            for g, w in enumerate((w_fo0, w_fo1, w_fo2)):
                loads(U_E[g], w_fi[2 * Q_E[g]:2 * (Q_E[g] + GROUPS[g])], 2 * GROUPS[g])
                loads(U_F[g], w, KT, GROUPS[g] * P)
            for k in range(KT):
                sp.wait_ge(y_ready, k + 1)
                sp.dma_start(y[:, k, :], x[:, k, :]).then_inc(y_stored, 16)
            sp.wait_ge(y_stored, 16 * KT)

        @block.gpsimd
        def _(pool):
            steps = Tally(pool, pool_step)
            pool.dma_start(gw[:, :, :], gate_w).then_inc(gw_loaded, 16)
            pool.dma_start(gb[:, :], gate_b).then_inc(gb_loaded, 16)
            pool.dma_start(m0[:, :], st_m).then_inc(m0_loaded, 16)
            pool.dma_start(a_s[:, :, :, 0:PAST], cache).then_inc(cache_loaded, 16)
            pool.dma_start(nst[:, :, :, :], st_n).then_inc(n_loaded, 16)
            pool.memset(mean_d[:, :], 1.0 / D).then_inc(consts_ready, 1)
            pool.memset(mean_c[:, :], 1.0 / DC).then_inc(consts_ready, 1)
            pool.memset(eps[:, :], EPS).then_inc(consts_ready, 1)

            steps.on(pool.memset(gstat[:, :, :].rearrange("p k c -> p (k c)").bitcast(F32), 0.0))
            for k in range(0, KT, 2):
                pool.wait_ge(xghi_ready, k + 1)
                pool.tensor_tensor(xg_lo[:, k, :], hf[:, 0, :], xg_hi[:, k, :].bitcast(F32), ALU.subtract)\
                    .then_inc(xglo_even, 1)
            steps.on(pool.memset(seg[:, :], 1.0))
            steps.on(pool.memset(rows[:, :], 1.0))
            steps.on(pool.memset(a_p[:, :, 0:PAST], 0.0))
            steps.on(pool.memset(ident[:, :], 0.0))
            steps.on(pool.memset(cmask[:, :], 0.0))
            steps.on(pool.memset(smask[:, :], 0.0))
            steps.on(pool.memset(onehot[:, :], 1.0))
            steps.on(pool.memset(sel[:, :, :], 1.0))
            steps.settle()
            steps.on(pool.memset(seg[:, 0:TP:P], 0.0))
            steps.on(pool.memset(seg[:, TP:T:SL], 0.0))
            steps.on(pool.affine_select(out=ident[:, :], in_=ident[:, :], compare_op=ALU.not_equal, fill=1.0,
                                        base=0, pattern=[[-1, P]], channel_multiplier=1))
            steps.on(pool.affine_select(out=cmask[:, :], in_=cmask[:, :], compare_op=ALU.is_ge, fill=-BIG,
                                        base=0, pattern=[[1, P]], channel_multiplier=-1))
            steps.on(pool.affine_select(out=smask[:, :], in_=smask[:, :], compare_op=ALU.is_ge, fill=-BIG,
                                        base=0, pattern=[[1, TS]], channel_multiplier=-1))
            steps.on(pool.affine_select(out=onehot[:, :], in_=onehot[:, :], compare_op=ALU.is_ge, fill=0.0,
                                        base=0, pattern=[[-SL, SB]], channel_multiplier=1))
            steps.on(pool.affine_select(out=sel[:, :, :], in_=sel[:, :, :], compare_op=ALU.is_equal, fill=0.0,
                                        base=0, pattern=[[-1, NH], [0, P]], channel_multiplier=1))
            steps.settle()
            sm = smask[:, :].rearrange("p (b j) -> p b j", b=SB)
            pool.affine_select(out=sm, in_=sm, compare_op=ALU.is_ge, fill=-BIG,
                               base=0, pattern=[[-SL, SB], [0, SL]], channel_multiplier=1).then_inc(masks_ready, 1)
            pool.affine_select(out=onehot[:, :], in_=onehot[:, :], compare_op=ALU.is_ge, fill=0.0,
                               base=SL - 1, pattern=[[SL, SB]], channel_multiplier=-1).then_inc(masks_ready, 1)
            for k in range(KT):
                pool.wait_ge(hhi_ready, k + 1)
                pool.tensor_tensor(h_lo[:, k, :], hf[:, k % 2, :], h_hi[:, k, :].bitcast(F32), ALU.subtract)\
                    .then_inc(hlo_ready, 1)
            pool.wait_ge(mrow_ready, 1)
            pool.dma_start(m_p, mrow[:, TP - 1:TP]).then_inc(out_stored, 16)
            pool.wait_ge(exps_in, 1)
            pool.dma_start(m_s, mend[:, :]).then_inc(out_stored, 16)
            pool.wait_ge(out_stored, 32)
            pool.wait_ge(slot_read[2], C2_HEADS)
            pool.wait_ge(slot_read[3], C3_HEADS)
            pool.wait_ge(unit_done, N_A)
            pool.memset(qm[:, :, :], 0.0).then_inc(head_bufs_set, 1)
            pool.memset(num[:, 4, :], 0.0).then_inc(head_bufs_set, 1)
            pool.memset(kvn[:, :, 2 * HD:2 * HD + 1], 1.0).then_inc(head_bufs_set, 1)
            pool.dma_start(cs[:, :, :, :], st_c[0]).then_inc(cs_loaded, 16)

            pool.wait_ge(a_ready, 2 * CT)
            pool.dma_start(conv_p, a_p[:, :, TP:TP + PAST]).then_inc(out_stored, 16)
            pool.wait_ge(cache_loaded, 16)
            pool.dma_start(conv_s, a_s[:, :, :, SL:SL + PAST]).then_inc(out_stored, 16)

            def states(h, last=False):
                pool.wait_ge(act_read, h * ACT_USES + (START + ACT_USES))
                pool.dma_start(cn_p[bass.ds(h, 1)].rearrange("o p k v -> (o p) k v"), cp[:, :, :])\
                    .then_inc(cp_stored, 16)
                pool.wait_ge(dve_read, h * DVE_USES + (START + 13))
                pool.dma_start(c_s[bass.ds(h, 1)].rearrange("o p b k v -> (o p) b k v"), cs[:, :, :, :])\
                    .then_inc(cs_stored, 16)
                pool.wait_ge(cs_stored, h * 16 + 16)
                pool.wait_ge(cp_stored, h * 16 + 16)
                pool.sem_inc(cp_free, 1)
                if not last:
                    pool.dma_start(cs[:, :, :, :], st_c[bass.ds(h + 1, 1)].rearrange("o p b k v -> (o p) b k v"))\
                        .then_inc(cs_loaded, 16)

            with pool.Fori(0, NH - 1) as h:
                states(h)
            states(NH - 1, last=True)
            pool.wait_ge(dve_read, START + NH * DVE_USES)
            pool.dma_start(n_s, nnew[:, :, :, :]).then_inc(out_stored, 16)
            for j in range(CT):
                pool.wait_ge(chi_ready, j + 1)
                pool.tensor_tensor(c_lo[:, j, :], conv[:, j, :], c_hi[:, j, :].bitcast(F32), ALU.subtract)\
                    .then_inc(clo_ready, 1)
            pool.wait_ge(cp_stored, 16 * NH)
            pool.wait_ge(out_stored, 16 * 5)
            with pool.Fori(0, KT) as j:
                pool.wait_ge(mhi_ready, j + 1)
                pool.tensor_tensor(row(m_lo, j), row(merged, j), row(m_hi, j).bitcast(F32), ALU.subtract)\
                    .then_inc(mlo_ready, 1)
            with pool.Fori(0, KT // 2) as i:
                for s in range(2):
                    pool.wait_ge(hhi_ready, i * 2 + (KT + s + 1))
                    pool.tensor_tensor(row(h_lo, i * 2 + s), hf[:, s, :], row(h_hi, i * 2 + s).bitcast(F32),
                                       ALU.subtract).then_inc(hlo_ready, 1)
            pool.wait_ge(rs_ready, 3)
            for g, n in enumerate(GROUPS):
                with pool.Fori(0, n // 2) as i:
                    for s in range(2):
                        pool.wait_ge(slot_read[2 * s + 1], i + (C_E[g][2 * s + 1] + 1))
                        pool.tensor_tensor(hf[:, s, :], hf[:, s, :], rs[:, :], ALU.mult).then_inc(hid_ready, 1)
                        pool.wait_ge(hidhi_ready, i * 2 + (Q_E[g] + s + 1))
                        pool.tensor_tensor(row(hid_lo, i * 2 + s), hf[:, s, :], row(hid_hi, i * 2 + s).bitcast(F32),
                                           ALU.subtract).then_inc(hidlo_ready, 1)

        @block.scalar
        def _(act):
            steps = Tally(act, act_step)

            def split_hi(pair, s, first=False):
                act.wait_ge(raw_loaded[s], pair * 16 + 16)
                if not first:
                    act.wait_ge(unit_done, pair * 2 + (s - 1))
                act.activation(w_hi[:, s, :], raw[:, s, :], ACT.Copy).then_inc(hi_ready, 1)

            for k in range(KT):
                act.wait_ge(x_loaded[k], 16)
                if k >= 2:
                    act.wait_ge(sq_added, k - 1)
                act.activation(tmp[:, k % 2, :], x[:, k, :], ACT.Square).then_inc(sq_ready, 1)
                act.wait_ge(xg_ready, k + 1)
                act.activation(xg_hi[:, k, :], hf[:, k % 2, :], ACT.Copy).then_inc(xghi_ready, 1)
                if k == 0:
                    split_hi(0, 0, True)
                    act.wait_ge(gw_loaded, 16)
                    act.wait_ge(pool_step, 1)
                    for g in range(2):
                        act.activation(gstat[:, :, 64 * g:64 * g + NH], gw[:, :, NH * g:NH * g + NH], ACT.Copy)\
                            .then_inc(gstat_hi, 1)
            split_hi(0, 1, True)

            def deviation(s, done_sem, n):
                act.wait_ge(done_sem, n)
                act.activation(flat(rs), slot(s), ACT.Sqrt, bias=eps[:, :]).then_inc(slot_read[s], 1)

            def norm_hi(k):
                act.wait_ge(hf_ready, k + 1)
                act.activation(h_hi[:, k, :], hf[:, k % 2, :], ACT.Copy).then_inc(hhi_ready, 1)

            def conv_gate(pair):
                act.wait_ge(slot_read[0], pair + START + 1)
                act.activation(tmp[:, pair % 2, :], tmp[:, pair % 2, :], ACT.Sigmoid, bias=vcol(2 * pair))\
                    .then_inc(sig_ready, 1)

            act.wait_ge(consts_ready, 3)
            deviation(3, sum_done, 1)
            act.wait_ge(gates_done, 1)
            for g in range(2):
                act.activation(gt[:, g, :].rearrange("p (b n) -> p b n", b=2),
                               ps[64 * g + 32:64 * g + 32 + NH, 4:6, 0:HALF], ACT.Copy).then_inc(gt_ready, 1)
            split_hi(1, 0)
            conv_gate(0)
            act.wait_ge(fabs_ready, 1)
            steps.on(act.activation(ft[:, :], ft[:, :], ACT.Exp, scale=-1.0))
            steps.settle()
            act.activation(ft[:, :], ft[:, :], ACT.Ln, bias=1.0).then_inc(ln_ready, 1)

            split_hi(1, 1)
            split_hi(2, 0)
            conv_gate(1)
            split_hi(2, 1)
            act.wait_ge(mrow_ready, 1)
            act.activation(rows[:, I_EM * P:I_EM * P + T], mrow[:, :], ACT.Exp, scale=-1.0).then_inc(exps_out, 1)
            split_hi(3, 0)
            act.wait_ge(exps_in, 1)
            act.activation(rows[:, I_WS * P:I_WS * P + T], rows[:, I_WS * P:I_WS * P + T], ACT.Exp)\
                .then_inc(exps_out, 1)
            act.activation(rows[:, I_WI * P:I_WI * P + TS], rows[:, I_WI * P:I_WI * P + TS], ACT.Exp)\
                .then_inc(exps_out, 1)
            act.activation(drow[:, :], t8[:, :], ACT.Exp).then_inc(exps_out, 1)
            conv_gate(2)
            for k in range(5):
                norm_hi(k)
            split_hi(3, 1)
            for k in range(5, KT):
                norm_hi(k)
            split_hi(4, 0)
            conv_gate(3)

            def keep_negm(h):
                act.wait_ge(negm_spread, h + 1)
                act.activation(halves(negm, h), slot(3 - h % 2), ACT.Copy).then_inc(slot_read[3 - h % 2], 1)

            keep_negm(0)
            split_hi(4, 1)
            for h in range(1, NH):
                keep_negm(h)

            def evac_bias(h, j, dst):
                act.wait_ge(unit_done, h * PER_HEAD + (U_B + j + 1))
                act.activation(dst, slot(j % 2), ACT.Identity, bias=vcol(h * PER_HEAD + (U_B + j)))\
                    .then_inc(slot_read[j % 2], 1)

            act.wait_ge(head_bufs_set, 3)
            act.wait_ge(slot_read[2], C2_HEADS)
            with act.Fori(0, NH) as h:
                def hi_of(j):
                    split_hi(h * (PER_HEAD // 2) + (U_B + j + 2) // 2, j % 2)

                def use(k):
                    act.wait_ge(attn_ready, h * USES + (k + 1))

                for j in range(2):
                    hi_of(j)
                    evac_bias(h, j, halves(qkv[:, 0, :, :], j))
                hi_of(2)
                act.wait_ge(mdiag_ready, h + 1)

                def gcol(item, parts=P):
                    return cols[0:parts, item, bass.ds(h, 1)]

                for s in range(NB):
                    act.activation(wts[:, W_OFF[s]:W_OFF[s] + P], mdiag[:, s, :], ACT.Exp, bias=gcol(I_G + s))\
                        .then_inc(w_ready, 1)
                    for t in range(s + 1, NB):
                        o = W_OFF[s] + (t - s) * P
                        act.activation(wts[:, o:o + P], negm[:, bass.ds(h, 1), t * P:t * P + P]
                                       .rearrange("p o n -> p (o n)"), ACT.Exp,
                                       bias=gcol(OFF[s, t])).then_inc(w_ready, 1)
                act.activation(wts[0:TS, W_OFF[NB]:W_COLS], msamp[0:TS, :], ACT.Exp, bias=gcol(I_G + NB, TS))\
                    .then_inc(w_ready, 1)
                hi_of(3)
                for j in range(4, 6):
                    hi_of(j)
                    evac_bias(h, j, halves(qkv[:, 2, :, :], j - 4))
                for i in range(5):
                    use(T_USE + i)
                    n = P if i < NB else TS
                    act.activation(kvn[0:n, i, 0:2 * HD], bank(T_USE + i)[0:n, :], ACT.Copy).then_inc(act_read, 1)
                use(I_USE)
                act.activation(inter[0:TS, :], bank(I_USE)[0:TS, 0:HD + SB], ACT.Copy).then_inc(act_read, 1)
                for j in range(6, 8):
                    hi_of(j)
                    act.wait_ge(unit_done, h * PER_HEAD + (U_B + j + 1))
                    act.activation(halves(merged, h * 2 + (j - 6)), slot(j % 2), ACT.Sigmoid,
                                   bias=vcol(h * PER_HEAD + (U_B + j))).then_inc(slot_read[j % 2], 1)
                for i in range(5):
                    use(PV_USE + i)
                    n = P if i < NB else TS
                    act.activation(num[0:n, i, :], bank(PV_USE + i)[0:n, 0:VE], ACT.Copy).then_inc(act_read, 1)
                act.wait_ge(cp_free, h + START)
                for k in range(2):
                    use(CP_USE + k)
                    act.activation(cp[:, k, :], bank(CP_USE + k)[:, 0:VE], ACT.Copy).then_inc(act_read, 1)
                act.wait_ge(hvar_ready, h + 1)
                act.activation(small[:, 2, :], small[:, 1, :], ACT.Sqrt, bias=eps[:, :]).then_inc(hdev_ready, 1)
                for j in range(8, 10):
                    hi_of(j)
                    act.wait_ge(unit_done, h * PER_HEAD + (U_B + j + 1))
                    act.wait_ge(gb_used, h * 2 + START)
                    act.activation(halves(tmp, j % 2), slot(j % 2), ACT.Sigmoid,
                                   bias=vcol(h * PER_HEAD + (U_B + j))).then_inc(slot_read[j % 2], 1)

            def ga_unit(i, s):
                split_hi(i + (U_GA + 2) // 2, s)
                act.wait_ge(unit_done, i * 2 + (U_GA + s + 1))
                act.activation(halves(ga, i * 2 + s), slot(s), ACT.Sigmoid, bias=vcol(i * 2 + (U_GA + s)))\
                    .then_inc(slot_read[s], 1)

            act.wait_ge(dve_read, START + NH * DVE_USES)
            act.wait_ge(out_stored, 16 * 4)
            ga_unit(0, 0)
            for j in range(CT):
                act.wait_ge(cdev_ready, j + 1)
                if j >= 2:
                    act.wait_ge(csq_added, j - 1)
                act.activation(tmp[:, j % 2, :], conv[:, j, :], ACT.Square).then_inc(csq_ready, 1)
            ga_unit(0, 1)
            ga_unit(1, 0)
            deviation(3, cstat_done, 2)
            ga_unit(1, 1)
            for j in range(CT):
                act.wait_ge(cnorm_ready, j + 1)
                act.activation(conv[:, j, :], conv[:, j, :], ACT.Silu, bias=vcol(V_BCN + j), scale=vcol(V_GCN + j))\
                    .then_inc(csilu_ready, 1)
                act.wait_ge(csilu_ready, j + 1)
                act.activation(c_hi[:, j, :], conv[:, j, :], ACT.Copy).then_inc(chi_ready, 1)

            with act.Fori(2, KT // 2) as i:
                for s in range(2):
                    ga_unit(i, s)

            act.wait_ge(out_stored, 16 * 5)
            act.wait_ge(cp_stored, 16 * NH)
            act.wait_ge(cs_stored, 16 * NH)
            with act.Fori(0, N_CO // 2) as i:
                for p in range(2):
                    for o in range(2):
                        j = i * 4 + (2 * p + o)
                        act.wait_ge(m_ready, j + 1)
                        act.activation(row(m_hi, j), row(merged, j), ACT.Copy).then_inc(mhi_ready, 1)
                        if o == 0:
                            split_hi(i + (U_CO + 2) // 2, p)

            def squares(i, base, contents, sq_base, last=False):
                for s in range(2):
                    if not last:
                        split_hi(i + (base + 2) // 2, s)
                    act.wait_ge(slot_read[s], i + (contents + 1))
                    act.wait_ge(sq_added, i * 2 + (sq_base + s - 1))
                    act.activation(tmp[:, s, :], row(x, i * 2 + s), ACT.Square).then_inc(sq_ready, 1)
                    if base == U_O:
                        act.wait_ge(hf_ready, i * 2 + (KT + s + 1))
                        act.activation(row(h_hi, i * 2 + s), hf[:, s, :], ACT.Copy).then_inc(hhi_ready, 1)

            with act.Fori(0, KT // 2) as i:
                squares(i, U_O, C_O, KT)
            deviation(2, sum_done, 2)
            for g, n in enumerate(GROUPS):
                with act.Fori(0, n // 2) as i:
                    for p in range(2):
                        split_hi(i * 2 + (U_E[g] // 2 + p + 1), 0)
                        act.wait_ge(slot_read[2 * p], i + (C_E[g][2 * p] + 1))
                        act.activation(tmp[:, p, :], tmp[:, p, :], ACT.Silu).then_inc(silu_ready, 1)
                        split_hi(i * 2 + (U_E[g] // 2 + p + 1), 1)
                        act.wait_ge(hid_ready, i * 2 + (Q_E[g] + p + 1))
                        act.activation(row(hid_hi, i * 2 + p), hf[:, p, :], ACT.Copy).then_inc(hidhi_ready, 1)
                if g < len(GROUPS) - 1:
                    with act.Fori(0, KT // 2) as i:
                        for s in range(2):
                            split_hi(i + (U_F[g] + 2) // 2, s)
            with act.Fori(0, KT // 2 - 1) as i:
                squares(i, U_F[-1], C_F[-1], 2 * KT)
            squares(KT // 2 - 1, U_F[-1], C_F[-1], 2 * KT, last=True)
            deviation(2, sum_done, 3)

        @block.tensor
        def _(pe):
            def unit(u, s, w, occupied, hi, lo, nkt, done=None, ready=None):
                pe.wait_ge(lo_ready, u + 1)
                pe.wait_ge(slot_read[s], occupied)
                for k in range(nkt):
                    if ready is not None:
                        ready(k)
                    for wt, parts in ((w_hi, (hi, lo)), (w_lo, (hi,))):
                        for src in parts:
                            for b in range(2):
                                last = pe.matmul(ps[:, 2 * s + b, 0:HALF], wt[:, w, k * P:k * P + P],
                                                 src[:, k, b * HALF:b * HALF + HALF],
                                                 start=(k == 0 and wt is w_hi and src is hi),
                                                 stop=(k == nkt - 1 and wt is w_lo))
                last.then_inc(unit_done, 1)

            def mean(s, weights, src, done):
                for b in range(2):
                    last = pe.matmul(ps[:, 2 * s + b, 0:HALF], weights[:, :], src[:, b * HALF:b * HALF + HALF],
                                     start=True, stop=True)
                last.then_inc(done, 1)

            pe.wait_ge(gstat_hi, 2)
            pe.wait_ge(gstat_lo, 2)

            def gate_tile(k):
                pe.wait_ge(xglo_odd if k % 2 else xglo_even, k // 2 + 1)
                for src in (xg_hi, xg_lo):
                    for b in range(2):
                        last = pe.matmul(ps[:, 4 + b, 0:HALF], gstat[:, k, :], src[:, k, b * HALF:b * HALF + HALF],
                                         start=(k == 0 and src is xg_hi), stop=(k == KT - 1 and src is xg_lo))
                if k == KT - 1:
                    last.then_inc(gates_done, 1)

            unit(0, 0, 0, START, xg_hi, xg_lo, KT, ready=gate_tile)
            pe.wait_ge(consts_ready, 2)
            pe.wait_ge(sq_added, KT)
            mean(3, mean_d, acc, sum_done)
            unit(1, 1, 1, START, xg_hi, xg_lo, KT)
            with pe.Fori(1, N_A // 2 - 1) as i:
                for s in range(2):
                    unit(i * 2 + s, s, s, i + START, xg_hi, xg_lo, KT)
            unit(N_A - 2, 0, 0, C_B - 1, xg_hi, xg_lo, KT)
            pe.wait_ge(slot_read[2], 1)
            pe.wait_ge(exps_out, 4)
            pe.wait_ge(masks_ready, 2)
            for n in range(NI):
                pe.transpose(ps[:, 4, n * NH:n * NH + NH], rows[:, n * P:n * P + P], ident[0:NH, 0:NH])
            for h in range(NH):
                last = pe.matmul(ps[:, 5, h * SB:h * SB + SB], sel[:, h, :], drow[:, :], start=True, stop=True)
            last.then_inc(turned, 1)
            for h in range(NH):
                s = 3 - h % 2
                pe.wait_ge(slot_read[s], (1 if s == 3 else 2) + h // 2)
                for b in range(2):
                    last = pe.matmul(ps[:, 2 * s + b, 0:HALF], sel[:, h, :], nrow[:, b * HALF:b * HALF + HALF],
                                     start=True, stop=True)
                last.then_inc(negm_spread, 1)
                if h == 0:
                    unit(N_A - 1, 1, 1, C_B - 1, xg_hi, xg_lo, KT)
            pe.wait_ge(slot_read[3], C3_HEADS)
            pe.wait_ge(slot_read[2], C2_HEADS)
            pe.wait_ge(hlo_ready, KT)

            with pe.Fori(0, NH) as h:
                def head_unit(j):
                    unit(h * PER_HEAD + (U_B + j), j % 2, j % 2, h * (PER_HEAD // 2) + (C_B + j // 2), h_hi, h_lo, KT)

                def use(k):
                    samples = (S_USE + 4, T_USE + 4, PV_USE + 4, HT_USE + 2)
                    if k + 1 in samples and k >= 3:
                        read(k - 3)
                    if k in samples:
                        return
                    if k == 0:
                        pe.wait_ge(act_read, h * ACT_USES + START)
                        pe.wait_ge(dve_read, h * DVE_USES + START)
                    elif k >= 4:
                        read(k - 4)

                def read(k):
                    if READER[k] == "act":
                        pe.wait_ge(act_read, h * ACT_USES + (READER[:k].count("act") + START + 1))
                    else:
                        pe.wait_ge(dve_read, h * DVE_USES + (READER[:k].count("dve") + START + 1))

                for j in range(6):
                    head_unit(j)
                for s in range(2):
                    pe.wait_ge(slot_read[s], h * (PER_HEAD // 2) + (C_B + 2))
                for s in range(5):
                    use(S_USE + s)
                    t0, n, rows_ = (s * P, TP - s * P, P) if s < NB else (TP, TS, TS)
                    for k in range(2):
                        last = pe.matmul(bank(S_USE + s)[0:rows_, 0:n], qkv[:, 1, k, t0:t0 + rows_],
                                         qkv[:, 0, k, t0:t0 + n], start=(k == 0), stop=(k == 1))
                    last.then_inc(attn_ready, 1)
                for s in range(2):
                    pe.wait_ge(slot_read[s], h * (PER_HEAD // 2) + (C_B + 3))
                for s in range(5):
                    use(T_USE + s)
                    n = P if s < NB else TS
                    for c in range(4):
                        last = pe.transpose(bank(T_USE + s)[0:n, c * P:c * P + P],
                                            qkv[:, 1 + c // 2, c % 2, s * P:s * P + n], ident[:, :])
                    last.then_inc(attn_ready, 1)
                use(I_USE)
                pe.wait_ge(qm_ready, h * 2 + 2)
                pe.wait_ge(cs_loaded, h * 16 + 16)
                for b in range(SB):
                    for k in range(2):
                        pe.matmul(bank(I_USE)[0:TS, 0:HD], qm[:, k, b * TS:b * TS + TS], cs[:, b, k, :],
                                  start=(b == 0 and k == 0), stop=(b == SB - 1 and k == 1))
                pe.wait_ge(n_loaded, 16)
                for k in range(2):
                    last = pe.matmul(bank(I_USE)[0:TS, HD:HD + SB], qkv[:, 0, k, TP:T],
                                     nst[:, bass.ds(h, 1), k, :].rearrange("p o b -> p (o b)"),
                                     start=(k == 0), stop=(k == 1))
                last.then_inc(attn_ready, 1)
                head_unit(6)
                head_unit(7)
                for t in range(5):
                    use(PV_USE + t)
                    if t == 0:
                        read(T_USE + 4)
                    if t < NB:
                        for s in range(t + 1):
                            o = W_OFF[s] + (t - s) * P
                            last = pe.matmul(bank(PV_USE + t)[:, 0:VE], wts[:, o:o + P], kvn[:, s, HD:2 * HD + 1],
                                             start=(s == 0), stop=(s == t))
                    else:
                        last = pe.matmul(bank(PV_USE + t)[0:TS, 0:VE], wts[0:TS, W_OFF[NB]:W_COLS],
                                         kvn[0:TS, NB, HD:2 * HD + 1], start=True, stop=True)
                    last.then_inc(attn_ready, 1)
                pe.wait_ge(wv_ready, h * (NB + SB) + (NB + SB))
                for k in range(2):
                    use(CP_USE + k)
                    for s in range(NB):
                        last = pe.matmul(bank(CP_USE + k)[:, 0:VE], kvn[:, s, k * P:k * P + P], wvn[:, s, :],
                                         start=(s == 0), stop=(s == NB - 1))
                    last.then_inc(attn_ready, 1)
                for b in range(SB):
                    use(CS_USE + b)
                    for k in range(2):
                        last = pe.matmul(bank(CS_USE + b)[:, k * HD:k * HD + HD], kvn[0:TS, NB, k * P:k * P + P],
                                         wvs[0:TS, b, :], start=True, stop=True)
                    last.then_inc(attn_ready, 1)
                use(N_USE)
                for k in range(2):
                    last = pe.matmul(bank(N_USE)[:, k * SB:k * SB + SB], kvn[0:TS, NB, k * P:k * P + P],
                                     wb[0:TS, bass.ds(h, 1), :].rearrange("p o b -> p (o b)"), start=True, stop=True)
                last.then_inc(attn_ready, 1)
                head_unit(8)
                head_unit(9)
                pe.wait_ge(hm_ready, h * 5 + 5)
                for v in range(2):
                    use(HT_USE + v)
                    for s in range(NB):
                        last = pe.transpose(bank(HT_USE + v)[:, s * P:s * P + P], num[:, s, v * P:v * P + P],
                                            ident[:, :])
                    last.then_inc(attn_ready, 1)
                use(HT_USE + 2)
                for v in range(2):
                    last = pe.transpose(bank(HT_USE + 2)[:, v * TS:v * TS + TS], num[0:TS, NB, v * P:v * P + P],
                                        ident[0:TS, 0:TS])
                last.then_inc(attn_ready, 1)

            def ga_unit(i, s):
                unit(i * 2 + (U_GA + s), s, s, i + C_GA, h_hi, h_lo, KT)

            ga_unit(0, 0)
            pe.wait_ge(act_read, START + NH * ACT_USES)
            pe.wait_ge(dve_read, START + NH * DVE_USES)
            pe.wait_ge(csum_ready, 1)
            mean(2, mean_c, acc, cstat_done)
            ga_unit(0, 1)
            ga_unit(1, 0)
            pe.wait_ge(csq_added, CT)
            mean(3, mean_c, acc, cstat_done)
            ga_unit(1, 1)
            with pe.Fori(2, KT // 2) as i:
                for s in range(2):
                    ga_unit(i, s)

            def two_units(base, count_before, hi, lo, nkt, ready_sem, ready_base):
                with pe.Fori(0, KT // 2) as i:
                    for s in range(2):
                        unit(i * 2 + (base + s), s, s, i + count_before, hi, lo, nkt,
                             ready=(lambda k: pe.wait_ge(ready_sem, ready_base + k + 1)) if s == 0 else None)

            pe.wait_ge(clo_ready, CT)
            with pe.Fori(0, N_CO // 2) as i:
                for p in range(2):
                    pe.wait_ge(lo_ready, i * 2 + (U_CO + p + 1))
                    for o in range(2):
                        s = 2 * p + o
                        pe.wait_ge(slot_read[s], i + (C_CO, C_CO, C2_CO, C3_CO)[s])
                        for k in range(CT):
                            at = (o * CT + k) * P
                            for wt, parts in ((w_hi, (c_hi, c_lo)), (w_lo, (c_hi,))):
                                for src in parts:
                                    for b in range(2):
                                        last = pe.matmul(ps[:, 2 * s + b, 0:HALF], wt[:, p, at:at + P],
                                                         src[:, k, b * HALF:b * HALF + HALF],
                                                         start=(k == 0 and wt is w_hi and src is c_hi),
                                                         stop=(k == CT - 1 and wt is w_lo))
                        last.then_inc(unit_done if o else co_first, 1)
            two_units(U_O, C_O, m_hi, m_lo, KT, mlo_ready, 0)
            pe.wait_ge(sq_added, 2 * KT)
            pe.wait_ge(slot_read[2], C2_NORM)
            mean(2, mean_d, acc, sum_done)
            for g, n in enumerate(GROUPS):
                with pe.Fori(0, n // 2) as i:
                    for j in range(4):
                        unit(i * 4 + (U_E[g] + j), j, j % 2, i + C_E[g][j], h_hi, h_lo, KT,
                             ready=(lambda k: pe.wait_ge(hlo_ready, KT + k + 1)) if j == 0 else None)
                two_units(U_F[g], C_F[g], hid_hi, hid_lo, n, hidlo_ready, START + Q_E[g])
            pe.wait_ge(sq_added, 3 * KT)
            pe.wait_ge(slot_read[2], C2_END)
            mean(2, mean_d, acc, sum_done)

        @block.vector
        def _(dve):
            steps = Tally(dve, dve_step)

            def split_lo(u, s):
                dve.wait_ge(hi_ready, u + 1)
                dve.tensor_tensor(w_lo[:, s, :], raw[:, s, :], w_hi[:, s, :].bitcast(F32), ALU.subtract)\
                    .then_inc(lo_ready, 1)

            def add_square(k, n):
                dve.wait_ge(sq_ready, n)
                if k == 0:
                    dve.tensor_copy(acc[:, :], tmp[:, 0, :]).then_inc(sq_added, 1)
                else:
                    dve.wait_ge(sq_added, n - 1)
                    dve.tensor_tensor(acc[:, :], acc[:, :], tmp[:, k % 2, :], ALU.add).then_inc(sq_added, 1)

            def rstd(s, contents, n):
                dve.wait_ge(slot_read[s], contents)
                dve.reciprocal(rs[:, :], rs[:, :]).then_inc(rs_ready, 1)

            def xg_lo_odd(k):
                dve.wait_ge(xghi_ready, k + 1)
                dve.tensor_tensor(xg_lo[:, k, :], hf[:, 1, :], xg_hi[:, k, :].bitcast(F32), ALU.subtract)\
                    .then_inc(xglo_odd, 1)

            dve.wait_ge(vec_loaded, 16)
            for k in range(KT):
                dve.wait_ge(x_loaded[k], 16)
                if k >= 2 and k % 2 == 0:
                    dve.wait_ge(xglo_even, k // 2)
                if k >= 3 and k % 2:
                    dve.wait_ge(xglo_odd, k // 2)
                dve.tensor_scalar(hf[:, k % 2, :], x[:, k, :], vcol(V_GMIX + k), None, ALU.mult).then_inc(xg_ready, 1)
                if k == 0:
                    split_lo(0, 0)
                    for g in range(2):
                        dve.wait_ge(gstat_hi, g + 1)
                        dve.tensor_tensor(gstat[:, :, 64 * g + 32:64 * g + 32 + NH], gw[:, :, NH * g:NH * g + NH],
                                          gstat[:, :, 64 * g:64 * g + NH].bitcast(F32), ALU.subtract)\
                            .then_inc(gstat_lo, 1)
                add_square(k, k + 1)
                if k % 2:
                    xg_lo_odd(k)
            split_lo(1, 1)
            cvt = conv

            def scaled(u):
                dve.wait_ge(unit_done, u + 1)
                dve.tensor_tensor(halves(cvt if u % 2 else tmp, u // 2 % 2), slot(u % 2), flat(rs), ALU.mult)\
                    .then_inc(slot_read[u % 2], 1)

            def conv_input(pair):
                dve.wait_ge(slot_read[1], pair + START + 1)
                dve.wait_ge(sig_ready, pair + 1)
                v, sg, bias = cvt[:, pair % 2, :], tmp[:, pair % 2, :], vcol(2 * pair + 1)
                dve.scalar_tensor_tensor(a_p[:, pair, PAST:PAST + TP], v[:, 0:TP], bias, sg[:, 0:TP],
                                         ALU.add, ALU.mult).then_inc(a_ready, 1)
                dve.scalar_tensor_tensor(a_s[:, pair, :, PAST:PAST + SL], v[:, TP:T].rearrange("p (b n) -> p b n", b=SB),
                                         bias, sg[:, TP:T].rearrange("p (b n) -> p b n", b=SB),
                                         ALU.add, ALU.mult).then_inc(a_ready, 1)

            def normalised(k):
                if k >= 2:
                    dve.wait_ge(hlo_ready, k - 1)
                dve.scalar_tensor_tensor(hf[:, k % 2, :], x[:, k, :], vcol(V_GMIX + k), rs[:, :], ALU.mult, ALU.mult)\
                    .then_inc(hf_ready, 1)

            rstd(3, 1, 1)
            dve.wait_ge(rs_ready, 1)
            dve.wait_ge(gates_done, 1)
            dve.wait_ge(gb_loaded, 16)
            dve.wait_ge(gt_ready, 2)
            for g, dst in ((1, fz), (0, li)):
                ins = dve.tensor_tensor(flat(dst), ps[64 * g:64 * g + NH, 4:6, 0:HALF],
                                        gt[:, g, :].rearrange("p (b n) -> p b n", b=2), ALU.add)
                if g:
                    steps.on(ins)
                else:
                    ins.then_inc(slot_read[2], 1)
            steps.settle()
            steps.on(dve.tensor_tensor(fz[:, :], fz[:, :], rs[0:NH, :], ALU.mult))
            steps.settle()
            steps.on(dve.tensor_scalar(fz[:, :], fz[:, :], gb[:, 1:2], None, ALU.add))
            steps.settle()
            dve.scalar_tensor_tensor(ft[:, :], fz[:, :], -1.0, fz[:, :], ALU.mult, ALU.max).then_inc(fabs_ready, 1)
            scaled(0)
            split_lo(2, 0)
            dve.wait_ge(slot_read[2], 1)
            steps.on(dve.tensor_tensor(li[:, :], li[:, :], rs[0:NH, :], ALU.mult))
            steps.settle()
            steps.on(dve.tensor_scalar(li[:, :], li[:, :], gb[:, 0:1], None, ALU.add))
            steps.settle()
            scaled(1)
            split_lo(3, 1)
            dve.wait_ge(pool_step, POOL_SET)
            dve.wait_ge(cache_loaded, 16)
            conv_input(0)

            dve.wait_ge(ln_ready, 1)
            steps.on(dve.scalar_tensor_tensor(lf[:, :], fz[:, :], 0.0, ft[:, :], ALU.min, ALU.subtract))
            steps.on(dve.tensor_copy(lim[:, :], li[:, :]))
            steps.settle()
            dve.wait_ge(m0_loaded, 16)
            first = slice(TP, T, SL)
            steps.on(dve.tensor_tensor(t8[:, :], lf[:, first], m0[:, :], ALU.add))
            steps.on(dve.tensor_copy(lfm[:, :], lf[:, :]))
            steps.on(dve.tensor_tensor_scan(ft[:, :], seg[:, :], lf[:, :], 0.0, ALU.mult, ALU.add))
            steps.settle()
            steps.on(dve.tensor_tensor(lim[:, first], t8[:, :], li[:, first], ALU.max))
            steps.on(dve.memset(lfm[:, first], -BIG))
            steps.settle()
            steps.on(dve.tensor_tensor(rows[:, 0:T], li[:, :], ft[:, :], ALU.subtract))
            dve.tensor_tensor_scan(mrow[:, :], lfm[:, :], lim[:, :], 0.0, ALU.add, ALU.max).then_inc(mrow_ready, 1)
            dve.wait_ge(mrow_ready, 1)
            end = slice(TP + SL - 1, T, SL)
            steps.on(dve.tensor_tensor(nrow[:, :], ft[:, :], mrow[:, :], ALU.subtract))
            steps.on(dve.tensor_tensor(t8[:, :], ft[:, end], mrow[:, end], ALU.subtract))
            steps.on(dve.tensor_copy(mend[:, :], mrow[:, end]))

            scaled(2)
            split_lo(4, 0)

            def total(t):
                return ft[:, t * P + P - 1:t * P + P]

            def item(n):
                return rows[:, n * P:n * P + P]

            for t in range(NB):
                steps.settle()
                for s in range(t + 1):
                    src = item(I_G + s) if s == t else item(OFF[s, t])
                    if t < NB - 1:
                        steps.on(dve.tensor_scalar(item(OFF[s, t + 1]), src, total(t), None, ALU.add))
                    else:
                        steps.on(dve.tensor_scalar(item(I_WS + s), src, total(t), mrow[:, TP - 1:TP],
                                                   ALU.add, ALU.subtract))

            def per_sample(t):
                return t.rearrange("p (b j) -> p b j", b=SB)

            def spread(t):
                return t.unsqueeze(2).broadcast_to([NH, SB, SL])

            steps.on(dve.tensor_tensor(per_sample(rows[:, I_WS * P + TP:I_WS * P + T]), per_sample(rows[:, TP:T]),
                                       spread(t8[:, :]), ALU.add))
            steps.on(dve.tensor_tensor(per_sample(rows[:, I_WI * P:I_WI * P + TS]), per_sample(nrow[:, TP:T]),
                                       spread(m0[:, :]), ALU.add))
            steps.settle()
            dve.tensor_tensor(t8[:, :], t8[:, :], m0[:, :], ALU.add).then_inc(exps_in, 1)
            scaled(3)
            split_lo(5, 1)
            conv_input(1)
            scaled(4)
            split_lo(6, 0)
            for k in range(5):
                normalised(k)
            scaled(5)
            split_lo(7, 1)
            conv_input(2)
            for k in range(5, KT):
                normalised(k)
            scaled(6)
            split_lo(8, 0)
            dve.wait_ge(turned, 1)
            steps.on(dve.tensor_copy(dec[:, :, :].rearrange("p h b -> p (h b)"), ps[:, 5, 0:NH * SB]))
            dve.tensor_copy(cols[:, :, :].rearrange("p i h -> p (i h)"), ps[:, 4, 0:NI * NH]).then_inc(slot_read[2], 1)
            dve.wait_ge(slot_read[2], 2)
            dve.wait_ge(masks_ready, 2)
            dve.wait_ge(n_loaded, 16)
            steps.on(dve.tensor_tensor(wb[0:TS, :, :], cols[0:TS, I_WS + NB, :].unsqueeze(2).broadcast_to([TS, NH, SB]),
                                       onehot[0:TS, :].unsqueeze(1).broadcast_to([TS, NH, SB]), ALU.mult))
            for k in range(2):
                steps.on(dve.tensor_tensor(nnew[:, :, k, :], nst[:, :, k, :], dec[:, :, :], ALU.mult))
            steps.settle()
            scaled(7)
            split_lo(9, 1)
            conv_input(3)
            dve.wait_ge(slot_read[2], C2_HEADS)
            dve.wait_ge(slot_read[3], C3_HEADS)
            dve.wait_ge(head_bufs_set, 3)
            dve.wait_ge(a_ready, 2 * CT)

            with dve.Fori(0, NH) as h:
                steps.loop(h, DVE_HEAD_STEPS)
                tap = [0]

                def lo_of(j):
                    split_lo(h * PER_HEAD + (U_B + j + 2), j % 2)
                    taps(j)

                def taps(j):
                    for _ in range(CONV_TAPS[j]):
                        conv_tap(tap[0])
                        tap[0] += 1

                def conv_tap(w):
                    out = row(conv, h)
                    wcol = vcol(h * CW + (V_WDW + w))
                    outs = (out[:, 0:TP], out[:, TP:T].rearrange("p (b j) -> p b j", b=SB))
                    ins = (row(a_p, h)[:, w:w + TP],
                           a_s[:, bass.ds(h, 1), :, w:w + SL].rearrange("p o b n -> p (o b) n"))
                    for o, a in zip(outs, ins):
                        if w == 0:
                            steps.on(dve.tensor_scalar(o, a, wcol, vcol(h + V_BDW), ALU.mult, ALU.add))
                        else:
                            steps.settle(back=1)
                            steps.on(dve.scalar_tensor_tensor(o, a, wcol, o, ALU.mult, ALU.add))

                def use(k):
                    dve.wait_ge(attn_ready, h * USES + (k + 1))

                def evacuated(s, n):
                    dve.wait_ge(slot_read[s], h * (PER_HEAD // 2) + (C_B + n))

                def hcol(item, parts=P):
                    return cols[0:parts, item, bass.ds(h, 1)]

                nh = row(negm, h)
                steps.on(dve.tensor_tensor(mdiag[:, :, :], nh[:, 0:TP].rearrange("p (s t) -> p s t", s=NB),
                                           cmask[:, :].unsqueeze(1).broadcast_to([P, NB, P]), ALU.add))
                dve.tensor_tensor(msamp[0:TS, :], nh[0:TS, TP:T], smask[0:TS, :], ALU.add).then_inc(mdiag_ready, 1)
                lo_of(0)
                lo_of(1)
                for j in (2, 3):
                    lo_of(j)
                    dve.wait_ge(unit_done, h * PER_HEAD + (U_B + j + 1))
                    dve.tensor_scalar(halves(qkv[:, 1, :, :], j - 2), slot(j % 2), vcol(h * PER_HEAD + (U_B + j)),
                                      HD ** -0.5, ALU.add, ALU.mult).then_inc(slot_read[j % 2], 1)
                for k in range(2):
                    evacuated(k, 1)
                    dve.tensor_copy(qm[:, k, :].rearrange("p (b t) -> p b t", b=SB)[:, :, 0:SL],
                                    qkv[:, 0, k, TP:T].rearrange("p (b j) -> p b j", b=SB)).then_inc(qm_ready, 1)
                lo_of(4)
                split_lo(h * PER_HEAD + (U_B + 7), 1)
                for s in range(5):
                    use(S_USE + s)
                    dve.wait_ge(w_ready, h * 11 + (4, 7, 9, 10, 11)[s])
                    parts, o, n = (P, W_OFF[s], TP - s * P) if s < NB else (TS, W_OFF[s], TS)
                    dve.tensor_tensor(wts[0:parts, o:o + n], bank(S_USE + s)[0:parts, 0:n], wts[0:parts, o:o + n],
                                      ALU.mult).then_inc(dve_read, 1)
                taps(5)
                use(I_USE)
                for s in range(NB):
                    dve.wait_ge(act_read, h * ACT_USES + (START + s + 1))
                    dve.tensor_scalar(wvn[:, s, :], kvn[:, s, HD:2 * HD + 1], hcol(I_WS + s), None, ALU.mult)\
                        .then_inc(wv_ready, 1)
                dve.wait_ge(act_read, h * ACT_USES + (START + 5))
                for b in range(SB):
                    dve.tensor_scalar(wvs[0:TS, b, :], kvn[0:TS, NB, HD:2 * HD],
                                      wb[0:TS, bass.ds(h, 1), b:b + 1].rearrange("p o b -> p (o b)"), None, ALU.mult)\
                        .then_inc(wv_ready, 1)
                lo_of(6)
                lo_of(7)
                for b in range(SB):
                    use(CS_USE + b)
                    c = cs[:, b, :, :].rearrange("p k v -> p (k v)")
                    dve.scalar_tensor_tensor(c, c, dec[:, bass.ds(h, 1), b:b + 1].rearrange("p o b -> p (o b)"),
                                             bank(CS_USE + b), ALU.mult, ALU.add).then_inc(dve_read, 1)
                use(N_USE)
                nn = nnew[:, bass.ds(h, 1), :, :].rearrange("p o k b -> p (o k b)")
                dve.tensor_tensor(nn, nn, bank(N_USE)[:, 0:2 * SB], ALU.add).then_inc(dve_read, 1)
                dve.wait_ge(act_read, h * ACT_USES + (START + 11))
                wi = hcol(I_WI, TS)
                steps.on(dve.tensor_tensor(nq8[0:TS, :], inter[0:TS, HD:HD + SB], onehot[0:TS, :], ALU.mult))
                steps.on(dve.scalar_tensor_tensor(num[0:TS, NB, 0:HD], inter[0:TS, 0:HD], wi, num[0:TS, NB, 0:HD],
                                                  ALU.mult, ALU.add))
                steps.settle(back=1)
                steps.on(dve.reduce_sum(nq1[0:TS, :], nq8[0:TS, :], axis=mybir.AxisListType.X))
                steps.settle()
                steps.on(dve.scalar_tensor_tensor(num[0:TS, NB, HD:VE], nq1[0:TS, :], wi, num[0:TS, NB, HD:VE],
                                                  ALU.mult, ALU.add))
                for i in range(5):
                    steps.on(dve.bn_stats(stats[:, i, :], num[:, i, 0:HD]))
                em = cols[:, I_EM:I_EM + 5, bass.ds(h, 1)].rearrange("p i o -> p (i o)")
                steps.settle()
                steps.on(dve.scalar_tensor_tensor(small[:, 0, :], num[:, :, HD], -1.0, num[:, :, HD],
                                                  ALU.mult, ALU.max))
                for i in range(5):
                    steps.on(dve.bn_aggr(mv[:, i, :], stats[:, i, :]))
                steps.settle()
                steps.on(dve.tensor_tensor(small[:, 0, :], small[:, 0, :], em, ALU.max))
                steps.settle()
                steps.on(dve.reciprocal(small[:, 0, :], small[:, 0, :]))
                steps.settle()
                steps.on(dve.tensor_tensor(small[:, 1, :], mv[:, :, 1], small[:, 0, :], ALU.mult))
                steps.settle()
                dve.tensor_tensor(small[:, 1, :], small[:, 1, :], small[:, 0, :], ALU.mult).then_inc(hvar_ready, 1)
                dve.wait_ge(hdev_ready, h + 1)
                steps.on(dve.reciprocal(small[:, 2, :], small[:, 2, :]))
                steps.settle()
                steps.on(dve.tensor_tensor(small[:, 3, :], small[:, 2, :], small[:, 0, :], ALU.mult))
                steps.settle()
                for i in range(5):
                    dve.tensor_scalar(num[:, i, 0:HD], num[:, i, 0:HD], mv[:, i, 0:1], small[:, 3, i:i + 1],
                                      ALU.subtract, ALU.mult).then_inc(hm_ready, 1)
                for j in (8, 9):
                    lo_of(j)
                    evacuated(j % 2, 5)
                    m = row(merged, h * 2 + (j - 8))
                    dve.tensor_tensor(m, m, tmp[:, j % 2, :], ALU.mult).then_inc(gb_used, 1)
                assert tap[0] == CW
                dve.wait_ge(gb_used, h * 2 + (START + 2))
                for v in range(2):
                    use(HT_USE + v)
                    m = row(merged, h * 2 + v)[:, 0:TP]
                    dve.scalar_tensor_tensor(m, bank(HT_USE + v), vcol(h * 2 + (V_GMN + v)), m, ALU.mult, ALU.mult)\
                        .then_inc(dve_read, 1)
                use(HT_USE + 2)
                for v in range(2):
                    m = row(merged, h * 2 + v)[:, TP:T]
                    ins = dve.scalar_tensor_tensor(m, bank(HT_USE + 2)[:, v * TS:v * TS + TS],
                                                   vcol(h * 2 + (V_GMN + v)), m, ALU.mult, ALU.mult)
                    if v:
                        ins.then_inc(dve_read, 1)
                    else:
                        steps.on(ins)
                steps.end(NH)

            steps.on(dve.tensor_tensor(hf[:, 0, :], conv[:, 0, :], conv[:, 1, :], ALU.add))
            steps.on(dve.tensor_tensor(hf[:, 1, :], conv[:, 2, :], conv[:, 3, :], ALU.add))
            steps.settle()
            dve.tensor_tensor(acc[:, :], hf[:, 0, :], hf[:, 1, :], ALU.add).then_inc(csum_ready, 1)
            split_lo(U_GA + 2, 0)
            dve.wait_ge(cstat_done, 1)
            for j in range(CT):
                ins = dve.tensor_tensor(halves(conv, j), halves(conv, j), slot(2), ALU.subtract)
                ins.then_inc(cdev_ready, 1)
            dve.wait_ge(cdev_ready, CT)
            dve.sem_inc(slot_read[2], 1)
            dve.wait_ge(csq_ready, 1)
            dve.tensor_copy(acc[:, :], tmp[:, 0, :]).then_inc(csq_added, 1)
            for j in range(1, CT):
                dve.wait_ge(csq_ready, j + 1)
                dve.wait_ge(csq_added, j)
                dve.tensor_tensor(acc[:, :], acc[:, :], tmp[:, j % 2, :], ALU.add).then_inc(csq_added, 1)
            split_lo(U_GA + 3, 1)
            split_lo(U_GA + 4, 0)
            rstd(3, C3_CO, 2)
            dve.wait_ge(rs_ready, 2)
            for j in range(CT):
                dve.tensor_tensor(conv[:, j, :], conv[:, j, :], rs[:, :], ALU.mult).then_inc(cnorm_ready, 1)
            split_lo(U_GA + 5, 1)
            with dve.Fori(2, KT // 2) as i:
                for s in range(2):
                    split_lo(i * 2 + (U_GA + s + 2), s)
            dve.wait_ge(dve_read, START + NH * DVE_USES)
            dve.wait_ge(slot_read[0], C_CO)
            dve.wait_ge(slot_read[1], C_CO)
            with dve.Fori(0, N_CO // 2) as i:
                for p in range(2):
                    for o in range(2):
                        s, j = 2 * p + o, i * 4 + (2 * p + o)
                        if o:
                            split_lo(i * 2 + (U_CO + p + 2), p)
                        dve.wait_ge(unit_done if o else co_first, i * 2 + ((U_CO if o else 0) + p + 1))
                        g = halves(ga, j)
                        dve.tensor_tensor(g, slot(s), g, ALU.mult).then_inc(slot_read[s], 1)
                        dve.wait_ge(slot_read[s], i + ((C_CO, C_CO, C2_CO, C3_CO)[s] + 1))
                        m = row(merged, j)
                        dve.tensor_tensor(m, m, row(ga, j), ALU.add).then_inc(m_ready, 1)

            def add_units(i, base, contents, sq_base=None, last=False):
                for s in range(2):
                    if not last:
                        split_lo(i * 2 + (base + s + 2), s)
                    dve.wait_ge(unit_done, i * 2 + (base + s + 1))
                    xs = halves(x, i * 2 + s)
                    dve.tensor_tensor(xs, slot(s), xs, ALU.add).then_inc(slot_read[s], 1)
                    if base == U_O:
                        dve.wait_ge(hlo_ready, i * 2 + (KT + s - 1))
                        dve.wait_ge(slot_read[s], i + (contents + 1))
                        dve.tensor_scalar(hf[:, s, :], row(x, i * 2 + s), vcol(i * 2 + (V_GFFN + s)), None, ALU.mult)\
                            .then_inc(hf_ready, 1)
                    if sq_base is not None:
                        dve.wait_ge(sq_ready, i * 2 + (sq_base + s + 1))
                        dve.wait_ge(sq_added, i * 2 + (sq_base + s))
                        dve.tensor_tensor(acc[:, :], acc[:, :], tmp[:, s, :], ALU.add).then_inc(sq_added, 1)

            dve.wait_ge(cstat_done, 2)
            dve.memset(acc[:, :], 0.0).then_inc(acc_zero, 1)
            dve.wait_ge(acc_zero, 1)
            with dve.Fori(0, KT // 2) as i:
                add_units(i, U_O, C_O, KT)
            rstd(2, C2_NORM + 1, 3)
            dve.memset(acc[:, :], 0.0).then_inc(acc_zero, 1)
            dve.wait_ge(acc_zero, 2)
            dve.wait_ge(rs_ready, 3)
            dve.wait_ge(hlo_ready, 2 * KT)
            for g, n in enumerate(GROUPS):
                with dve.Fori(0, n // 2) as i:
                    for p in range(2):
                        dve.wait_ge(unit_done, i * 4 + (U_E[g] + 2 * p + 1))
                        dve.tensor_tensor(halves(tmp, p), slot(2 * p), flat(rs), ALU.mult).then_inc(slot_read[2 * p], 1)
                        split_lo(i * 4 + (U_E[g] + 2 * p + 2), 0)
                        dve.wait_ge(silu_ready, i * 2 + (Q_E[g] + p + 1))
                        dve.wait_ge(hidlo_ready, i * 2 + (START + Q_E[g]))
                        dve.wait_ge(unit_done, i * 4 + (U_E[g] + 2 * p + 2))
                        dve.tensor_tensor(halves(hf, p), slot(2 * p + 1), halves(tmp, p), ALU.mult)\
                            .then_inc(slot_read[2 * p + 1], 1)
                        split_lo(i * 4 + (U_E[g] + 2 * p + 3), 1)
                if g < len(GROUPS) - 1:
                    with dve.Fori(0, KT // 2) as i:
                        add_units(i, U_F[g], C_F[g])
            with dve.Fori(0, KT // 2 - 1) as i:
                add_units(i, U_F[-1], C_F[-1], 2 * KT)
            add_units(KT // 2 - 1, U_F[-1], C_F[-1], 2 * KT, last=True)
            rstd(2, C2_END + 1, 4)
            dve.wait_ge(rs_ready, 4)
            for k in range(KT):
                dve.scalar_tensor_tensor(x[:, k, :], x[:, k, :], vcol(V_GFIN + k), rs[:, :], ALU.mult, ALU.mult)\
                    .then_inc(y_ready, 1)


def kernel(**inputs):
    import concourse.bacc as bacc
    from concourse.bass_utils import run_bass_kernel_spmd

    a = {k: np.asarray(v) for k, v in inputs.items()}

    def blocks(w):
        k, n = w.shape[0] // P, w.shape[1] // P
        return w.reshape(k, P, n, P).transpose(2, 1, 0, 3).reshape(n, P, k * P)

    def per_tile(v):
        return v.reshape(-1, P).T

    w_in, b_in = a["w_in"][0], a["b_in"][0]
    sizes = [DC, DC] + [NH * HD] * 4 + [NH, NH, D, D]
    at = np.cumsum([0] + sizes)
    cut = [slice(int(at[i]), int(at[i + 1])) for i in range(len(sizes))]
    wb = {n: blocks(w_in[:, cut[i]]) for n, i in zip("cv cg q k v og ga gb".split(), (0, 1, 2, 3, 4, 5, 8, 9))}
    bb = {n: b_in[cut[i]].reshape(-1, P) for n, i in zip("cv cg q k v og ga gb".split(), (0, 1, 2, 3, 4, 5, 8, 9))}

    def heads(d):
        return np.concatenate([d[n][2 * h:2 * h + 2] for h in range(NH) for n in ("q", "k", "v", "og", "gb")])

    def pairs(p, q):
        return np.stack([p, q], 1).reshape((-1,) + p.shape[1:])

    vecs = np.concatenate(
        [pairs(bb["cg"], bb["cv"]).T, heads(bb).T, bb["ga"].T]
        + [per_tile(a[n].reshape(-1)) for n in ("g_mix_norm", "g_ffn_norm", "g_final", "g_mlstm_norm",
                                                "g_conv_norm", "b_conv_norm", "b_dwconv")]
        + [a["w_dwconv"][0].reshape(CW, CT, P).transpose(2, 1, 0).reshape(P, CT * CW)], axis=1)
    wfi = blocks(a["w_ffn_in"][0])
    wfo = a["w_ffn_out"][0]
    rows_of = np.cumsum([0] + [P * g for g in GROUPS])
    x_all = np.concatenate([a["x_prompt"].reshape(TP, D), a["x_sample"].reshape(TS, D)])
    ins = {
        "xT": x_all.reshape(T, KT, P).transpose(2, 1, 0),
        "vecs": vecs,
        "gate_w": w_in[:, cut[6].start:cut[7].stop].reshape(KT, P, 2 * NH).transpose(1, 0, 2),
        "gate_b": np.stack([b_in[cut[6]], b_in[cut[7]]], 1),
        "cache": a["cache_conv"][0].reshape(SB, PAST, CT, P).transpose(3, 2, 0, 1),
        "w_cgcv": pairs(wb["cg"], wb["cv"]),
        "w_head": heads(wb),
        "w_ga": wb["ga"],
        "w_co": blocks(a["w_conv_out"][0]).reshape(N_CO, 2, P, CT * P).transpose(0, 2, 1, 3).reshape(N_CO, P, KT * P),
        "w_o": blocks(a["w_out"][0]),
        "w_fi": pairs(wfi[:FT], wfi[FT:]),
        "w_fo0": blocks(wfo[rows_of[0]:rows_of[1]]),
        "w_fo1": blocks(wfo[rows_of[1]:rows_of[2]]),
        "w_fo2": blocks(wfo[rows_of[2]:rows_of[3]]),
        "st_c": a["state_mlstm_C"][0].reshape(SB, NH, HD, 2, P).transpose(1, 4, 0, 3, 2),
        "st_n": a["state_mlstm_n"][0].reshape(SB, NH, 2, P).transpose(3, 1, 2, 0),
        "st_m": a["state_mlstm_m"][0].T,
    }
    outs = {
        "y": (P, KT, T), "conv_p": (P, CT, PAST), "conv_s": (P, CT, SB, PAST), "cn_p": (NH, P, 2, VE),
        "m_p": (NH, 1), "c_s": (NH, P, SB, 2, HD), "n_s": (P, NH, 2, SB), "m_s": (NH, SB),
    }
    nc = bacc.Bacc("TRN2", target_bir_lowering=False, num_devices=1)
    ins = {f"{k}_in": np.ascontiguousarray(v) for k, v in ins.items()}
    args = [nc.dram_tensor(k, v.shape, F32, kind="ExternalInput").ap() for k, v in ins.items()]
    args += [nc.dram_tensor(f"{k}_out", v, F32, kind="ExternalOutput").ap() for k, v in outs.items()]
    build(nc, *args)
    res = run_bass_kernel_spmd(nc, [ins], core_ids=[0]).results[0]
    r = {k: res[f"{k}_out"] for k in outs}

    yt = r["y"].transpose(2, 1, 0).reshape(T, D)
    cn = r["cn_p"].transpose(0, 3, 2, 1).reshape(NH, VE, HD)
    c = np.ascontiguousarray
    return (c(yt[:TP]).reshape(1, TP, D), c(yt[TP:]).reshape(SB, SL, D),
            c(r["conv_p"].transpose(2, 1, 0)).reshape(1, 1, PAST, DC),
            c(cn[:, :HD]).reshape(1, 1, NH, HD, HD), c(cn[:, HD]).reshape(1, 1, NH, HD),
            c(r["m_p"]).reshape(1, 1, NH),
            c(r["conv_s"].transpose(2, 3, 1, 0)).reshape(1, SB, PAST, DC),
            c(r["c_s"].transpose(2, 0, 4, 3, 1)).reshape(1, SB, NH, HD, HD),
            c(r["n_s"].transpose(3, 1, 2, 0)).reshape(1, SB, NH, HD),
            c(r["m_s"].T).reshape(1, SB, NH))
```

```python
from contextlib import ExitStack

import numpy as np

import concourse.bass as bass
from concourse import mybir

F32 = mybir.dt.float32
F32R = mybir.dt.float32r
ALU = mybir.AluOpType
ACT = mybir.ActivationFunctionType

P = 128
D = 1024
KT = D // P
TP, TS = 512, 64
T = TP + TS
HALF = T // 2
SB, SL = 8, 8
SG = SB // 2
GT = SG * SL
RING = 3
NH, HD = 4, 256
VE = HD + 1
NB = TP // P
DC = 512
CT = DC // P
CW = 31
PAST = CW - 1
FF = 2816
FT = FF // P
GROUPS = (8, 8, 6)
EPS = 1e-6
BIG = 1e30

U_A = 0
N_A = 2 * CT
U_B = U_A + N_A
PER_HEAD = 10
U_GA = U_B + NH * PER_HEAD
U_CO = U_GA + KT
N_CO = KT // 2
U_O = U_CO + N_CO
U_FF = U_O + KT
U_E, U_F, Q_E = [], [], []
_u, _q = U_FF, 0
for _g in GROUPS:
    U_E.append(_u)
    U_F.append(_u + 2 * _g)
    Q_E.append(_q)
    _u += 2 * _g + KT
    _q += _g
NU = _u

V_BIAS = 0
V_GMIX = U_CO
V_GFFN = V_GMIX + KT
V_GFIN = V_GFFN + KT
V_GMN = V_GFIN + KT
V_GCN = V_GMN + KT
V_BCN = V_GCN + CT
V_BDW = V_BCN + CT
V_WDW = V_BDW + CT
NV = V_WDW + CT * CW

I_G = 0
I_EM = 5
I_WS = 10
I_OFF = 15
I_WI = 21
NI = 22
OFF = {}
for _s in range(NB):
    for _t in range(_s + 1, NB):
        OFF[_s, _t] = I_OFF + len(OFF)

S_USE, T_USE, I_USE, K_USE, PV_USE, CP_USE, CS_USE, N_USE, HT_USE = 0, 5, 10, 11, 13, 18, 20, 28, 29
USES = 32
READER = ["dve"] * 5 + ["act"] * (5 + 1 + 2 + 5 + 2) + ["dve"] * (8 + 1 + 3)
ACT_USES, DVE_USES = READER.count("act"), READER.count("dve")
W_OFF = [0, 512, 896, 1152, 1280]
W_COLS = 1280 + TS

Y_POOL = 3
SQ1 = KT // 2 + 1
START = 1
C_B = START + N_A // 2
C_GA = C_B + NH * PER_HEAD // 2
C_CO = C_GA + KT // 2
C_O = C_CO + N_CO // 2
C2_HEADS, C3_HEADS = 4, 3
C2_CO, C3_CO = C2_HEADS + 1, C3_HEADS + 1
C2_NORM = C2_CO + N_CO // 2
C_E, C_F = [], []
_c, _c2, _c3 = C_O + 4, C2_NORM + 1, C3_CO + N_CO // 2
for _g in GROUPS:
    C_E.append((_c, _c, _c2, _c3))
    C_F.append(_c + _g // 2)
    _c, _c2, _c3 = _c + _g // 2 + 4, _c2 + _g // 2, _c3 + _g // 2
C2_END = _c2

POOL_SET = 17
DVE_HEAD_STEPS = 89
CONV_TAPS = (4, 5, 5, 5, 4, 4, 2, 2, 0, 0)


class Tally:

    def __init__(self, eng, sem):
        self.eng, self.sem, self.n, self.turn = eng, sem, 0, 0

    def on(self, ins):
        ins.then_inc(self.sem, 1)
        self.n += 1

    def settle(self, back=0):
        self.eng.wait_ge(self.sem, self.turn + (self.n - back))

    def loop(self, i, per):
        self.start, self.per, self.turn = self.n, per, i * per

    def end(self, iters):
        assert self.n - self.start == self.per, f"per iteration: {self.n - self.start}, not {self.per}"
        self.n, self.turn = self.start + iters * self.per, 0


def build(nc, xT, vecs, gate_w, gate_b, cache, w_cgcv, w_head, w_ga, w_co, w_o, w_fi, w_fo0, w_fo1, w_fo2,
          st_c, st_n, st_m, y, conv_p, conv_s, cn_p, m_p, c_s, n_s, m_s):
    with ExitStack() as ctx:
        place = [-(-nc.sbuf_base // 32) * 32]

        def sb(name, cols, dt=F32, parts=P):
            shape = [parts] + (list(cols) if isinstance(cols, (list, tuple)) else [cols])
            t = nc.alloc_sbuf_tensor_at(name, shape, dt, offset=place[0])
            place[0] += -(-4 * int(np.prod(shape[1:])) // 32) * 32
            return t

        def sem(name):
            return ctx.enter_context(nc.semaphore(name))

        x_base = place[0]
        x = sb("x", [KT, T])
        h_hi = sb("h_hi", [KT, T], F32R)
        h_lo = sb("h_lo", [KT, T], F32R)
        raw = sb("raw", [2, KT * P])
        w_hi = sb("w_hi", [2, KT * P], F32R)
        w_lo = sb("w_lo", [2, KT * P], F32R)
        vec = sb("vec", NV)
        mean_d = sb("mean_d", P)
        mean_c = sb("mean_c", P)
        eps = sb("eps", 1)
        warm = sb("warm", 1)
        tmp = sb("tmp", [2, T])
        hf_base = place[0]
        hf = sb("hf", [2, T])
        acc = sb("acc", T)
        rs = sb("rs", T)
        merged_base = place[0]
        merged = sb("merged", [KT, T])
        conv = sb("conv", [CT, T])
        ident = sb("ident", P)
        xg_hi = nc.alloc_sbuf_tensor_at("xg_hi", [P, KT, T], F32R, offset=merged_base)
        pool_base = place[0]
        a_p = sb("a_p", [CT, PAST + TP])
        a_s = sb("a_s", [CT, SB, PAST + SL])
        negm = sb("negm", [NH, T])
        place3 = sb("place3", [2, 6, GT], F32R)
        cols = sb("cols", [NI, NH])
        dec = sb("dec", [NH, SB])
        onehot = sb("onehot", SB)
        oh96 = sb("oh96", SG)
        wb = sb("wb", [NH, SB])
        nst = sb("nst", [NH, 2, SB])
        nnew = sb("nnew", [NH, 2, SB])
        cmask = sb("cmask", P)
        smask = sb("smask", TS)
        head_base = place[0]
        gw = sb("gw", [KT, 2 * NH])
        gstat = sb("gstat", [KT, P], F32R)
        gt = sb("gt", [2, T], parts=NH)
        gb = sb("gb", 2, parts=NH)
        m0 = sb("m0", SB, parts=NH)
        li = sb("li", T, parts=NH)
        fz = sb("fz", T, parts=NH)
        lf = sb("lf", T, parts=NH)
        ft = sb("ft", T, parts=NH)
        seg = sb("seg", T, parts=NH)
        lfm = sb("lfm", T, parts=NH)
        lim = sb("lim", T, parts=NH)
        mrow = sb("mrow", T, parts=NH)
        nrow = sb("nrow", T, parts=NH)
        rows = sb("rows", NI * P, parts=NH)
        t8 = sb("t8", SB, parts=NH)
        mend = sb("mend", SB, parts=NH)
        drow = sb("drow", SB, parts=NH)
        sel = sb("sel", [NH, P], parts=NH)
        xg_lo = sb("xg_lo", [KT, T], F32R)
        assert place[0] <= nc.sbuf_usable_end
        place[0] = head_base
        qkv = sb("qkv", [3, 2, T])
        qk_flat = qkv[:, :, :, :].rearrange("p a b n -> p (a b n)")
        wvn = qk_flat[:, 0:NB * VE].rearrange("p (s v) -> p s v", s=NB)
        wvs = nc.alloc_sbuf_tensor_at("wvs", [P, SB, HD], F32R, offset=head_base + 4 * 2 * T)
        kvn_base = place[0]
        kvn = sb("kvn", [5, 2 * HD + 2])
        num = sb("num", [5, VE])
        wts_base = place[0]
        wts = sb("wts", W_COLS)
        mdiag = sb("mdiag", [NB, P])
        msamp = sb("msamp", TS)

        cs = sb("cs", [SB, 2, HD])
        cp = sb("cp", [2, VE])
        cs_lo_base = place[0]
        cs_lo = sb("cs_lo", [RING, 2 * HD], F32R)
        stats = sb("stats", [5, 6])
        mv = sb("mv", [5, 2])
        small = sb("small", [4, 5])
        nq8 = sb("nq8", SB)
        nq1 = sb("nq1", 1)
        assert place[0] <= nc.sbuf_usable_end, place[0]
        place[0] = x_base
        qm = sb("qm", [2, SB * (2 * TS + SL)], F32R)
        cs_hi_base = place[0]
        cs_hi = sb("cs_hi", [RING, 2 * HD], F32R)
        inter = sb("inter", HD + SB)
        inter_lo = sb("inter_lo", HD)
        assert place[0] <= x_base + 4 * KT * T
        w2_hi = nc.alloc_sbuf_tensor_at("wts_hi", [P, W_OFF[NB]], F32R, offset=cs_hi_base)
        w2_lo = nc.alloc_sbuf_tensor_at("wts_lo", [P, W_OFF[NB]], F32R, offset=wts_base)
        v_hi = nc.alloc_sbuf_tensor_at("v_hi", [P, NB, VE + 1], F32R, offset=cs_lo_base)
        kvn_lo = nc.alloc_sbuf_tensor_at("kvn_lo", [P, 5, 2 * HD + 2], F32R, offset=kvn_base)
        assert W_OFF[NB] <= RING * 2 * HD and NB * (VE + 1) <= RING * 2 * HD
        kv_hi = nc.alloc_sbuf_tensor_at("kv_hi", [P, 2 * HD], F32R, offset=hf_base)
        kv_lo = nc.alloc_sbuf_tensor_at("kv_lo", [P, 2 * HD], F32R, offset=hf_base + 4 * 2 * HD)
        stk = nc.alloc_sbuf_tensor_at("stk", [P, 2, 2 * HD], F32R, offset=hf_base + 4 * 2 * T)
        place[0] = pool_base
        ga = sb("ga", [KT, T])
        place[0] = head_base
        c_hi = sb("c_hi", [CT, T], F32R)
        c_lo = sb("c_lo", [CT, T], F32R)
        m_hi = sb("m_hi", [KT, T], F32R)
        m_lo = sb("m_lo", [KT, T], F32R)
        assert place[0] <= nc.sbuf_usable_end, place[0]
        place[0] = pool_base
        hid_hi = sb("hid_hi", [8, T], F32R)
        hid_lo = sb("hid_lo", [8, T], F32R)
        assert place[0] <= head_base + 2 * CT * T * 4

        ps = ctx.enter_context(nc.psum_tensor("ps", [P, 8, 512], F32))

        def slot(s):
            return ps[:, 2 * s:2 * s + 2, 0:HALF]

        def bank(k):
            return ps[:, 4 + k % 4, :]

        def halves(t, j):
            if isinstance(j, int):
                return t[:, j, :].rearrange("p (b n) -> p b n", b=2)
            return t[:, bass.ds(j, 1), :].rearrange("p o (b n) -> p (o b) n", b=2)

        def flat(t):
            return t[:, :].rearrange("p (b n) -> p b n", b=2)

        def row(t, j):
            if isinstance(j, int):
                return t[:, j, :]
            return t[:, bass.ds(j, 1), :].rearrange("p o n -> p (o n)")

        def vcol(c, parts=P):
            return vec[0:parts, c:c + 1] if isinstance(c, int) else vec[0:parts, bass.ds(c, 1)]

        x_loaded = [sem(f"x_loaded{k}") for k in range(KT)]
        vec_loaded = sem("vec_loaded")
        gw_loaded = sem("gw_loaded")
        gb_loaded = sem("gb_loaded")
        m0_loaded = sem("m0_loaded")
        cache_loaded = sem("cache_loaded")
        n_loaded = sem("n_loaded")
        cs_loaded = sem("cs_loaded")
        raw_loaded = [sem(f"raw_loaded{s}") for s in range(2)]
        consts_ready = sem("consts_ready")
        masks_ready = sem("masks_ready")
        head_bufs_set = sem("head_bufs_set")
        hi_ready = sem("hi_ready")
        lo_ready = sem("lo_ready")
        unit_done = sem("unit_done")
        slot_read = [sem(f"slot_read{s}") for s in range(4)]
        sq_ready = sem("sq_ready")
        sq_added = sem("sq_added")
        sq_added_odd = sem("sq_added_odd")
        sum_done = sem("sum_done")
        xghi_ready = sem("xg_hi_ready")
        xglo_ready = sem("xg_lo_ready")
        hf_ready = sem("hf_ready")
        hhi_ready = sem("h_hi_ready")
        hlo_ready = sem("h_lo_ready")
        h2lo_ready = sem("ffn_input_lo_ready")
        sig_ready = sem("sigmoid_ready")
        a_ready = sem("a_ready")
        gstat_hi = sem("gstat_hi_ready")
        gstat_lo = sem("gstat_lo_ready")
        gates_done = sem("gates_done")
        gt_ready = sem("gt_ready")
        fabs_ready = sem("fabs_ready")
        ln_ready = sem("ln_ready")
        mrow_ready = sem("mrow_ready")
        exps_in = sem("exp_rows_ready")
        exps_out = sem("exps_done")
        turned = sem("cols_turned")
        negm_spread = sem("negm_spread")
        mdiag_ready = sem("mdiag_ready")
        w_ready = sem("w_ready")
        qm_ready = sem("qm_ready")
        gb_used = sem("gb_used")
        attn_ready = sem("attn_ready")
        act_read = sem("bank_read_by_act")
        dve_read = sem("bank_read_by_dve")
        wv_ready = sem("wv_ready")
        place_ready = sem("placement_ready")
        kvsplit_ready = sem("samples_kv_split")
        wvs_ready = sem("wvs_ready")
        pvhi_ready = sem("weights_and_v_hi_ready")
        pvlo_ready = sem("weights_and_v_lo_ready")
        cshi_ready = sem("old_state_hi_ready")
        cslo_ready = sem("old_state_lo_ready")
        old_used = sem("old_state_used")
        x_reloaded = sem("x_reloaded")

        hm_ready = sem("hm_ready")
        rs_ready = sem("rs_ready")
        hvar_ready = sem("hvar_ready")
        hdev_ready = sem("hdev_ready")
        cp_stored = sem("cp_stored")
        cp_free = sem("cp_free")
        cs_stored = sem("cs_stored")
        out_stored = sem("out_stored")
        csum_ready = sem("csum_ready")
        cstat_done = sem("cstat_done")
        cdev_ready = sem("cdev_ready")
        csq_ready = sem("csq_ready")
        csq_added = sem("csq_added")
        cnorm_ready = sem("cnorm_ready")
        csilu_ready = sem("csilu_ready")
        chi_ready = sem("chi_ready")
        clo_ready = sem("clo_ready")
        co_first = sem("co_first_done")
        m_ready = sem("merged_ready")
        mhi_ready = sem("merged_hi_ready")
        mlo_ready = sem("merged_lo_ready")
        silu_ready = sem("silu_ready")
        hid_ready = sem("hid_ready")
        hidhi_ready = sem("hid_hi_ready")
        hidlo_ready = sem("hid_lo_ready")
        y_ready = sem("y_ready")
        y_pool_ready = sem("y_pool_ready")
        xfin_ready = sem("x_times_final_gain_ready")
        y_stored = sem("y_stored")
        acc_zero = sem("acc_zero")
        dve_step = sem("dve_step")
        act_step = sem("act_step")
        pool_step = sem("pool_step")

        block = ctx.enter_context(nc.Block())

        @block.sync
        def _(sp):
            for s in (slot_read[0], slot_read[1], act_read, dve_read, gb_used, hidlo_ready, cp_free):
                sp.sem_inc(s, START)
            sp.dma_start(vec[:, :], vecs).then_inc(vec_loaded, 16)
            sp.dma_start(gw[:, :, :], gate_w).then_inc(gw_loaded, 16)
            for k in range(KT):
                sp.dma_start(x[:, k, :], xT[:, k, :]).then_inc(x_loaded[k], 16)
                if k == 0:
                    sp.dma_start(raw[:, 0, :], w_cgcv[0]).then_inc(raw_loaded[0], 16)
            sp.dma_start(raw[:, 1, :], w_cgcv[1]).then_inc(raw_loaded[1], 16)
            sp.dma_start(gb[:, :], gate_b).then_inc(gb_loaded, 16)
            sp.dma_start(m0[:, :], st_m).then_inc(m0_loaded, 16)
            sp.dma_start(a_s[:, :, :, 0:PAST], cache).then_inc(cache_loaded, 16)
            sp.dma_start(nst[:, :, :, :], st_n).then_inc(n_loaded, 16)

            def loads(base, w, count, cols=KT * P, first=0):
                with sp.Fori(first, count // 2) as i:
                    for s in range(2):
                        sp.wait_ge(lo_ready, i * 2 + (base + s - 1))
                        sp.dma_start(raw[:, s, 0:cols], w[bass.ds(i * 2 + s, 1)].rearrange("o p n -> (o p) n"))\
                          .then_inc(raw_loaded[s], 16)

            loads(U_A, w_cgcv, N_A, first=1)
            loads(U_B, w_head, NH * PER_HEAD)
            loads(U_GA, w_ga, KT)
            sp.wait_ge(hvar_ready, NH)
            for c in range(N_CO):
                sp.wait_ge(lo_ready, U_CO + c - 1)
                sp.dma_start(raw[:, c % 2, :], w_co[c]).then_inc(raw_loaded[c % 2], 16)
                for k in range(2 * c, 2 * c + 2):
                    sp.dma_start(x[:, k, :], xT[:, k, :]).then_inc(x_reloaded, 16)
            loads(U_O, w_o, KT)
            for g, w in enumerate((w_fo0, w_fo1, w_fo2)):
                loads(U_E[g], w_fi[2 * Q_E[g]:2 * (Q_E[g] + GROUPS[g])], 2 * GROUPS[g])
                loads(U_F[g], w, KT, GROUPS[g] * P)
            for n in range(KT - Y_POOL):
                sp.wait_ge(y_ready, n + 1)
                sp.dma_start(y[:, Y_POOL + n, :], x[:, Y_POOL + n, :]).then_inc(y_stored, 16)
                if n < Y_POOL:
                    sp.wait_ge(y_pool_ready, n + 1)
                    sp.dma_start(y[:, n, :], x[:, n, :]).then_inc(y_stored, 16)
            sp.wait_ge(y_stored, 16 * KT)

        @block.gpsimd
        def _(pool):
            steps = Tally(pool, pool_step)
            steps.on(pool.memset(gstat[:, :, :].rearrange("p k c -> p (k c)").bitcast(F32), 0.0))
            pool.memset(mean_d[:, :], 1.0 / D).then_inc(consts_ready, 1)
            pool.memset(mean_c[:, :], 1.0 / DC).then_inc(consts_ready, 1)
            pool.memset(eps[:, :], EPS).then_inc(consts_ready, 1)

            for k in range(1, KT, 2):
                pool.wait_ge(sq_ready, k + 1)
                if k == 1:
                    pool.tensor_copy(hf[:, 0, :], tmp[:, 1, :]).then_inc(sq_added_odd, 1)
                else:
                    pool.wait_ge(sq_added_odd, k // 2)
                    pool.tensor_tensor(hf[:, 0, :], hf[:, 0, :], tmp[:, 1, :], ALU.add).then_inc(sq_added_odd, 1)
            steps.on(pool.memset(seg[:, :], 1.0))
            steps.on(pool.memset(rows[:, :], 1.0))
            steps.on(pool.memset(a_p[:, :, 0:PAST], 0.0))
            steps.on(pool.memset(ident[:, :], 0.0))
            steps.on(pool.memset(cmask[:, :], 0.0))
            steps.on(pool.memset(smask[:, :], 0.0))
            steps.on(pool.memset(onehot[:, :], 1.0))
            steps.on(pool.memset(place3[:, :, :, :].rearrange("p g r t -> p (g r t)").bitcast(F32), 0.0))
            steps.on(pool.memset(sel[:, :, :], 1.0))
            steps.settle()
            steps.on(pool.memset(seg[:, 0:TP:P], 0.0))
            steps.on(pool.memset(seg[:, TP:T:SL], 0.0))
            steps.on(pool.affine_select(out=ident[:, :], in_=ident[:, :], compare_op=ALU.not_equal, fill=1.0,
                                        base=0, pattern=[[-1, P]], channel_multiplier=1))
            steps.on(pool.affine_select(out=cmask[:, :], in_=cmask[:, :], compare_op=ALU.is_ge, fill=-BIG,
                                        base=0, pattern=[[1, P]], channel_multiplier=-1))
            steps.on(pool.affine_select(out=smask[:, :], in_=smask[:, :], compare_op=ALU.is_ge, fill=-BIG,
                                        base=0, pattern=[[1, TS]], channel_multiplier=-1))
            steps.on(pool.affine_select(out=onehot[:, :], in_=onehot[:, :], compare_op=ALU.is_ge, fill=0.0,
                                        base=0, pattern=[[-SL, SB]], channel_multiplier=1))
            steps.on(pool.affine_select(out=sel[:, :, :], in_=sel[:, :, :], compare_op=ALU.is_equal, fill=0.0,
                                        base=0, pattern=[[-1, NH], [0, P]], channel_multiplier=1))
            steps.settle()
            sm = smask[:, :].rearrange("p (b j) -> p b j", b=SB)
            pool.affine_select(out=sm, in_=sm, compare_op=ALU.is_ge, fill=-BIG,
                               base=0, pattern=[[-SL, SB], [0, SL]], channel_multiplier=1).then_inc(masks_ready, 1)
            pool.affine_select(out=onehot[:, :], in_=onehot[:, :], compare_op=ALU.is_ge, fill=0.0,
                               base=SL - 1, pattern=[[SL, SB]], channel_multiplier=-1).then_inc(masks_ready, 1)
            for k in range(KT):
                pool.wait_ge(hhi_ready, k + 1)
                pool.tensor_tensor(h_lo[:, k, :], hf[:, k % 2, :], h_hi[:, k, :].bitcast(F32), ALU.subtract)\
                    .then_inc(hlo_ready, 1)
            pool.wait_ge(mrow_ready, 1)
            pool.dma_start(m_p, mrow[:, TP - 1:TP]).then_inc(out_stored, 16)
            pool.wait_ge(exps_in, 1)
            pool.dma_start(m_s, mend[:, :]).then_inc(out_stored, 16)
            pool.wait_ge(out_stored, 32)
            pool.wait_ge(slot_read[2], C2_HEADS)
            pool.wait_ge(slot_read[3], C3_HEADS)
            pool.wait_ge(unit_done, N_A)
            pool.wait_ge(hf_ready, KT)
            pool.memset(qm[:, :, :].rearrange("p k n -> p (k n)").bitcast(F32), 0.0).then_inc(head_bufs_set, 1)
            pool.memset(num[:, 4, :], 0.0).then_inc(head_bufs_set, 1)
            pool.memset(kvn[:, :, 2 * HD:2 * HD + 2], 1.0).then_inc(head_bufs_set, 1)
            pool.dma_start(cs[:, :, :, :], st_c[0]).then_inc(cs_loaded, 16)

            pool.wait_ge(a_ready, 2 * CT)
            pool.dma_start(conv_p, a_p[:, :, TP:TP + PAST]).then_inc(out_stored, 16)
            pool.wait_ge(cache_loaded, 16)
            pool.dma_start(conv_s, a_s[:, :, :, SL:SL + PAST]).then_inc(out_stored, 16)

            def states(h, last=False):
                for b in range(SB):
                    pool.wait_ge(cshi_ready, h * SB + (b + 1))
                    pool.tensor_tensor(cs_lo[:, b % RING, :], cs[:, b, :, :].rearrange("p k v -> p (k v)"),
                                       cs_hi[:, b % RING, :].bitcast(F32), ALU.subtract).then_inc(cslo_ready, 1)
                for g in range(2):
                    pool.wait_ge(act_read, h * ACT_USES + (START + READER[:K_USE + g].count("act") + 1))
                    pool.tensor_tensor(wvs[0:3 * GT, g * SG:g * SG + SG, :],
                                       stk[0:3 * GT, g, HD:2 * HD].bitcast(F32).unsqueeze(1)
                                       .broadcast_to([3 * GT, SG, HD]),
                                       oh96[0:3 * GT, :].unsqueeze(2).broadcast_to([3 * GT, SG, HD]), ALU.mult)\
                        .then_inc(wvs_ready, 1)
                pool.wait_ge(act_read, h * ACT_USES + (START + ACT_USES))
                pool.dma_start(cn_p[bass.ds(h, 1)].rearrange("o p k v -> (o p) k v"), cp[:, :, :])\
                    .then_inc(cp_stored, 16)
                pool.wait_ge(dve_read, h * DVE_USES + (START + 13))
                pool.dma_start(c_s[bass.ds(h, 1)].rearrange("o p b k v -> (o p) b k v"), cs[:, :, :, :])\
                    .then_inc(cs_stored, 16)
                pool.wait_ge(cs_stored, h * 16 + 16)
                pool.wait_ge(cp_stored, h * 16 + 16)
                pool.sem_inc(cp_free, 1)
                if not last:
                    pool.dma_start(cs[:, :, :, :], st_c[bass.ds(h + 1, 1)].rearrange("o p b k v -> (o p) b k v"))\
                        .then_inc(cs_loaded, 16)

            with pool.Fori(0, NH - 1) as h:
                states(h)
            states(NH - 1, last=True)
            pool.wait_ge(dve_read, START + NH * DVE_USES)
            pool.dma_start(n_s, nnew[:, :, :, :]).then_inc(out_stored, 16)
            for j in range(CT):
                pool.wait_ge(chi_ready, j + 1)
                pool.tensor_tensor(c_lo[:, j, :], conv[:, j, :], c_hi[:, j, :].bitcast(F32), ALU.subtract)\
                    .then_inc(clo_ready, 1)
            pool.wait_ge(cp_stored, 16 * NH)
            pool.wait_ge(out_stored, 16 * 5)
            with pool.Fori(0, KT) as j:
                pool.wait_ge(mhi_ready, j + 1)
                pool.tensor_tensor(row(m_lo, j), row(merged, j), row(m_hi, j).bitcast(F32), ALU.subtract)\
                    .then_inc(mlo_ready, 1)

            pool.wait_ge(rs_ready, 3)
            for g, n in enumerate(GROUPS):
                with pool.Fori(0, n // 2) as i:
                    for s in range(2):
                        pool.wait_ge(slot_read[2 * s + 1], i + (C_E[g][2 * s + 1] + 1))
                        pool.tensor_tensor(hf[:, s, :], hf[:, s, :], rs[:, :], ALU.mult).then_inc(hid_ready, 1)
                        pool.wait_ge(hidhi_ready, i * 2 + (Q_E[g] + s + 1))
                        pool.tensor_tensor(row(hid_lo, i * 2 + s), hf[:, s, :], row(hid_hi, i * 2 + s).bitcast(F32),
                                           ALU.subtract).then_inc(hidlo_ready, 1)
            pool.wait_ge(xfin_ready, KT)
            for b in range(2):
                pool.wait_ge(rs_ready, 4 + b)
                for k in range(Y_POOL):
                    at = slice(b * HALF, (b + 1) * HALF)
                    ins = pool.tensor_tensor(x[:, k, at], x[:, k, at], rs[:, at], ALU.mult)
                    if b:
                        ins.then_inc(y_pool_ready, 1)
                    else:
                        steps.on(ins)

        @block.scalar
        def _(act):
            steps = Tally(act, act_step)

            def split_hi(pair, s, first=False):
                act.wait_ge(raw_loaded[s], pair * 16 + 16)
                if not first:
                    act.wait_ge(unit_done, pair * 2 + (s - 1))
                act.activation(w_hi[:, s, :], raw[:, s, :], ACT.Copy).then_inc(hi_ready, 1)

            act.wait_ge(consts_ready, 3)
            steps.on(act.activation(warm[:, :], eps[:, :], ACT.Copy))
            act.wait_ge(vec_loaded, 16)
            for k in range(KT):
                act.wait_ge(x_loaded[k], 16)
                act.activation(xg_hi[:, k, :], x[:, k, :], ACT.Copy, scale=vcol(V_GMIX + k)).then_inc(xghi_ready, 1)
                if k >= 2:
                    act.wait_ge(sq_added_odd if k % 2 else sq_added, k // 2)
                act.activation(tmp[:, k % 2, :], x[:, k, :], ACT.Square).then_inc(sq_ready, 1)
                if k == 1:
                    split_hi(0, 0, True)
                if k == 0:
                    act.wait_ge(gw_loaded, 16)
                    act.wait_ge(pool_step, 1)
                    for g in range(2):
                        act.activation(gstat[:, :, 64 * g:64 * g + NH], gw[:, :, NH * g:NH * g + NH], ACT.Copy)\
                            .then_inc(gstat_hi, 1)
            split_hi(0, 1, True)

            def deviation(s, done_sem, n):
                act.wait_ge(done_sem, n)
                act.activation(flat(rs), slot(s), ACT.Sqrt, bias=eps[:, :]).then_inc(slot_read[s], 1)

            def norm_hi(k):
                act.wait_ge(hf_ready, k + 1)
                act.activation(h_hi[:, k, :], hf[:, k % 2, :], ACT.Copy).then_inc(hhi_ready, 1)

            def conv_gate(pair):
                act.wait_ge(slot_read[0], pair + START + 1)
                act.activation(tmp[:, pair % 2, :], tmp[:, pair % 2, :], ACT.Sigmoid, bias=vcol(2 * pair))\
                    .then_inc(sig_ready, 1)

            act.wait_ge(consts_ready, 3)
            deviation(3, sum_done, 1)
            act.wait_ge(gates_done, 1)
            for g in range(2):
                act.activation(gt[:, g, :].rearrange("p (b n) -> p b n", b=2),
                               ps[64 * g + 32:64 * g + 32 + NH, 4:6, 0:HALF], ACT.Copy).then_inc(gt_ready, 1)
            split_hi(1, 0)
            conv_gate(0)
            split_hi(1, 1)
            act.wait_ge(fabs_ready, 1)
            steps.on(act.activation(ft[:, :], ft[:, :], ACT.Exp, scale=-1.0))
            steps.settle()
            act.activation(ft[:, :], ft[:, :], ACT.Ln, bias=1.0).then_inc(ln_ready, 1)

            split_hi(2, 0)
            conv_gate(1)
            split_hi(2, 1)
            act.wait_ge(mrow_ready, 1)
            act.activation(rows[:, I_EM * P:I_EM * P + T], mrow[:, :], ACT.Exp, scale=-1.0).then_inc(exps_out, 1)
            split_hi(3, 0)
            act.wait_ge(exps_in, 1)
            act.activation(rows[:, I_WS * P:I_WS * P + T], rows[:, I_WS * P:I_WS * P + T], ACT.Exp)\
                .then_inc(exps_out, 1)
            act.activation(rows[:, I_WI * P:I_WI * P + TS], rows[:, I_WI * P:I_WI * P + TS], ACT.Exp)\
                .then_inc(exps_out, 1)
            act.activation(drow[:, :], t8[:, :], ACT.Exp).then_inc(exps_out, 1)
            conv_gate(2)
            for k in range(5):
                norm_hi(k)
            split_hi(3, 1)
            for k in range(5, KT):
                norm_hi(k)
            split_hi(4, 0)
            conv_gate(3)

            def keep_negm(h):
                act.wait_ge(negm_spread, h + 1)
                act.activation(halves(negm, h), slot(3 - h % 2), ACT.Copy).then_inc(slot_read[3 - h % 2], 1)

            keep_negm(0)
            split_hi(4, 1)
            for h in range(1, NH):
                keep_negm(h)

            def evac_bias(h, j, dst):
                act.wait_ge(unit_done, h * PER_HEAD + (U_B + j + 1))
                act.activation(dst, slot(j % 2), ACT.Identity, bias=vcol(h * PER_HEAD + (U_B + j)))\
                    .then_inc(slot_read[j % 2], 1)

            act.wait_ge(head_bufs_set, 3)
            act.wait_ge(slot_read[2], C2_HEADS)
            act.wait_ge(slot_read[1], C_B)
            with act.Fori(0, NH) as h:
                def hi_of(j):
                    split_hi(h * (PER_HEAD // 2) + (U_B + j + 2) // 2, j % 2)

                def use(k):
                    act.wait_ge(attn_ready, h * USES + (k + 1))

                for j in range(2):
                    hi_of(j)
                    evac_bias(h, j, halves(qkv[:, 0, :, :], j))
                hi_of(2)
                act.wait_ge(mdiag_ready, h + 1)

                def gcol(item, parts=P):
                    return cols[0:parts, item, bass.ds(h, 1)]

                for s in range(NB):
                    act.activation(wts[:, W_OFF[s]:W_OFF[s] + P], mdiag[:, s, :], ACT.Exp, bias=gcol(I_G + s))\
                        .then_inc(w_ready, 1)
                    for t in range(s + 1, NB):
                        o = W_OFF[s] + (t - s) * P
                        act.activation(wts[:, o:o + P], negm[:, bass.ds(h, 1), t * P:t * P + P]
                                       .rearrange("p o n -> p (o n)"), ACT.Exp,
                                       bias=gcol(OFF[s, t])).then_inc(w_ready, 1)
                act.activation(wts[0:TS, W_OFF[NB]:W_COLS], msamp[0:TS, :], ACT.Exp, bias=gcol(I_G + NB, TS))\
                    .then_inc(w_ready, 1)
                hi_of(3)
                for j in range(4, 6):
                    hi_of(j)
                    evac_bias(h, j, halves(qkv[:, 2, :, :], j - 4))
                def old_hi(b):
                    if b >= RING:
                        act.wait_ge(old_used, h * SB + (b - RING + 1))
                    act.activation(cs_hi[:, b % RING, :], cs[:, b, :, :].rearrange("p k v -> p (k v)"), ACT.Copy)\
                        .then_inc(cshi_ready, 1)

                act.wait_ge(cs_loaded, h * 16 + 16)
                for b in range(RING):
                    old_hi(b)
                for i in range(5):
                    use(T_USE + i)
                    n = P if i < NB else TS
                    act.activation(kvn[0:n, i, 0:2 * HD], bank(T_USE + i)[0:n, :], ACT.Copy).then_inc(act_read, 1)

                for b in range(RING, SB):
                    old_hi(b)
                use(I_USE)
                act.activation(inter_lo[0:TS, :], bank(I_USE)[TS:P, 0:HD], ACT.Copy)
                act.activation(inter[0:TS, :], bank(I_USE)[0:TS, 0:HD + SB], ACT.Copy).then_inc(act_read, 1)
                for g in range(2):
                    use(K_USE + g)
                    act.activation(stk[0:3 * GT, g, :], bank(K_USE + g)[0:3 * GT, :], ACT.Copy).then_inc(act_read, 1)
                act.wait_ge(dve_read, h * DVE_USES + (START + 5))
                act.activation(w2_hi[:, :], wts[:, 0:W_OFF[NB]], ACT.Copy).then_inc(pvhi_ready, 1)
                act.wait_ge(act_read, h * ACT_USES + (START + 5))
                act.activation(v_hi[:, :, :], kvn[:, 0:NB, HD:2 * HD + 2], ACT.Copy).then_inc(pvhi_ready, 1)
                for j in range(6, 8):
                    hi_of(j)
                    act.wait_ge(unit_done, h * PER_HEAD + (U_B + j + 1))
                    act.activation(halves(merged, h * 2 + (j - 6)), slot(j % 2), ACT.Sigmoid,
                                   bias=vcol(h * PER_HEAD + (U_B + j))).then_inc(slot_read[j % 2], 1)
                for i in range(5):
                    use(PV_USE + i)
                    n = P if i < NB else TS
                    act.activation(num[0:n, i, :], bank(PV_USE + i)[0:n, 0:VE], ACT.Copy).then_inc(act_read, 1)
                act.wait_ge(cp_free, h + START)
                for k in range(2):
                    use(CP_USE + k)
                    act.activation(cp[:, k, :], bank(CP_USE + k)[:, 0:VE], ACT.Copy).then_inc(act_read, 1)
                act.wait_ge(hvar_ready, h + 1)
                act.activation(small[:, 2, :], small[:, 1, :], ACT.Sqrt, bias=eps[:, :]).then_inc(hdev_ready, 1)
                for j in range(8, 10):
                    hi_of(j)
                    act.wait_ge(unit_done, h * PER_HEAD + (U_B + j + 1))
                    act.wait_ge(gb_used, h * 2 + START)
                    act.activation(halves(tmp, j % 2), slot(j % 2), ACT.Sigmoid,
                                   bias=vcol(h * PER_HEAD + (U_B + j))).then_inc(slot_read[j % 2], 1)

            def ga_unit(i, s):
                split_hi(i + (U_GA + 2) // 2, s)
                act.wait_ge(unit_done, i * 2 + (U_GA + s + 1))
                act.activation(halves(ga, i * 2 + s), slot(s), ACT.Sigmoid, bias=vcol(i * 2 + (U_GA + s)))\
                    .then_inc(slot_read[s], 1)

            act.wait_ge(dve_read, START + NH * DVE_USES)
            act.wait_ge(out_stored, 16 * 4)
            ga_unit(0, 0)
            for j in range(CT):
                act.wait_ge(cdev_ready, j + 1)
                if j >= 2:
                    act.wait_ge(csq_added, j - 1)
                act.activation(tmp[:, j % 2, :], conv[:, j, :], ACT.Square).then_inc(csq_ready, 1)
            ga_unit(0, 1)
            ga_unit(1, 0)
            deviation(3, cstat_done, 2)
            ga_unit(1, 1)
            for j in range(CT):
                if j == CT // 2:
                    ga_unit(2, 0)
                act.wait_ge(cnorm_ready, j + 1)
                act.activation(conv[:, j, :], conv[:, j, :], ACT.Silu, bias=vcol(V_BCN + j), scale=vcol(V_GCN + j))\
                    .then_inc(csilu_ready, 1)
                act.wait_ge(csilu_ready, j + 1)
                act.activation(c_hi[:, j, :], conv[:, j, :], ACT.Copy).then_inc(chi_ready, 1)

            for i, s in ((2, 1), (3, 0), (3, 1)):
                ga_unit(i, s)

            act.wait_ge(out_stored, 16 * 5)
            act.wait_ge(cp_stored, 16 * NH)
            act.wait_ge(cs_stored, 16 * NH)
            with act.Fori(0, N_CO // 2) as i:
                for p in range(2):
                    for o in range(2):
                        j = i * 4 + (2 * p + o)
                        act.wait_ge(m_ready, j + 1)
                        act.activation(row(m_hi, j), row(merged, j), ACT.Copy).then_inc(mhi_ready, 1)
                        if o == 0:
                            split_hi(i + (U_CO + 2) // 2, p)

            def squares(i, base, contents, sq_base, last=False):
                for s in range(2):
                    act.wait_ge(slot_read[s], i + (contents + 1))
                    act.wait_ge(sq_added, i * 2 + (sq_base + s - 1))
                    act.activation(tmp[:, s, :], row(x, i * 2 + s), ACT.Square).then_inc(sq_ready, 1)
                    if base == U_O:
                        act.activation(row(h_hi, i * 2 + s), row(x, i * 2 + s), ACT.Copy,
                                       scale=vcol(i * 2 + (V_GFFN + s))).then_inc(hhi_ready, 1)
                    if not last:
                        split_hi(i + (base + 2) // 2, s)
                    if base != U_O:
                        act.activation(row(x, i * 2 + s), row(x, i * 2 + s), ACT.Copy,
                                       scale=vcol(i * 2 + (V_GFIN + s))).then_inc(xfin_ready, 1)

            with act.Fori(0, KT // 2) as i:
                squares(i, U_O, C_O, SQ1)
            deviation(2, sum_done, 2)
            for g, n in enumerate(GROUPS):
                with act.Fori(0, n // 2) as i:
                    for p in range(2):
                        split_hi(i * 2 + (U_E[g] // 2 + p + 1), 0)
                        act.wait_ge(slot_read[2 * p], i + (C_E[g][2 * p] + 1))
                        act.activation(tmp[:, p, :], tmp[:, p, :], ACT.Silu).then_inc(silu_ready, 1)
                        split_hi(i * 2 + (U_E[g] // 2 + p + 1), 1)
                        act.wait_ge(hid_ready, i * 2 + (Q_E[g] + p + 1))
                        act.activation(row(hid_hi, i * 2 + p), hf[:, p, :], ACT.Copy).then_inc(hidhi_ready, 1)
                if g < len(GROUPS) - 1:
                    with act.Fori(0, KT // 2) as i:
                        for s in range(2):
                            split_hi(i + (U_F[g] + 2) // 2, s)
            with act.Fori(0, KT // 2 - 1) as i:
                squares(i, U_F[-1], C_F[-1], SQ1 + KT)
            squares(KT // 2 - 1, U_F[-1], C_F[-1], SQ1 + KT, last=True)
            deviation(2, sum_done, 3)

        @block.tensor
        def _(pe):
            def unit(u, s, w, occupied, hi, lo, nkt, ready=None):
                pe.wait_ge(lo_ready, u + 1)
                pe.wait_ge(slot_read[s], occupied)
                for k in range(nkt):
                    if ready is not None:
                        ready(k)
                    for wt, parts in ((w_hi, (hi, lo)), (w_lo, (hi,))):
                        for src in parts:
                            for b in range(2):
                                last = pe.matmul(ps[:, 2 * s + b, 0:HALF], wt[:, w, k * P:k * P + P],
                                                 src[:, k, b * HALF:b * HALF + HALF],
                                                 start=(k == 0 and wt is w_hi and src is hi),
                                                 stop=(k == nkt - 1 and wt is w_lo))
                last.then_inc(unit_done, 1)

            def mean(s, weights, src, done):
                for b in range(2):
                    last = pe.matmul(ps[:, 2 * s + b, 0:HALF], weights[:, :], src[:, b * HALF:b * HALF + HALF],
                                     start=True, stop=True)
                last.then_inc(done, 1)

            pe.wait_ge(gstat_hi, 2)
            pe.wait_ge(gstat_lo, 2)

            def gate_tile(k):
                pe.wait_ge(xglo_ready, k + 1)
                for src in (xg_hi, xg_lo):
                    for b in range(2):
                        last = pe.matmul(ps[:, 4 + b, 0:HALF], gstat[:, k, :], src[:, k, b * HALF:b * HALF + HALF],
                                         start=(k == 0 and src is xg_hi), stop=(k == KT - 1 and src is xg_lo))
                if k == KT - 1:
                    last.then_inc(gates_done, 1)

            gate_tile(0)
            gate_tile(1)
            def beside_first_unit(k):
                if k + 2 < KT:
                    gate_tile(k + 2)
                elif k == KT - 1:
                    pe.wait_ge(consts_ready, 2)
                    pe.wait_ge(sq_added, SQ1)
                    mean(3, mean_d, acc, sum_done)

            unit(0, 0, 0, START, xg_hi, xg_lo, KT, ready=beside_first_unit)
            unit(1, 1, 1, START, xg_hi, xg_lo, KT)
            with pe.Fori(1, N_A // 2 - 1) as i:
                for s in range(2):
                    unit(i * 2 + s, s, s, i + START, xg_hi, xg_lo, KT)
            unit(N_A - 2, 0, 0, C_B - 1, xg_hi, xg_lo, KT)
            pe.wait_ge(slot_read[2], 1)
            pe.wait_ge(exps_out, 4)
            pe.wait_ge(masks_ready, 2)
            for n in range(NI):
                pe.transpose(ps[:, 4, n * NH:n * NH + NH], rows[:, n * P:n * P + P], ident[0:NH, 0:NH])
            for h in range(NH):
                last = pe.matmul(ps[:, 5, h * SB:h * SB + SB], sel[:, h, :], drow[:, :], start=True, stop=True)
            last.then_inc(turned, 1)
            for h in range(NH):
                s = 3 - h % 2
                pe.wait_ge(slot_read[s], (1 if s == 3 else 2) + h // 2)
                for b in range(2):
                    last = pe.matmul(ps[:, 2 * s + b, 0:HALF], sel[:, h, :], nrow[:, b * HALF:b * HALF + HALF],
                                     start=True, stop=True)
                last.then_inc(negm_spread, 1)
                if h == 0:
                    unit(N_A - 1, 1, 1, C_B - 1, xg_hi, xg_lo, KT)
            pe.wait_ge(hlo_ready, KT)

            with pe.Fori(0, NH) as h:
                def head_unit(j, beside=None):
                    unit(h * PER_HEAD + (U_B + j), j % 2, j % 2, h * (PER_HEAD // 2) + (C_B + j // 2), h_hi, h_lo, KT,
                         ready=beside)

                def use(k):
                    samples = (S_USE + 4, T_USE + 4, PV_USE + 4, HT_USE + 2)
                    if k + 1 in samples and k >= 3:
                        read(k - 3)
                    if k in samples:
                        return
                    if k == 0:
                        pe.wait_ge(act_read, h * ACT_USES + START)
                        pe.wait_ge(dve_read, h * DVE_USES + START)
                    elif k >= 4:
                        read(k - 4)

                def read(k):
                    if READER[k] == "act":
                        pe.wait_ge(act_read, h * ACT_USES + (READER[:k].count("act") + START + 1))
                    else:
                        pe.wait_ge(dve_read, h * DVE_USES + (READER[:k].count("dve") + START + 1))

                for j in range(6):
                    head_unit(j)
                for s in range(2):
                    pe.wait_ge(slot_read[s], h * (PER_HEAD // 2) + (C_B + 2))
                for s in range(5):
                    use(S_USE + s)
                    t0, n, rows_ = (s * P, TP - s * P, P) if s < NB else (TP, TS, TS)
                    for k in range(2):
                        last = pe.matmul(bank(S_USE + s)[0:rows_, 0:n], qkv[:, 1, k, t0:t0 + rows_],
                                         qkv[:, 0, k, t0:t0 + n], start=(k == 0), stop=(k == 1))
                    last.then_inc(attn_ready, 1)
                for s in range(2):
                    pe.wait_ge(slot_read[s], h * (PER_HEAD // 2) + (C_B + 3))
                for s in range(5):
                    use(T_USE + s)
                    n = P if s < NB else TS
                    for c in range(4):
                        last = pe.transpose(bank(T_USE + s)[0:n, c * P:c * P + P],
                                            qkv[:, 1 + c // 2, c % 2, s * P:s * P + n], ident[:, :])
                    last.then_inc(attn_ready, 1)

                use(I_USE)
                pe.wait_ge(qm_ready, h * 2 + 2)

                def old_state(b):
                    pe.wait_ge(cslo_ready, h * SB + (b + 1))
                    for src in ((cs_hi, cs_lo) if b == 0 else (cs_lo, cs_hi)):
                        n = 2 * TS if src is cs_hi else TS
                        for k in range(2):
                            last = pe.matmul(bank(I_USE)[0:n, 0:HD], qm[:, k, b * 2 * TS:b * 2 * TS + n],
                                             src[:, b % RING, k * HD:k * HD + HD], start=(b == 0 and k == 0 and n > TS),
                                             stop=(b == SB - 1 and k == 1 and n > TS))
                    last.then_inc(old_used, 1)

                head_unit(6, beside=old_state)
                pe.wait_ge(n_loaded, 16)
                for k in range(2):
                    last = pe.matmul(bank(I_USE)[0:TS, HD:HD + SB], qkv[:, 0, k, TP:T],
                                     nst[:, bass.ds(h, 1), k, :].rearrange("p o b -> p (o b)"),
                                     start=(k == 0), stop=(k == 1))
                last.then_inc(attn_ready, 1)
                pe.wait_ge(place_ready, 4)
                pe.wait_ge(kvsplit_ready, h * 2 + 2)
                for g in range(2):
                    use(K_USE + g)
                    for c, (of_hi, of_lo) in enumerate(((2, 0), (1, 3))):
                        for first, src in ((of_hi, kv_hi), (of_lo, kv_lo)):
                            last = pe.matmul(bank(K_USE + g)[0:3 * GT, c * HD:c * HD + HD],
                                             place3[0:TS, g, first:first + 3, :].rearrange("p r t -> p (r t)"),
                                             src[0:TS, c * HD:c * HD + HD], start=(src is kv_hi), stop=(src is kv_lo))
                    last.then_inc(attn_ready, 1)
                head_unit(7)
                for t in range(5):
                    use(PV_USE + t)
                    if t == 0:
                        read(T_USE + 4)
                        pe.wait_ge(pvlo_ready, h * 2 + 2)
                    if t < NB:
                        for s in range(t + 1):
                            o = W_OFF[s] + (t - s) * P
                            pe.matmul(bank(PV_USE + t)[:, 0:VE + 1], w2_hi[:, o:o + P], v_hi[:, s, :],
                                      start=(s == 0), stop=False)
                            pe.matmul(bank(PV_USE + t)[:, 0:HD], w2_hi[:, o:o + P], kvn_lo[:, s, HD:2 * HD],
                                      start=False, stop=False)
                            last = pe.matmul(bank(PV_USE + t)[:, 0:VE + 1], w2_lo[:, o:o + P], v_hi[:, s, :],
                                             start=False, stop=(s == t))
                    else:
                        last = pe.matmul(bank(PV_USE + t)[0:TS, 0:VE], wts[0:TS, W_OFF[NB]:W_COLS],
                                         kvn[0:TS, NB, HD:2 * HD + 1], start=True, stop=True)
                    last.then_inc(attn_ready, 1)
                pe.wait_ge(wv_ready, h * NB + NB)
                for k in range(2):
                    use(CP_USE + k)
                    for s in range(NB):
                        last = pe.matmul(bank(CP_USE + k)[:, 0:VE], kvn[:, s, k * P:k * P + P], wvn[:, s, :],
                                         start=(s == 0), stop=(s == NB - 1))
                    last.then_inc(attn_ready, 1)
                pe.wait_ge(wvs_ready, h * 2 + 2)

                def state_update(b):
                    use(CS_USE + b)
                    for k in range(2):
                        last = pe.matmul(bank(CS_USE + b)[:, k * HD:k * HD + HD],
                                         stk[0:3 * GT, b // SG, k * P:k * P + P],
                                         wvs[0:3 * GT, b, :], start=True, stop=True)
                    last.then_inc(attn_ready, 1)

                head_unit(8, beside=state_update)
                use(N_USE)
                for k in range(2):
                    last = pe.matmul(bank(N_USE)[:, k * SB:k * SB + SB], kvn[0:TS, NB, k * P:k * P + P],
                                     wb[0:TS, bass.ds(h, 1), :].rearrange("p o b -> p (o b)"), start=True, stop=True)
                last.then_inc(attn_ready, 1)
                head_unit(9)
                pe.wait_ge(hm_ready, h * 5 + 5)
                for v in range(2):
                    use(HT_USE + v)
                    for s in range(NB):
                        last = pe.transpose(bank(HT_USE + v)[:, s * P:s * P + P], num[:, s, v * P:v * P + P],
                                            ident[:, :])
                    last.then_inc(attn_ready, 1)
                use(HT_USE + 2)
                for v in range(2):
                    last = pe.transpose(bank(HT_USE + 2)[:, v * TS:v * TS + TS], num[0:TS, NB, v * P:v * P + P],
                                        ident[0:TS, 0:TS])
                last.then_inc(attn_ready, 1)

            def ga_unit(i, s):
                unit(i * 2 + (U_GA + s), s, s, i + C_GA, h_hi, h_lo, KT)

            ga_unit(0, 0)
            pe.wait_ge(act_read, START + NH * ACT_USES)
            pe.wait_ge(dve_read, START + NH * DVE_USES)
            pe.wait_ge(csum_ready, 1)
            mean(2, mean_c, acc, cstat_done)
            ga_unit(0, 1)
            ga_unit(1, 0)
            pe.wait_ge(csq_added, CT)
            mean(3, mean_c, acc, cstat_done)
            ga_unit(1, 1)
            with pe.Fori(2, KT // 2) as i:
                for s in range(2):
                    ga_unit(i, s)

            def two_units(base, count_before, hi, lo, nkt, ready_sem, ready_base):
                with pe.Fori(0, KT // 2) as i:
                    for s in range(2):
                        unit(i * 2 + (base + s), s, s, i + count_before, hi, lo, nkt,
                             ready=(lambda k: pe.wait_ge(ready_sem, ready_base + k + 1)) if s == 0 else None)

            pe.wait_ge(clo_ready, CT)
            with pe.Fori(0, N_CO // 2) as i:
                for p in range(2):
                    pe.wait_ge(lo_ready, i * 2 + (U_CO + p + 1))
                    for o in range(2):
                        s = 2 * p + o
                        pe.wait_ge(slot_read[s], i + (C_CO, C_CO, C2_CO, C3_CO)[s])
                        for k in range(CT):
                            at = (o * CT + k) * P
                            for wt, parts in ((w_hi, (c_hi, c_lo)), (w_lo, (c_hi,))):
                                for src in parts:
                                    for b in range(2):
                                        last = pe.matmul(ps[:, 2 * s + b, 0:HALF], wt[:, p, at:at + P],
                                                         src[:, k, b * HALF:b * HALF + HALF],
                                                         start=(k == 0 and wt is w_hi and src is c_hi),
                                                         stop=(k == CT - 1 and wt is w_lo))
                        last.then_inc(unit_done if o else co_first, 1)
            two_units(U_O, C_O, m_hi, m_lo, KT, mlo_ready, 0)
            def ffn_input(k):
                if k == KT - 1:
                    pe.wait_ge(sq_added, SQ1 + KT)
                    pe.wait_ge(slot_read[2], C2_NORM)
                    mean(2, mean_d, acc, sum_done)
                pe.wait_ge(h2lo_ready, k + 1)

            for g, n in enumerate(GROUPS):
                if g == 0:
                    for j in range(4):
                        unit(U_E[0] + j, j, j % 2, C_E[0][j], h_hi, h_lo, KT, ready=ffn_input if j == 0 else None)
                with pe.Fori(1 if g == 0 else 0, n // 2) as i:
                    for j in range(4):
                        unit(i * 4 + (U_E[g] + j), j, j % 2, i + C_E[g][j], h_hi, h_lo, KT)
                two_units(U_F[g], C_F[g], hid_hi, hid_lo, n, hidlo_ready, START + Q_E[g])
            pe.wait_ge(sq_added, SQ1 + 2 * KT)
            pe.wait_ge(slot_read[2], C2_END)
            mean(2, mean_d, acc, sum_done)

        @block.vector
        def _(dve):
            steps = Tally(dve, dve_step)

            def split_lo(u, s):
                dve.wait_ge(hi_ready, u + 1)
                dve.tensor_tensor(w_lo[:, s, :], raw[:, s, :], w_hi[:, s, :].bitcast(F32), ALU.subtract)\
                    .then_inc(lo_ready, 1)

            def add_square(k):
                dve.wait_ge(sq_ready, k + 1)
                if k == 0:
                    dve.tensor_copy(acc[:, :], tmp[:, 0, :]).then_inc(sq_added, 1)
                else:
                    dve.wait_ge(sq_added, k // 2)
                    dve.tensor_tensor(acc[:, :], acc[:, :], tmp[:, 0, :], ALU.add).then_inc(sq_added, 1)

            def rstd(s, contents, n):
                dve.wait_ge(slot_read[s], contents)
                dve.reciprocal(rs[:, :], rs[:, :]).then_inc(rs_ready, 1)

            dve.wait_ge(vec_loaded, 16)
            for k in range(KT):
                dve.wait_ge(x_loaded[k], 16)
                dve.wait_ge(xghi_ready, k + 1)
                dve.scalar_tensor_tensor(xg_lo[:, k, :], x[:, k, :], vcol(V_GMIX + k), xg_hi[:, k, :].bitcast(F32),
                                         ALU.mult, ALU.subtract).then_inc(xglo_ready, 1)
                if k == 1:
                    split_lo(0, 0)
                if k == 0:
                    for g in range(2):
                        dve.wait_ge(gstat_hi, g + 1)
                        dve.tensor_tensor(gstat[:, :, 64 * g + 32:64 * g + 32 + NH], gw[:, :, NH * g:NH * g + NH],
                                          gstat[:, :, 64 * g:64 * g + NH].bitcast(F32), ALU.subtract)\
                            .then_inc(gstat_lo, 1)
                if k % 2 == 0:
                    add_square(k)
            dve.wait_ge(sq_added_odd, KT // 2)
            dve.wait_ge(sq_added, KT // 2)
            dve.tensor_tensor(acc[:, :], acc[:, :], hf[:, 0, :], ALU.add).then_inc(sq_added, 1)
            split_lo(1, 1)
            cvt = conv

            def scaled(u):
                dve.wait_ge(unit_done, u + 1)
                dve.tensor_tensor(halves(cvt if u % 2 else tmp, u // 2 % 2), slot(u % 2), flat(rs), ALU.mult)\
                    .then_inc(slot_read[u % 2], 1)

            def conv_input(pair):
                dve.wait_ge(slot_read[1], pair + START + 1)
                dve.wait_ge(sig_ready, pair + 1)
                v, sg, bias = cvt[:, pair % 2, :], tmp[:, pair % 2, :], vcol(2 * pair + 1)
                dve.scalar_tensor_tensor(a_p[:, pair, PAST:PAST + TP], v[:, 0:TP], bias, sg[:, 0:TP],
                                         ALU.add, ALU.mult).then_inc(a_ready, 1)
                per_sample = [t[:, TP:T].rearrange("p (b n) -> p b n", b=SB) for t in (v, sg)]
                dve.scalar_tensor_tensor(a_s[:, pair, :, PAST:PAST + SL], per_sample[0], bias, per_sample[1],
                                         ALU.add, ALU.mult).then_inc(a_ready, 1)

            def normalised(k):
                if k >= 2:
                    dve.wait_ge(hlo_ready, k - 1)
                dve.scalar_tensor_tensor(hf[:, k % 2, :], x[:, k, :], vcol(V_GMIX + k), rs[:, :], ALU.mult, ALU.mult)\
                    .then_inc(hf_ready, 1)

            rstd(3, 1, 1)
            dve.wait_ge(rs_ready, 1)
            scaled(0)
            split_lo(2, 0)
            scaled(1)
            split_lo(3, 1)
            dve.wait_ge(gates_done, 1)
            dve.wait_ge(gb_loaded, 16)
            dve.wait_ge(gt_ready, 2)
            for g, dst in ((1, fz), (0, li)):
                ins = dve.tensor_tensor(flat(dst), ps[64 * g:64 * g + NH, 4:6, 0:HALF],
                                        gt[:, g, :].rearrange("p (b n) -> p b n", b=2), ALU.add)
                if g:
                    steps.on(ins)
                else:
                    ins.then_inc(slot_read[2], 1)
            steps.settle()
            steps.on(dve.tensor_tensor(fz[:, :], fz[:, :], rs[0:NH, :], ALU.mult))
            steps.settle()
            steps.on(dve.tensor_scalar(fz[:, :], fz[:, :], gb[:, 1:2], None, ALU.add))
            steps.settle()
            dve.scalar_tensor_tensor(ft[:, :], fz[:, :], -1.0, fz[:, :], ALU.mult, ALU.max).then_inc(fabs_ready, 1)
            dve.wait_ge(slot_read[2], 1)
            steps.on(dve.tensor_tensor(li[:, :], li[:, :], rs[0:NH, :], ALU.mult))
            steps.settle()
            steps.on(dve.tensor_scalar(li[:, :], li[:, :], gb[:, 0:1], None, ALU.add))
            steps.settle()
            dve.wait_ge(pool_step, POOL_SET)
            dve.wait_ge(cache_loaded, 16)
            conv_input(0)
            scaled(2)
            split_lo(4, 0)

            dve.wait_ge(ln_ready, 1)
            steps.on(dve.scalar_tensor_tensor(lf[:, :], fz[:, :], 0.0, ft[:, :], ALU.min, ALU.subtract))
            steps.on(dve.tensor_copy(lim[:, :], li[:, :]))
            steps.settle()
            dve.wait_ge(m0_loaded, 16)
            first = slice(TP, T, SL)
            steps.on(dve.tensor_tensor(t8[:, :], lf[:, first], m0[:, :], ALU.add))
            steps.on(dve.tensor_copy(lfm[:, :], lf[:, :]))
            steps.on(dve.tensor_tensor_scan(ft[:, :], seg[:, :], lf[:, :], 0.0, ALU.mult, ALU.add))
            steps.settle()
            steps.on(dve.tensor_tensor(lim[:, first], t8[:, :], li[:, first], ALU.max))
            steps.on(dve.memset(lfm[:, first], -BIG))
            steps.settle()
            steps.on(dve.tensor_tensor(rows[:, 0:T], li[:, :], ft[:, :], ALU.subtract))
            dve.tensor_tensor_scan(mrow[:, :], lfm[:, :], lim[:, :], 0.0, ALU.add, ALU.max).then_inc(mrow_ready, 1)
            dve.wait_ge(mrow_ready, 1)
            end = slice(TP + SL - 1, T, SL)
            steps.on(dve.tensor_tensor(nrow[:, :], ft[:, :], mrow[:, :], ALU.subtract))
            steps.on(dve.tensor_tensor(t8[:, :], ft[:, end], mrow[:, end], ALU.subtract))
            steps.on(dve.tensor_copy(mend[:, :], mrow[:, end]))

            def total(t):
                return ft[:, t * P + P - 1:t * P + P]

            def item(n):
                return rows[:, n * P:n * P + P]

            for t in range(NB):
                steps.settle()
                for s in range(t + 1):
                    src = item(I_G + s) if s == t else item(OFF[s, t])
                    if t < NB - 1:
                        steps.on(dve.tensor_scalar(item(OFF[s, t + 1]), src, total(t), None, ALU.add))
                    else:
                        steps.on(dve.tensor_scalar(item(I_WS + s), src, total(t), mrow[:, TP - 1:TP],
                                                   ALU.add, ALU.subtract))
                if t == 0:
                    scaled(3)
                    split_lo(5, 1)

            def per_sample(t):
                return t.rearrange("p (b j) -> p b j", b=SB)

            def spread(t):
                return t.unsqueeze(2).broadcast_to([NH, SB, SL])

            steps.on(dve.tensor_tensor(per_sample(rows[:, I_WS * P + TP:I_WS * P + T]), per_sample(rows[:, TP:T]),
                                       spread(t8[:, :]), ALU.add))
            steps.on(dve.tensor_tensor(per_sample(rows[:, I_WI * P:I_WI * P + TS]), per_sample(nrow[:, TP:T]),
                                       spread(m0[:, :]), ALU.add))
            steps.settle()
            dve.tensor_tensor(t8[:, :], t8[:, :], m0[:, :], ALU.add).then_inc(exps_in, 1)
            conv_input(1)
            scaled(4)
            split_lo(6, 0)
            for k in range(5):
                normalised(k)
            scaled(5)
            split_lo(7, 1)
            conv_input(2)
            for k in range(5, KT):
                normalised(k)
            scaled(6)
            split_lo(8, 0)
            dve.wait_ge(turned, 1)
            steps.on(dve.tensor_copy(dec[:, :, :].rearrange("p h b -> p (h b)"), ps[:, 5, 0:NH * SB]))
            dve.tensor_copy(cols[:, :, :].rearrange("p i h -> p (i h)"), ps[:, 4, 0:NI * NH]).then_inc(slot_read[2], 1)
            dve.wait_ge(slot_read[2], 2)
            dve.wait_ge(masks_ready, 2)
            dve.wait_ge(n_loaded, 16)
            steps.on(dve.tensor_tensor(wb[0:TS, :, :], cols[0:TS, I_WS + NB, :].unsqueeze(2).broadcast_to([TS, NH, SB]),
                                       onehot[0:TS, :].unsqueeze(1).broadcast_to([TS, NH, SB]), ALU.mult))
            for r, g in enumerate((0, 1, 0)):
                steps.on(dve.tensor_copy(oh96[r * GT:r * GT + GT, :], onehot[g * GT:g * GT + GT, g * SG:g * SG + SG]))
            for g in range(2):
                for r in (2, 3):
                    dve.tensor_copy(place3[0:TS, g, r, :], ident[0:TS, g * GT:g * GT + GT]).then_inc(place_ready, 1)
            for k in range(2):
                steps.on(dve.tensor_tensor(nnew[:, :, k, :], nst[:, :, k, :], dec[:, :, :], ALU.mult))
            steps.settle()
            scaled(7)
            split_lo(9, 1)
            conv_input(3)
            dve.wait_ge(slot_read[2], C2_HEADS)
            dve.wait_ge(slot_read[3], C3_HEADS)
            dve.wait_ge(head_bufs_set, 3)
            dve.wait_ge(a_ready, 2 * CT)

            with dve.Fori(0, NH) as h:
                steps.loop(h, DVE_HEAD_STEPS)
                tap = [0]

                def lo_of(j):
                    split_lo(h * PER_HEAD + (U_B + j + 2), j % 2)
                    taps(j)

                def taps(j):
                    for _ in range(CONV_TAPS[j]):
                        conv_tap(tap[0])
                        tap[0] += 1

                def conv_tap(w):
                    out = row(conv, h)
                    wcol = vcol(h * CW + (V_WDW + w))
                    outs = (out[:, 0:TP], out[:, TP:T].rearrange("p (b j) -> p b j", b=SB))
                    ins = (row(a_p, h)[:, w:w + TP],
                           a_s[:, bass.ds(h, 1), :, w:w + SL].rearrange("p o b n -> p (o b) n"))
                    for o, a in zip(outs, ins):
                        if w == 0:
                            steps.on(dve.tensor_scalar(o, a, wcol, vcol(h + V_BDW), ALU.mult, ALU.add))
                        else:
                            steps.settle(back=1)
                            steps.on(dve.scalar_tensor_tensor(o, a, wcol, o, ALU.mult, ALU.add))

                def use(k):
                    dve.wait_ge(attn_ready, h * USES + (k + 1))

                def evacuated(s, n):
                    dve.wait_ge(slot_read[s], h * (PER_HEAD // 2) + (C_B + n))

                def hcol(item, parts=P):
                    return cols[0:parts, item, bass.ds(h, 1)]

                nh = row(negm, h)
                steps.on(dve.tensor_tensor(mdiag[:, :, :], nh[:, 0:TP].rearrange("p (s t) -> p s t", s=NB),
                                           cmask[:, :].unsqueeze(1).broadcast_to([P, NB, P]), ALU.add))
                dve.tensor_tensor(msamp[0:TS, :], nh[0:TS, TP:T], smask[0:TS, :], ALU.add).then_inc(mdiag_ready, 1)
                lo_of(0)
                lo_of(1)
                for j in (2, 3):
                    dve.wait_ge(unit_done, h * PER_HEAD + (U_B + j + 1))
                    dve.tensor_scalar(halves(qkv[:, 1, :, :], j - 2), slot(j % 2), vcol(h * PER_HEAD + (U_B + j)),
                                      HD ** -0.5, ALU.add, ALU.mult).then_inc(slot_read[j % 2], 1)
                    lo_of(j)
                def alone(part, k):
                    return qm[:, k, :].rearrange("p (b t) -> p b t", b=SB)[:, :, part * TS:part * TS + SL]

                for k in range(2):
                    evacuated(k, 1)
                    steps.on(dve.tensor_copy(alone(0, k), qkv[:, 0, k, TP:T].rearrange("p (b j) -> p b j", b=SB)))
                steps.settle()
                for k in range(2):
                    dve.tensor_tensor(alone(1, k), qkv[:, 0, k, TP:T].rearrange("p (b j) -> p b j", b=SB),
                                      alone(0, k).bitcast(F32), ALU.subtract).then_inc(qm_ready, 1)
                lo_of(4)
                split_lo(h * PER_HEAD + (U_B + 7), 1)
                for s in range(5):
                    use(S_USE + s)
                    dve.wait_ge(w_ready, h * 11 + (4, 7, 9, 10, 11)[s])
                    parts, o, n = (P, W_OFF[s], TP - s * P) if s < NB else (TS, W_OFF[s], TS)
                    dve.tensor_tensor(wts[0:parts, o:o + n], bank(S_USE + s)[0:parts, 0:n], wts[0:parts, o:o + n],
                                      ALU.mult).then_inc(dve_read, 1)
                taps(5)
                dve.wait_ge(act_read, h * ACT_USES + (START + 5))
                w5 = hcol(I_WS + NB, TS)
                k5, v5 = kvn[0:TS, NB, 0:HD], kvn[0:TS, NB, HD:2 * HD]
                steps.on(dve.tensor_copy(kv_hi[0:TS, 0:HD], k5))
                steps.on(dve.tensor_scalar(kv_hi[0:TS, HD:2 * HD], v5, w5, None, ALU.mult))
                steps.settle()
                dve.tensor_tensor(kv_lo[0:TS, 0:HD], k5, kv_hi[0:TS, 0:HD].bitcast(F32), ALU.subtract)\
                    .then_inc(kvsplit_ready, 1)
                dve.scalar_tensor_tensor(kv_lo[0:TS, HD:2 * HD], v5, w5, kv_hi[0:TS, HD:2 * HD].bitcast(F32),
                                         ALU.mult, ALU.subtract).then_inc(kvsplit_ready, 1)
                use(I_USE)
                for s in range(NB):
                    dve.wait_ge(act_read, h * ACT_USES + (START + s + 1))
                    dve.tensor_scalar(wvn[:, s, :], kvn[:, s, HD:2 * HD + 1], hcol(I_WS + s), None, ALU.mult)\
                        .then_inc(wv_ready, 1)
                dve.wait_ge(pvhi_ready, h * 2 + 1)
                dve.tensor_tensor(w2_lo[:, :], wts[:, 0:W_OFF[NB]], w2_hi[:, :].bitcast(F32), ALU.subtract)\
                    .then_inc(pvlo_ready, 1)
                dve.wait_ge(wv_ready, h * NB + NB)
                dve.wait_ge(pvhi_ready, h * 2 + 2)
                dve.tensor_tensor(kvn_lo[:, 0:NB, HD:2 * HD], kvn[:, 0:NB, HD:2 * HD], v_hi[:, :, 0:HD].bitcast(F32),
                                  ALU.subtract).then_inc(pvlo_ready, 1)

                lo_of(6)
                lo_of(7)
                dve.wait_ge(act_read, h * ACT_USES + (START + 13))
                wi = hcol(I_WI, TS)
                steps.on(dve.tensor_tensor(nq8[0:TS, :], inter[0:TS, HD:HD + SB], onehot[0:TS, :], ALU.mult))
                steps.on(dve.scalar_tensor_tensor(num[0:TS, NB, 0:HD], inter[0:TS, 0:HD], wi, num[0:TS, NB, 0:HD],
                                                  ALU.mult, ALU.add))
                steps.settle()
                steps.on(dve.scalar_tensor_tensor(num[0:TS, NB, 0:HD], inter_lo[0:TS, :], wi, num[0:TS, NB, 0:HD],
                                                  ALU.mult, ALU.add))
                steps.on(dve.reduce_sum(nq1[0:TS, :], nq8[0:TS, :], axis=mybir.AxisListType.X))
                steps.settle()
                steps.on(dve.scalar_tensor_tensor(num[0:TS, NB, HD:VE], nq1[0:TS, :], wi, num[0:TS, NB, HD:VE],
                                                  ALU.mult, ALU.add))
                for i in range(5):
                    steps.on(dve.bn_stats(stats[:, i, :], num[:, i, 0:HD]))
                em = cols[:, I_EM:I_EM + 5, bass.ds(h, 1)].rearrange("p i o -> p (i o)")
                steps.settle()
                steps.on(dve.scalar_tensor_tensor(small[:, 0, :], num[:, :, HD], -1.0, num[:, :, HD],
                                                  ALU.mult, ALU.max))
                for i in range(5):
                    steps.on(dve.bn_aggr(mv[:, i, :], stats[:, i, :]))
                steps.settle()
                steps.on(dve.tensor_tensor(small[:, 0, :], small[:, 0, :], em, ALU.max))
                steps.settle()
                steps.on(dve.reciprocal(small[:, 0, :], small[:, 0, :]))
                steps.settle()
                steps.on(dve.tensor_tensor(small[:, 1, :], mv[:, :, 1], small[:, 0, :], ALU.mult))
                steps.settle()
                dve.tensor_tensor(small[:, 1, :], small[:, 1, :], small[:, 0, :], ALU.mult).then_inc(hvar_ready, 1)
                for b in range(SB):
                    use(CS_USE + b)
                    c = cs[:, b, :, :].rearrange("p k v -> p (k v)")
                    dve.scalar_tensor_tensor(c, c, dec[:, bass.ds(h, 1), b:b + 1].rearrange("p o b -> p (o b)"),
                                             bank(CS_USE + b), ALU.mult, ALU.add).then_inc(dve_read, 1)
                use(N_USE)
                nn = nnew[:, bass.ds(h, 1), :, :].rearrange("p o k b -> p (o k b)")
                dve.tensor_tensor(nn, nn, bank(N_USE)[:, 0:2 * SB], ALU.add).then_inc(dve_read, 1)
                dve.wait_ge(hdev_ready, h + 1)
                steps.on(dve.reciprocal(small[:, 2, :], small[:, 2, :]))
                steps.settle()
                steps.on(dve.tensor_tensor(small[:, 3, :], small[:, 2, :], small[:, 0, :], ALU.mult))
                steps.settle()
                for i in range(5):
                    dve.tensor_scalar(num[:, i, 0:HD], num[:, i, 0:HD], mv[:, i, 0:1], small[:, 3, i:i + 1],
                                      ALU.subtract, ALU.mult).then_inc(hm_ready, 1)
                for j in (8, 9):
                    lo_of(j)
                    evacuated(j % 2, 5)
                    m = row(merged, h * 2 + (j - 8))
                    dve.tensor_tensor(m, m, tmp[:, j % 2, :], ALU.mult).then_inc(gb_used, 1)
                assert tap[0] == CW
                dve.wait_ge(gb_used, h * 2 + (START + 2))
                for v in range(2):
                    use(HT_USE + v)
                    m = row(merged, h * 2 + v)[:, 0:TP]
                    dve.scalar_tensor_tensor(m, bank(HT_USE + v), vcol(h * 2 + (V_GMN + v)), m, ALU.mult, ALU.mult)\
                        .then_inc(dve_read, 1)
                use(HT_USE + 2)
                for v in range(2):
                    m = row(merged, h * 2 + v)[:, TP:T]
                    ins = dve.scalar_tensor_tensor(m, bank(HT_USE + 2)[:, v * TS:v * TS + TS],
                                                   vcol(h * 2 + (V_GMN + v)), m, ALU.mult, ALU.mult)
                    if v:
                        ins.then_inc(dve_read, 1)
                    else:
                        steps.on(ins)
                steps.end(NH)

            steps.on(dve.tensor_tensor(hf[:, 0, :], conv[:, 0, :], conv[:, 1, :], ALU.add))
            steps.on(dve.tensor_tensor(hf[:, 1, :], conv[:, 2, :], conv[:, 3, :], ALU.add))
            steps.settle()
            dve.tensor_tensor(acc[:, :], hf[:, 0, :], hf[:, 1, :], ALU.add).then_inc(csum_ready, 1)
            split_lo(U_GA + 2, 0)
            dve.wait_ge(cstat_done, 1)
            for j in range(CT):
                ins = dve.tensor_tensor(halves(conv, j), halves(conv, j), slot(2), ALU.subtract)
                ins.then_inc(cdev_ready, 1)
            dve.wait_ge(cdev_ready, CT)
            dve.sem_inc(slot_read[2], 1)
            dve.wait_ge(csq_ready, 1)
            dve.tensor_copy(acc[:, :], tmp[:, 0, :]).then_inc(csq_added, 1)
            for j in range(1, CT):
                dve.wait_ge(csq_ready, j + 1)
                dve.wait_ge(csq_added, j)
                dve.tensor_tensor(acc[:, :], acc[:, :], tmp[:, j % 2, :], ALU.add).then_inc(csq_added, 1)
            split_lo(U_GA + 3, 1)
            split_lo(U_GA + 4, 0)
            rstd(3, C3_CO, 2)
            dve.wait_ge(rs_ready, 2)
            for j in range(CT):
                dve.tensor_tensor(conv[:, j, :], conv[:, j, :], rs[:, :], ALU.mult).then_inc(cnorm_ready, 1)
            split_lo(U_GA + 5, 1)
            with dve.Fori(2, KT // 2) as i:
                for s in range(2):
                    split_lo(i * 2 + (U_GA + s + 2), s)
            dve.wait_ge(dve_read, START + NH * DVE_USES)
            dve.wait_ge(slot_read[0], C_CO)
            dve.wait_ge(slot_read[1], C_CO)
            with dve.Fori(0, N_CO // 2) as i:
                for p in range(2):
                    for o in range(2):
                        s, j = 2 * p + o, i * 4 + (2 * p + o)
                        dve.wait_ge(unit_done if o else co_first, i * 2 + ((U_CO if o else 0) + p + 1))
                        g = halves(ga, j)
                        dve.tensor_tensor(g, slot(s), g, ALU.mult).then_inc(slot_read[s], 1)
                        dve.wait_ge(slot_read[s], i + ((C_CO, C_CO, C2_CO, C3_CO)[s] + 1))
                        m = row(merged, j)
                        dve.tensor_tensor(m, m, row(ga, j), ALU.add).then_inc(m_ready, 1)
                    split_lo(i * 2 + (U_CO + p + 2), p)

            def add_units(i, base, contents, sq_base=None, last=False):
                for s in range(2):
                    dve.wait_ge(unit_done, i * 2 + (base + s + 1))
                    xs = halves(x, i * 2 + s)
                    dve.tensor_tensor(xs, slot(s), xs, ALU.add).then_inc(slot_read[s], 1)
                    if sq_base is not None:
                        dve.wait_ge(sq_ready, i * 2 + (sq_base + s + 1))
                        dve.wait_ge(sq_added, i * 2 + (sq_base - KT + SQ1 + s))
                        dve.tensor_tensor(acc[:, :], acc[:, :], tmp[:, s, :], ALU.add).then_inc(sq_added, 1)
                    if base == U_O:
                        dve.wait_ge(hhi_ready, i * 2 + (KT + s + 1))
                        dve.scalar_tensor_tensor(row(h_lo, i * 2 + s), row(x, i * 2 + s), vcol(i * 2 + (V_GFFN + s)),
                                                 row(h_hi, i * 2 + s).bitcast(F32), ALU.mult, ALU.subtract)\
                            .then_inc(h2lo_ready, 1)
                    if not last:
                        split_lo(i * 2 + (base + s + 2), s)

            dve.wait_ge(x_reloaded, 16 * KT)
            dve.wait_ge(cstat_done, 2)
            dve.memset(acc[:, :], 0.0).then_inc(acc_zero, 1)
            dve.wait_ge(acc_zero, 1)
            with dve.Fori(0, KT // 2) as i:
                add_units(i, U_O, C_O, KT)
            def hidden(g, i, p):
                split_lo(i * 4 + (U_E[g] + 2 * p + 2), 0)
                if g == 0 and p == 0 and isinstance(i, int):
                    rstd(2, C2_NORM + 1, 3)
                    dve.wait_ge(rs_ready, 3)
                dve.wait_ge(unit_done, i * 4 + (U_E[g] + 2 * p + 1))
                dve.tensor_tensor(halves(tmp, p), slot(2 * p), flat(rs), ALU.mult).then_inc(slot_read[2 * p], 1)
                dve.wait_ge(silu_ready, i * 2 + (Q_E[g] + p + 1))
                dve.wait_ge(hidlo_ready, i * 2 + (START + Q_E[g]))
                dve.wait_ge(unit_done, i * 4 + (U_E[g] + 2 * p + 2))
                dve.tensor_tensor(halves(hf, p), slot(2 * p + 1), halves(tmp, p), ALU.mult)\
                    .then_inc(slot_read[2 * p + 1], 1)
                split_lo(i * 4 + (U_E[g] + 2 * p + 3), 1)

            for g, n in enumerate(GROUPS):
                if g == 0:
                    for p in range(2):
                        hidden(0, 0, p)
                    dve.memset(acc[:, :], 0.0).then_inc(acc_zero, 1)
                    dve.wait_ge(acc_zero, 2)
                with dve.Fori(1 if g == 0 else 0, n // 2) as i:
                    for p in range(2):
                        hidden(g, i, p)
                if g < len(GROUPS) - 1:
                    with dve.Fori(0, KT // 2) as i:
                        add_units(i, U_F[g], C_F[g])
            with dve.Fori(0, KT // 2 - 1) as i:
                add_units(i, U_F[-1], C_F[-1], 2 * KT)
            add_units(KT // 2 - 1, U_F[-1], C_F[-1], 2 * KT, last=True)
            dve.wait_ge(slot_read[2], C2_END + 1)
            for b in range(2):
                half = rs[:, b * HALF:(b + 1) * HALF]
                dve.reciprocal(half, half).then_inc(rs_ready, 1)
            dve.wait_ge(rs_ready, 5)
            dve.wait_ge(xfin_ready, KT)
            for k in range(Y_POOL, KT):
                dve.tensor_tensor(x[:, k, :], x[:, k, :], rs[:, :], ALU.mult).then_inc(y_ready, 1)


def kernel(**inputs):
    import concourse.bacc as bacc
    from concourse.bass_utils import run_bass_kernel_spmd

    a = {k: np.asarray(v) for k, v in inputs.items()}

    def blocks(w):
        k, n = w.shape[0] // P, w.shape[1] // P
        return w.reshape(k, P, n, P).transpose(2, 1, 0, 3).reshape(n, P, k * P)

    def per_tile(v):
        return v.reshape(-1, P).T

    w_in, b_in = a["w_in"][0], a["b_in"][0]
    sizes = [DC, DC] + [NH * HD] * 4 + [NH, NH, D, D]
    at = np.cumsum([0] + sizes)
    cut = [slice(int(at[i]), int(at[i + 1])) for i in range(len(sizes))]
    wb = {n: blocks(w_in[:, cut[i]]) for n, i in zip("cv cg q k v og ga gb".split(), (0, 1, 2, 3, 4, 5, 8, 9))}
    bb = {n: b_in[cut[i]].reshape(-1, P) for n, i in zip("cv cg q k v og ga gb".split(), (0, 1, 2, 3, 4, 5, 8, 9))}

    def heads(d):
        return np.concatenate([d[n][2 * h:2 * h + 2] for h in range(NH) for n in ("q", "k", "v", "og", "gb")])

    def pairs(p, q):
        return np.stack([p, q], 1).reshape((-1,) + p.shape[1:])

    vecs = np.concatenate(
        [pairs(bb["cg"], bb["cv"]).T, heads(bb).T, bb["ga"].T]
        + [per_tile(a[n].reshape(-1)) for n in ("g_mix_norm", "g_ffn_norm", "g_final", "g_mlstm_norm",
                                                "g_conv_norm", "b_conv_norm", "b_dwconv")]
        + [a["w_dwconv"][0].reshape(CW, CT, P).transpose(2, 1, 0).reshape(P, CT * CW)], axis=1)
    wfi = blocks(a["w_ffn_in"][0])
    wfo = a["w_ffn_out"][0]
    rows_of = np.cumsum([0] + [P * g for g in GROUPS])
    x_all = np.concatenate([a["x_prompt"].reshape(TP, D), a["x_sample"].reshape(TS, D)])
    ins = {
        "xT": x_all.reshape(T, KT, P).transpose(2, 1, 0),
        "vecs": vecs,
        "gate_w": w_in[:, cut[6].start:cut[7].stop].reshape(KT, P, 2 * NH).transpose(1, 0, 2),
        "gate_b": np.stack([b_in[cut[6]], b_in[cut[7]]], 1),
        "cache": a["cache_conv"][0].reshape(SB, PAST, CT, P).transpose(3, 2, 0, 1),
        "w_cgcv": pairs(wb["cg"], wb["cv"]),
        "w_head": heads(wb),
        "w_ga": wb["ga"],
        "w_co": blocks(a["w_conv_out"][0]).reshape(N_CO, 2, P, CT * P).transpose(0, 2, 1, 3).reshape(N_CO, P, KT * P),
        "w_o": blocks(a["w_out"][0]),
        "w_fi": pairs(wfi[:FT], wfi[FT:]),
        "w_fo0": blocks(wfo[rows_of[0]:rows_of[1]]),
        "w_fo1": blocks(wfo[rows_of[1]:rows_of[2]]),
        "w_fo2": blocks(wfo[rows_of[2]:rows_of[3]]),
        "st_c": a["state_mlstm_C"][0].reshape(SB, NH, HD, 2, P).transpose(1, 4, 0, 3, 2),
        "st_n": a["state_mlstm_n"][0].reshape(SB, NH, 2, P).transpose(3, 1, 2, 0),
        "st_m": a["state_mlstm_m"][0].T,
    }
    outs = {
        "y": (P, KT, T), "conv_p": (P, CT, PAST), "conv_s": (P, CT, SB, PAST), "cn_p": (NH, P, 2, VE),
        "m_p": (NH, 1), "c_s": (NH, P, SB, 2, HD), "n_s": (P, NH, 2, SB), "m_s": (NH, SB),
    }
    nc = bacc.Bacc("TRN2", target_bir_lowering=False, num_devices=1)
    ins = {f"{k}_in": np.ascontiguousarray(v) for k, v in ins.items()}
    args = [nc.dram_tensor(k, v.shape, F32, kind="ExternalInput").ap() for k, v in ins.items()]
    args += [nc.dram_tensor(f"{k}_out", v, F32, kind="ExternalOutput").ap() for k, v in outs.items()]
    build(nc, *args)
    res = run_bass_kernel_spmd(nc, [ins], core_ids=[0]).results[0]
    r = {k: res[f"{k}_out"] for k in outs}

    yt = r["y"].transpose(2, 1, 0).reshape(T, D)
    cn = r["cn_p"].transpose(0, 3, 2, 1).reshape(NH, VE, HD)
    c = np.ascontiguousarray
    return (c(yt[:TP]).reshape(1, TP, D), c(yt[TP:]).reshape(SB, SL, D),
            c(r["conv_p"].transpose(2, 1, 0)).reshape(1, 1, PAST, DC),
            c(cn[:, :HD]).reshape(1, 1, NH, HD, HD), c(cn[:, HD]).reshape(1, 1, NH, HD),
            c(r["m_p"]).reshape(1, 1, NH),
            c(r["conv_s"].transpose(2, 3, 1, 0)).reshape(1, SB, PAST, DC),
            c(r["c_s"].transpose(2, 0, 4, 3, 1)).reshape(1, SB, NH, HD, HD),
            c(r["n_s"].transpose(3, 1, 2, 0)).reshape(1, SB, NH, HD),
            c(r["m_s"].T).reshape(1, SB, NH))
```
